# Optimizing a Trainium2 kernel written in Bass

```python
import math
import jax
import jax.numpy as jnp
from jax import lax
import numpy as np

D_MODEL = 1024
BATCH = 1
SEQ = 1024
DEPTH = 1

HEAD_DIM = 64
N_Q_HEADS = 16
N_KV_HEADS = 4
Q_PER_KV = N_Q_HEADS // N_KV_HEADS
ATTN_WIDTH = N_Q_HEADS * HEAD_DIM
KV_WIDTH = N_KV_HEADS * HEAD_DIM
DILATED_PATTERNS = ((128, 1), (512, 4), (2048, 16))
ATTN_BLOCK = 128
ROPE_THETA = 10000.0

SSM_HEADS = 16
SSM_HEAD_DIM = 64
SSM_WIDTH = SSM_HEADS * SSM_HEAD_DIM
SSM_STATE = 128
SSM_GROUPS = 2
SSM_HEADS_PER_GROUP = SSM_HEADS // SSM_GROUPS
BC_WIDTH = SSM_GROUPS * SSM_STATE
CONV_WIDTH = 4
CONV_CHANNELS = SSM_WIDTH + 2 * BC_WIDTH
SSD_CHUNK = 128
DT_MIN = 0.001
DT_MAX = 0.1
A_INIT_MIN = 1.0
A_INIT_MAX = 16.0

MIX_WIDTH = ATTN_WIDTH + SSM_WIDTH
IN_SPLITS = (
    ATTN_WIDTH,
    ATTN_WIDTH + KV_WIDTH,
    ATTN_WIDTH + 2 * KV_WIDTH,
    ATTN_WIDTH + 2 * KV_WIDTH + CONV_CHANNELS,
    ATTN_WIDTH + 2 * KV_WIDTH + CONV_CHANNELS + SSM_WIDTH,
)
IN_PROJ_COLS = IN_SPLITS[-1] + SSM_HEADS

D_FF = 2816
MACARON_WEIGHT = 0.5
NORM_EPS = 1e-6
POS_OFFSET_MAX = 1024

kernel_name = 'hymba_dilated_attn_mamba2_macaron_sandwich'

def rmsnorm(x, g):
    xf = x.astype(jnp.float32)
    y = xf * lax.rsqrt(jnp.mean(xf * xf, axis=-1, keepdims=True) + NORM_EPS)
    return (y * g.astype(jnp.float32)).astype(x.dtype)

def swiglu(x, w_gate, w_up, w_down):
    return (jax.nn.silu(x @ w_gate) * (x @ w_up)) @ w_down

def rope_cos_sin(positions):
    inv_freq = ROPE_THETA ** (-jnp.arange(0, HEAD_DIM, 2, dtype=jnp.float32) / HEAD_DIM)
    ang = positions.astype(jnp.float32)[..., None] * inv_freq
    ang = jnp.concatenate([ang, ang], axis=-1)
    return jnp.cos(ang), jnp.sin(ang)

def apply_rope(t, cos, sin):
    shape = cos.shape[:2] + (1,) * (t.ndim - 3) + (HEAD_DIM,)
    c = cos.reshape(shape)
    s = sin.reshape(shape)
    tf = t.astype(jnp.float32)
    t1, t2 = jnp.split(tf, 2, axis=-1)
    rot = jnp.concatenate([-t2, t1], axis=-1)
    return (tf * c + rot * s).astype(t.dtype)

def _to_strided_blocks(t, dilation, n_blocks):
    b, s = t.shape[:2]
    sub_len = s // dilation
    t = t.reshape((b, sub_len, dilation) + t.shape[2:])
    pad = n_blocks * ATTN_BLOCK - sub_len
    t = jnp.pad(t, [(0, 0), (0, pad)] + [(0, 0)] * (t.ndim - 2))
    return t.reshape((b, n_blocks, ATTN_BLOCK, dilation) + t.shape[3:])

def _from_strided_blocks(t, seq):
    b, n_blocks, _, dilation = t.shape[:4]
    sub_len = seq // dilation
    t = t.reshape((b, n_blocks * ATTN_BLOCK, dilation) + t.shape[4:])[:, :sub_len]
    return t.reshape((b, seq) + t.shape[3:])

def _with_prev_block(t):
    prev = jnp.concatenate([jnp.zeros_like(t[:, :1]), t[:, :-1]], axis=1)
    return jnp.concatenate([prev, t], axis=2)

def dilated_window_attention(q, k, v, window, dilation):
    b, s = q.shape[:2]
    sub_len = s // dilation
    span = window // dilation
    n_blocks = -(-sub_len // ATTN_BLOCK)
    qb = _to_strided_blocks(q, dilation, n_blocks)
    kk = _with_prev_block(_to_strided_blocks(k, dilation, n_blocks))
    vv = _with_prev_block(_to_strided_blocks(v, dilation, n_blocks))
    scores = jnp.einsum('bnqrkgh,bnsrkh->bnrkgqs', qb, kk, preferred_element_type=jnp.float32)
    qi = jnp.arange(ATTN_BLOCK)[:, None]
    si = jnp.arange(2 * ATTN_BLOCK)[None, :]
    dist = qi + ATTN_BLOCK - si
    band = (dist >= 0) & (dist <= span)
    key_idx = jnp.arange(n_blocks)[:, None, None] * ATTN_BLOCK + si[None] - ATTN_BLOCK
    mask = band[None] & (key_idx >= 0)
    scores = jnp.where(mask[None, :, None, None, None], scores, -jnp.inf)
    m = jnp.max(scores, axis=-1)
    p = jnp.exp(scores - m[..., None])
    l = jnp.sum(p, axis=-1)
    o = jnp.einsum('bnrkgqs,bnsrkh->bnqrkgh', p.astype(vv.dtype), vv, preferred_element_type=jnp.float32)
    l_t = jnp.moveaxis(l, -1, 2)
    o = o / l_t[..., None]
    return (_from_strided_blocks(o, s),
            _from_strided_blocks(jnp.moveaxis(m, -1, 2), s),
            _from_strided_blocks(l_t, s))

def mixture_of_dilations(q, k, v):
    outs, maxes, dens = [], [], []
    for window, dilation in DILATED_PATTERNS:
        o, m, l = dilated_window_attention(q, k, v, window, dilation)
        outs.append(o)
        maxes.append(m)
        dens.append(l)
    m_all = jnp.stack(maxes)
    w = jnp.stack(dens) * jnp.exp(m_all - jnp.max(m_all, axis=0, keepdims=True))
    o_all = jnp.stack(outs)
    return jnp.sum(w[..., None] * o_all, axis=0) / jnp.sum(w, axis=0)[..., None]

def causal_depthwise_conv(u, w, bias):
    y = lax.conv_general_dilated(u, w[:, None, :].astype(u.dtype), window_strides=(1,),
                                 padding=[(CONV_WIDTH - 1, 0)],
                                 dimension_numbers=('NWC', 'WIO', 'NWC'),
                                 feature_group_count=u.shape[-1])
    return y + bias

def ssd_chunked_scan(x, dt, a, b_in, c_in):
    bsz, s = x.shape[:2]
    n_chunks = s // SSD_CHUNK
    g, e, p, n = SSM_GROUPS, SSM_HEADS_PER_GROUP, SSM_HEAD_DIM, SSM_STATE
    xs = (x.astype(jnp.float32) * dt[..., None]).reshape(bsz, n_chunks, SSD_CHUNK, g, e, p)
    a_dt = jnp.moveaxis((dt * a).reshape(bsz, n_chunks, SSD_CHUNK, g, e), 2, -1)
    a_cs = jnp.cumsum(a_dt, axis=-1)
    bc = b_in.astype(jnp.float32).reshape(bsz, n_chunks, SSD_CHUNK, g, n)
    cc = c_in.astype(jnp.float32).reshape(bsz, n_chunks, SSD_CHUNK, g, n)
    idx = jnp.arange(SSD_CHUNK)
    causal = idx[:, None] >= idx[None, :]
    seg = a_cs[..., :, None] - a_cs[..., None, :]
    decay_in = jnp.exp(jnp.where(causal, seg, -jnp.inf))
    cb = jnp.einsum('bclgn,bcsgn->bcgls', cc, bc)
    y_diag = jnp.einsum('bcgels,bcsgep->bclgep', cb[:, :, :, None] * decay_in, xs)
    decay_to_end = jnp.exp(a_cs[..., -1:] - a_cs)
    states = jnp.einsum('bclgn,bcgel,bclgep->bcgepn', bc, decay_to_end, xs)
    chunk_decay = jnp.exp(a_cs[..., -1])

    def step(h, inp):
        st, dec = inp
        return h * dec[..., None, None] + st, h

    h0 = jnp.zeros((bsz, g, e, p, n), jnp.float32)
    _, prev_states = lax.scan(step, h0, (jnp.moveaxis(states, 1, 0), jnp.moveaxis(chunk_decay, 1, 0)))
    prev_states = jnp.moveaxis(prev_states, 0, 1)
    y_off = jnp.einsum('bclgn,bcgepn,bcgel->bclgep', cc, prev_states, jnp.exp(a_cs))
    return (y_diag + y_off).reshape(bsz, s, SSM_HEADS, p)

def hybrid_mixer(h, cos, sin, w_in, conv_w, conv_b, dt_bias, a_log, d_skip, ssm_norm, w_out):
    bsz, s, _ = h.shape
    proj = h @ w_in
    q, k, v, xbc, z, dt_raw = jnp.split(proj, list(IN_SPLITS), axis=-1)

    q = apply_rope(q.reshape(bsz, s, N_KV_HEADS, Q_PER_KV, HEAD_DIM), cos, sin) * (HEAD_DIM ** -0.5)
    k = apply_rope(k.reshape(bsz, s, N_KV_HEADS, HEAD_DIM), cos, sin)
    v = v.reshape(bsz, s, N_KV_HEADS, HEAD_DIM)
    attn_out = mixture_of_dilations(q, k, v).reshape(bsz, s, ATTN_WIDTH)

    xbc = jax.nn.silu(causal_depthwise_conv(xbc, conv_w, conv_b))
    xs, b_in, c_in = jnp.split(xbc, [SSM_WIDTH, SSM_WIDTH + BC_WIDTH], axis=-1)
    xs = xs.reshape(bsz, s, SSM_HEADS, SSM_HEAD_DIM)
    b_in = b_in.reshape(bsz, s, SSM_GROUPS, SSM_STATE)
    c_in = c_in.reshape(bsz, s, SSM_GROUPS, SSM_STATE)
    dt = jax.nn.softplus(dt_raw.astype(jnp.float32) + dt_bias.astype(jnp.float32))
    a = -jnp.exp(a_log.astype(jnp.float32))
    y = ssd_chunked_scan(xs, dt, a, b_in, c_in)
    y = y + d_skip.astype(jnp.float32)[:, None] * xs.astype(jnp.float32)
    y = y.reshape(bsz, s, SSM_WIDTH) * jax.nn.silu(z.astype(jnp.float32))
    y = y.reshape(bsz, s, SSM_GROUPS, SSM_WIDTH // SSM_GROUPS)
    y = y * lax.rsqrt(jnp.mean(y * y, axis=-1, keepdims=True) + NORM_EPS)
    y = y.reshape(bsz, s, SSM_WIDTH) * ssm_norm.astype(jnp.float32)

    mixed = jnp.concatenate([attn_out.astype(h.dtype), y.astype(h.dtype)], axis=-1)
    return mixed @ w_out

def setup_inputs(seed: int = 0) -> dict:
    key = jax.random.key(seed)
    ks = jax.random.split(key, 24)
    f32 = jnp.float32

    def dense(k, shape, fan_in):
        return jax.random.normal(k, shape, f32) * fan_in ** -0.5

    def gain(k, shape):
        return 1.0 + 0.05 * jax.random.normal(k, shape, f32)

    x = jax.random.normal(ks[0], (BATCH, SEQ, D_MODEL), f32)
    positions = (jnp.arange(SEQ, dtype=jnp.int32)[None, :]
                 + jax.random.randint(ks[1], (BATCH, 1), 0, POS_OFFSET_MAX, dtype=jnp.int32))
    dt = jnp.exp(jax.random.uniform(ks[11], (DEPTH, SSM_HEADS), f32)
                 * (math.log(DT_MAX) - math.log(DT_MIN)) + math.log(DT_MIN))
    dt_bias = dt + jnp.log(-jnp.expm1(-dt))
    a_log = jnp.log(jax.random.uniform(ks[12], (DEPTH, SSM_HEADS), f32, A_INIT_MIN, A_INIT_MAX))
    return {
        'x': x,
        'positions': positions,
        'ffn1_pre_norm': gain(ks[2], (DEPTH, D_MODEL)),
        'ffn1_w_gate': dense(ks[3], (DEPTH, D_MODEL, D_FF), D_MODEL),
        'ffn1_w_up': dense(ks[4], (DEPTH, D_MODEL, D_FF), D_MODEL),
        'ffn1_w_down': dense(ks[5], (DEPTH, D_FF, D_MODEL), D_FF),
        'ffn1_post_norm': gain(ks[6], (DEPTH, D_MODEL)),
        'mix_pre_norm': gain(ks[7], (DEPTH, D_MODEL)),
        'w_in': dense(ks[8], (DEPTH, D_MODEL, IN_PROJ_COLS), D_MODEL),
        'conv_w': dense(ks[9], (DEPTH, CONV_WIDTH, CONV_CHANNELS), CONV_WIDTH),
        'conv_b': 0.02 * jax.random.normal(ks[10], (DEPTH, CONV_CHANNELS), f32),
        'dt_bias': dt_bias,
        'a_log': a_log,
        'd_skip': 1.0 + 0.1 * jax.random.normal(ks[13], (DEPTH, SSM_HEADS), f32),
        'ssm_norm': gain(ks[14], (DEPTH, SSM_WIDTH)),
        'w_out': dense(ks[15], (DEPTH, MIX_WIDTH, D_MODEL), MIX_WIDTH),
        'mix_post_norm': gain(ks[16], (DEPTH, D_MODEL)),
        'ffn2_pre_norm': gain(ks[17], (DEPTH, D_MODEL)),
        'ffn2_w_gate': dense(ks[18], (DEPTH, D_MODEL, D_FF), D_MODEL),
        'ffn2_w_up': dense(ks[19], (DEPTH, D_MODEL, D_FF), D_MODEL),
        'ffn2_w_down': dense(ks[20], (DEPTH, D_FF, D_MODEL), D_FF),
        'ffn2_post_norm': gain(ks[21], (DEPTH, D_MODEL)),
    }

def reference(x, positions, ffn1_pre_norm, ffn1_w_gate, ffn1_w_up, ffn1_w_down, ffn1_post_norm,
              mix_pre_norm, w_in, conv_w, conv_b, dt_bias, a_log, d_skip, ssm_norm, w_out, mix_post_norm,
              ffn2_pre_norm, ffn2_w_gate, ffn2_w_up, ffn2_w_down, ffn2_post_norm):
    cos, sin = rope_cos_sin(positions)
    for i in range(DEPTH):
        h = swiglu(rmsnorm(x, ffn1_pre_norm[i]), ffn1_w_gate[i], ffn1_w_up[i], ffn1_w_down[i])
        x = x + MACARON_WEIGHT * rmsnorm(h, ffn1_post_norm[i])
        h = hybrid_mixer(rmsnorm(x, mix_pre_norm[i]), cos, sin, w_in[i], conv_w[i], conv_b[i],
                         dt_bias[i], a_log[i], d_skip[i], ssm_norm[i], w_out[i])
        x = x + rmsnorm(h, mix_post_norm[i])
        h = swiglu(rmsnorm(x, ffn2_pre_norm[i]), ffn2_w_gate[i], ffn2_w_up[i], ffn2_w_down[i])
        x = x + MACARON_WEIGHT * rmsnorm(h, ffn2_post_norm[i])
    return x


_drawn_inputs = setup_inputs


def setup_inputs(seed=0):
    import zlib

    import numpy as np

    out = dict(_drawn_inputs(seed))
    spreads = {}
    factors = {'conv_b': 2.848, 'ffn2_post_norm': 3.463}
    for name, (base, spread) in spreads.items():
        noise = np.random.default_rng([zlib.crc32(name.encode()), seed]).standard_normal(out[name].shape)
        drawn = base * np.exp(spread * noise) if base else spread * noise
        out[name] = jnp.asarray(drawn.astype(out[name].dtype))
    for name, factor in factors.items():
        out[name] = (out[name] * factor).astype(out[name].dtype)
    return out
```

```python
from contextlib import ExitStack

import numpy as np

import concourse.bass as bass
from concourse import mybir

F32 = mybir.dt.float32
FR = mybir.dt.float32r
I32 = mybir.dt.int32
ALU = mybir.AluOpType
ACT = mybir.ActivationFunctionType

P = 128
S = 1024
D = 1024
KT = D // P
HALF = 512
NH2 = S // HALF
FF = 2816
FT = FF // P
FG = FT // 2
HD = 64
HEADS = 16
KVH = 4
CH = S // P
XBC_T = 12
Z_T = 8
BC0 = 8
MIX_T = 16
GROUPS = 2
EPS = 1e-6
KB = 1024
NORM_COLS = {"ffn1_pre": 0, "ffn1_post": 8, "mix_pre": 16, "mix_post": 24, "ffn2_pre": 32, "ffn2_post": 40}
CONVW, CONVB, SSMN, DSK, INVF, EPSC = 48, 96, 108, 116, 124, 125
NCOLS = 126
TWO_PI = 2 * np.pi
C1 = 6.28125
C2 = float(np.float32(np.floor((TWO_PI - C1) * 2**22) / 2**22))
C3 = float(np.float32(TWO_PI - C1 - C2))
ROUND = 12582912.0
PI_IN = 3.1415925


def build(nc, a):
    with ExitStack() as ctx:
        sems = {}

        def sem(name):
            if name not in sems:
                sems[name] = ctx.enter_context(nc.semaphore(name))
            return sems[name]

        map_base = -(-nc.sbuf_base // 64) * 64

        def at(name, kb, shape, dt=F32):
            return nc.alloc_sbuf_tensor_at(name, shape, dt, offset=map_base + int(kb * KB))

        def wait(eng, name, value):
            if not isinstance(value, int) or value > 0:
                eng.wait_ge(sem(name), value)

        nh = at("norm_hi", 0, [P, KT, S], FR)
        nl = at("norm_lo", 32, [P, KT, S], FR)
        acc = at("acc", 64, [P, KT, S])
        acth = at("act_hi", 96, [P, 2, S], FR)
        actl = at("act_lo", 104, [P, 2, S], FR)
        rawg = at("raw_gate_up", 112, [P, 2, KT, P])
        guh = at("gate_up_hi", 120, [P, 2, 2, KT, P], FR)
        gul = at("gate_up_lo", 136, [P, 2, 2, KT, P], FR)
        raww = at("raw_tile", 152, [P, KT, P])
        wh = at("tile_hi", 156, [P, 2, KT, P], FR)
        wl = at("tile_lo", 164, [P, 2, KT, P], FR)
        xs = at("x_stream", 172, [P, 2, S])
        sq = at("squares", 180, [P, 2, S])
        diag = at("rstd_diagonal", 180, [P, CH, P])
        tg = at("gate_scaled", 180, [P, HALF])
        ts = at("gate_silu", 182, [P, HALF])
        tu = at("up_scaled", 184, [P, HALF])
        sqs = at("square_sums", 188, [P, S])
        rb = at("rstd_rows", 192, [P, S])
        cos = at("cos", 196, [P, S])
        sin = at("sin", 200, [P, S])
        ident = at("ident", 204, [P, P])
        tri = at("tri", 204.5, [P, P])
        ones = at("ones", 205, [P, P])
        rot = at("rot", 205.5, [P, P])
        cols = at("cols", 206, [P, NCOLS])
        rc0 = at("rms_col", 206.5, [P, CH])
        rc = at("rstd_col", 206.53125, [P, CH])
        hcols = at("half_post_cols", 206.5625, [P, 48])
        ang = at("angle", 172, [P, S])
        turns = at("turns", 176, [P, S])
        qh = at("q_hi", 64, [P, 2, S], FR)
        ql = at("q_lo", 72, [P, 2, S], FR)
        kh = at("k_hi", 80, [P, S], FR)
        kl = at("k_lo", 84, [P, S], FR)
        vg = at("v_hi_lo", 88, [P, CH, 2, HD], FR)
        pe0 = at("probs_even", 92, [P, 4, 7 * P])
        pe1 = at("probs_odd", 106, [P, 4, 8 * P])
        pth = at("probs_t_hi", 122, [P, 2, 4, P], FR)
        ptl = at("probs_t_lo", 126, [P, 2, 4, P], FR)
        attg = at("att_group", 130, [P, 2, S])
        mask = at("mask", 138, [P, S])
        vall = at("v_all", 142, [P, CH, 256])
        dtr = at("dt_raw", 150, [P, CH, HEADS])
        nmax = at("neg_max", 150.5, [P, 8])
        den = at("denom", 150.53125, [P, 8])
        rden = at("denom_recip", 150.5625, [P, 8])
        qr = at("q_raw", 172, [P, S])
        qt = at("q_rotated", 176, [P, S])
        ovt = at("out_lo_part", 180, [64, HALF])
        vraw = at("v_weights_raw", 92, [P, KT, 272])
        vwh = at("v_weights_hi", 101, [P, KT, 272], FR)
        vwl = at("v_weights_lo", 110, [P, KT, 272], FR)
        xbc = at("xbc", 64, [P, XBC_T, S])
        cv = at("conv_in", 112, [P, 2, S + 4])
        ct = at("conv_out", 121, [P, 2, S])
        zt = at("z_scaled", 129, [P, 2, S])
        zs = at("z_silu", 137, [P, 2, S])
        xc = at("xbc_chunk", 0, [P, XBC_T, P])
        rows = at("cum_rows", 6, [P, HEADS, P])
        dec = at("decay", 14, [P, HEADS, P])
        mt = at("mix_t", 22, [P, HEADS, P])
        xd = at("x_dt", 30, [P, HEADS, HD])
        xw = at("x_to_end", 34, [P, HEADS, HD])
        bt = at("b_tokens", 38, [P, GROUPS, P])
        cbm = at("cb_causal", 39, [P, GROUPS, P])
        st = at("state", 40, [P, HEADS, HD])
        yo = at("y_off", 44, [P, HEADS, HD])
        ya = at("y_tokens", 48, [P, HEADS, HD])
        hp = at("state_decayed", 52, [P, HEADS, HD])
        small = {n: at(n, 56 + 0.5 * i, [P, CH, HEADS]) for i, n in enumerate(
            ["dt_x", "dt_abs", "dt_e", "dt_u", "dt_ln", "dt_c", "dt", "adt", "acs", "eac", "tmp", "wend", "chd", "cst"])}
        arow = at("a_row", 63, [P, 2, HEADS])
        yt = at("y_features", 112, [P, 8, S])
        zr = at("z_in", 172, [P, 2, S])
        mixs = at("mixed_stream", 172, [P, 2, S])

        psum = ctx.enter_context(nc.psum_tensor("psum", [P, 8, 512], F32))

        def banks(b, n=1):
            return psum[:, b:b + n, :].rearrange("p b n -> p (b n)")

        x1 = nc.dram_tensor("x1_scratch", (KT, P, S), F32).ap()
        x2 = nc.dram_tensor("x2_scratch", (KT, P, S), F32).ap()
        zscr = nc.dram_tensor("z_scratch", (Z_T, P, S), F32).ap()
        mixed = nc.dram_tensor("mixed_scratch", (MIX_T, P, S), F32).ap()
        cum = nc.dram_tensor("cum_scratch", (P, P), F32).ap()

        def past(t, name):
            per = {"in": 16 * KT // 2, "out": 16 * KT // 2}.get(name, KT)
            return per * (int(t[1]) if name in ("in", "hi", "lo", "sq", "sum") else int(t[1]) - 1)

        RSTD = {t: n + 1 for n, t in enumerate(
            ("t0_pre", "t1_post", "t1_pre", "gt0", "gt1", "t2_post", "t2_pre", "t3_post"))}

        def tile_of(ap, n):
            return ap[bass.ds(n, 1)].rearrange("a p ... -> (a p) ...") if not isinstance(n, int) else ap[n]

        block = ctx.enter_context(nc.Block())

        def rstd_pe_cols(pe, ready, value):
            pe.wait_ge(sem(ready), value)
            for c in range(CH):
                mm = pe.matmul(psum[:, 6, c:c + 1], sqs[:, c * P:(c + 1) * P], ones[:, 0:1], start=True, stop=True)
            mm.then_inc(sem("rstd_sum_cols"), 1)

        def rstd_act(act, t, n):
            act.wait_ge(sem("rstd_sum_cols"), RSTD[t])
            act.activation(rc0[:], psum[:, 6, 0:CH], ACT.Sqrt, bias=cols[:, EPSC:EPSC + 1], scale=1.0 / n)\
               .then_inc(sem("rstd_rms"), 1)
            act.wait_ge(sem("rstd_row_mm"), RSTD[t])
            act.copy(rb[:], banks(4, 2)).then_inc(sem("rstd_rb"), 1)

        def rstd_dve(v, t):
            v.wait_ge(sem("rstd_rms"), RSTD[t])
            v.reciprocal(rc[:], rc0[:]).then_inc(sem("rstd_rc"), 1)
            v.wait_ge(sem("rstd_rc"), RSTD[t])
            v.tensor_tensor(diag[:], ident[:].unsqueeze(1).to_broadcast([P, CH, P]),
                            rc[:].unsqueeze(2).to_broadcast([P, CH, P]), ALU.mult).then_inc(sem("rstd_diag"), 1)

        def rstd_pe_rows(pe, t):
            pe.wait_ge(sem("rstd_diag"), RSTD[t])
            for h in range(NH2):
                mm = pe.matmul(banks(4 + h), ones[:], diag[:, 4 * h:4 * h + 4, :].rearrange("p a b -> p (a b)"),
                               start=True, stop=True)
            mm.then_inc(sem("rstd_row_mm"), 1)

        def post_act(act, t, done, base):
            for k in range(KT):
                act.wait_ge(sem(done), base + KT + k + 1)
                if k >= 2:
                    act.wait_ge(sem("turn_a_sum"), past(t, "a_sum") + k - 1)
                act.activation(sq[:, k % 2, :], acc[:, k, :], ACT.Square).then_inc(sem("turn_a_sq"), 1)

        def post_dve(v, t):
            for k in range(KT):
                v.wait_ge(sem("turn_a_sq"), past(t, "a_sq") + k + 1)
                if k == 0:
                    v.tensor_copy(sqs[:], sq[:, 0, :]).then_inc(sem("turn_a_sum"), 1)
                else:
                    v.wait_ge(sem("turn_a_sum"), past(t, "a_sum") + k)
                    v.tensor_tensor(sqs[:], sqs[:], sq[:, k % 2, :], ALU.add).then_inc(sem("turn_a_sum"), 1)

        def turn_sp(sp, t, src, dst, nxt):
            for k in range(KT):
                if k >= 2:
                    if nxt:
                        sp.wait_ge(sem("turn_lo"), past(t, "lo") + k - 1)
                        sp.wait_ge(sem("turn_sq"), past(t, "sq") + k - 1)
                    if dst is not None:
                        sp.wait_ge(sem(f"turn_out{k % 2}"), past(t, "out") + 16 * (k // 2))
                sp.dma_start(xs[:, k % 2, :], src[k]).then_inc(sem(f"turn_in{k % 2}"), 16)
                if dst is not None and k >= 1:
                    sp.wait_ge(sem("turn_x"), past(t, "x") + k)
                    sp.dma_start(dst[k - 1], xs[:, (k - 1) % 2, :]).then_inc(sem(f"turn_out{(k - 1) % 2}"), 16)
            if dst is not None:
                sp.wait_ge(sem("turn_x"), past(t, "x") + KT)
                sp.dma_start(dst[KT - 1], xs[:, 1, :]).then_inc(sem("turn_out1"), 16)
                for s in range(2):
                    sp.wait_ge(sem(f"turn_out{s}"), past(t, "out") + 16 * (KT // 2))

        def turn_dve(v, t, post, pre):
            def lo(k):
                v.wait_ge(sem("turn_hi"), past(t, "hi") + k + 1)
                v.scalar_tensor_tensor(out=nl[:, k, :], in0=xs[:, k % 2, :], scalar=cols[:, pre + k:pre + k + 1],
                                       in1=nh[:, k, :].bitcast(F32), op0=ALU.mult, op1=ALU.subtract)\
                 .then_inc(sem("turn_lo"), 1)

            for k in range(KT):
                if post is not None:
                    v.wait_ge(sem("rstd_rb"), RSTD[t + "_post"])
                    v.tensor_tensor(acc[:, k, :], acc[:, k, :], rb[:], ALU.mult).then_inc(sem("turn_scaled"), 1)
                v.wait_ge(sem(f"turn_in{k % 2}"), past(t, "in") + 16 * (k // 2 + 1))
                if post is not None:
                    v.wait_ge(sem("turn_scaled"), past(t, "scaled") + k + 1)
                    v.scalar_tensor_tensor(out=xs[:, k % 2, :], in0=acc[:, k, :], scalar=post[:, k:k + 1],
                                           in1=xs[:, k % 2, :], op0=ALU.mult, op1=ALU.add).then_inc(sem("turn_x"), 1)
                if pre is not None and k >= 1:
                    lo(k - 1)
            if pre is not None:
                lo(KT - 1)

        def turn_act(act, t, post, pre):
            for k in range(KT):
                if post is not None:
                    act.wait_ge(sem("turn_x"), past(t, "x") + k + 1)
                else:
                    act.wait_ge(sem(f"turn_in{k % 2}"), past(t, "in") + 16 * (k // 2 + 1))
                act.activation(nh[:, k, :], xs[:, k % 2, :], ACT.Copy, scale=cols[:, pre + k:pre + k + 1])\
                   .then_inc(sem("turn_hi"), 1)
                if k >= 2:
                    act.wait_ge(sem("turn_sum"), past(t, "sum") + k - 1)
                act.activation(sq[:, k % 2, :], xs[:, k % 2, :], ACT.Square).then_inc(sem("turn_sq"), 1)

        def turn_pool(g, t):
            for k in range(KT):
                g.wait_ge(sem("turn_sq"), past(t, "sq") + k + 1)
                if k == 0:
                    g.tensor_copy(sqs[:], sq[:, 0, :]).then_inc(sem("turn_sum"), 1)
                else:
                    g.wait_ge(sem("turn_sum"), past(t, "sum") + k)
                    g.tensor_tensor(sqs[:], sqs[:], sq[:, k % 2, :], ALU.add).then_inc(sem("turn_sum"), 1)

        def ffn_sp(sp, p, wgu, wd, start):
            start(sp)
            sp.dma_start(rawg[:], wgu[0]).then_inc(sem(p + "_gu_in"), 16)
            sp.dma_start(raww[:], wd[0]).then_inc(sem(p + "_d_in"), 16)
            with sp.Fori(1, FT) as j:
                sp.wait_ge(sem(p + "_gu_lo"), j)
                sp.dma_start(rawg[:], tile_of(wgu, j)).then_inc(sem(p + "_gu_in"), 16)
                sp.wait_ge(sem(p + "_d_lo"), j)
                sp.dma_start(raww[:], tile_of(wd, j)).then_inc(sem(p + "_d_in"), 16)

        def ffn_pe(pe, p, t):
            def pair(bank, slot, m, k, h):
                o, x = banks(bank), slice(h * HALF, (h + 1) * HALF)
                pe.matmul(o, guh[:, slot, m, k, :], nh[:, k, x], start=(k == 0), stop=False)
                pe.matmul(o, guh[:, slot, m, k, :], nl[:, k, x], start=False, stop=False)
                return pe.matmul(o, gul[:, slot, m, k, :], nh[:, k, x], start=False, stop=(k == KT - 1))

            def body(i, first):
                for s in range(2):
                    pe.wait_ge(sem(p + "_gu_lo"), 2 * i + s + 1)
                    if first and s == 0:
                        for k in range(KT):
                            pe.wait_ge(sem("turn_lo"), past(t, "lo") + k + 1)
                            for h in range(NH2):
                                for m in range(2):
                                    mm = pair(2 * h + m, s, m, k, h)
                        mm.then_inc(sem(p + "_gu_mm"), 2)
                        rstd_pe_cols(pe, "turn_sum", past(t, "sum") + KT)
                        rstd_pe_rows(pe, t + "_pre")
                        continue
                    for h in range(NH2):
                        u = 4 * i + 2 * s + h
                        wait(pe, p + "_up", u - 1)
                        for m in range(2):
                            for k in range(KT):
                                mm = pair(2 * h + m, s, m, k, h)
                        mm.then_inc(sem(p + "_gu_mm"), 1)
                pe.wait_ge(sem(p + "_d_lo"), 2 * i + 2)
                for h in range(NH2):
                    pe.wait_ge(sem(p + "_act_lo"), 4 * i + 3 + h)
                    if first and h == 0:
                        pe.wait_ge(sem("rstd_rb"), RSTD[t + "_pre"])
                    down_pe(pe, p, i, h)
            body(0, True)
            with pe.Fori(1, FG) as i:
                body(i, False)

        def down_pe(pe, p, i, h):
            for d in range(KT):
                u = 16 * i + 8 * h + d
                wait(pe, p + "_acc", u - 3)
                o, x = banks(4 + d % 4), slice(h * HALF, (h + 1) * HALF)
                for s in range(2):
                    pe.matmul(o, wh[:, s, d, :], acth[:, s, x], start=(s == 0), stop=False)
                    pe.matmul(o, wh[:, s, d, :], actl[:, s, x], start=False, stop=False)
                    mm = pe.matmul(o, wl[:, s, d, :], acth[:, s, x], start=False, stop=(s == 1))
                mm.then_inc(sem(p + "_down_mm"), 1)

        def down_dve(v, p, i, first):
            for h in range(NH2):
                for d in range(KT):
                    u = 16 * i + 8 * h + d
                    a_, b_ = acc[:, d, h * HALF:(h + 1) * HALF], banks(4 + d % 4)
                    v.wait_ge(sem(p + "_down_mm"), u + 1)
                    if first:
                        v.tensor_copy(a_, b_).then_inc(sem(p + "_acc"), 1)
                    else:
                        v.wait_ge(sem(p + "_acc"), u - 15)
                        v.tensor_tensor(a_, b_, a_, ALU.add).then_inc(sem(p + "_acc"), 1)

        def ffn_act(act, p, t, between):
            def gu_hi(j, s, used):
                act.wait_ge(sem(p + "_gu_in"), 16 * j + 16)
                wait(act, p + "_gu_mm", used)
                act.copy(guh[:, s], rawg[:]).then_inc(sem(p + "_gu_hi"), 1)

            def d_hi(j, s, used):
                act.wait_ge(sem(p + "_d_in"), 16 * j + 16)
                wait(act, p + "_down_mm", used)
                act.copy(wh[:, s], raww[:]).then_inc(sem(p + "_d_hi"), 1)

            def body(i, more):
                for s in range(2):
                    for h in range(NH2):
                        u = 4 * i + 2 * s + h
                        act.wait_ge(sem(p + "_gate"), u + 1)
                        wait(act, p + "_prod", u)
                        act.activation(ts[:], tg[:], ACT.Silu).then_inc(sem(p + "_silu"), 1)
                        act.wait_ge(sem(p + "_prod"), u + 1)
                        wait(act, p + "_down_mm", 16 * i - 8 + 8 * h)
                        act.copy(acth[:, s, h * HALF:(h + 1) * HALF], tu[:]).then_inc(sem(p + "_act_hi"), 1)
                    if more:
                        gu_hi(2 * i + 2 + s, s, 4 * i + 2 * s + 2)
                if more:
                    for s in range(2):
                        d_hi(2 * i + 2 + s, s, 16 * i + 16)

            for s in range(2):
                gu_hi(s, s, 0)
                d_hi(s, s, 0)
            yield
            body(0, True)
            between(act)
            with act.Fori(1, FG - 1) as i:
                body(i, True)
            body(FG - 1, False)
            yield

        def ffn_dve(v, p, t, between):
            def gu_lo(j, s):
                v.wait_ge(sem(p + "_gu_hi"), j + 1)
                v.tensor_tensor(gul[:, s], rawg[:], guh[:, s].bitcast(F32), ALU.subtract).then_inc(sem(p + "_gu_lo"), 1)

            def d_lo(j, s):
                v.wait_ge(sem(p + "_d_hi"), j + 1)
                v.tensor_tensor(wl[:, s], raww[:], wh[:, s].bitcast(F32), ALU.subtract).then_inc(sem(p + "_d_lo"), 1)

            def body(i, first, more):
                for s in range(2):
                    for h in range(NH2):
                        u = 4 * i + 2 * s + h
                        x = slice(h * HALF, (h + 1) * HALF)
                        v.wait_ge(sem(p + "_gu_mm"), u + 1)
                        wait(v, p + "_silu", u)
                        v.tensor_tensor(tg[:], banks(2 * h), rb[:, x], ALU.mult).then_inc(sem(p + "_gate"), 1)
                        wait(v, p + "_act_lo", u)
                        v.tensor_tensor(tu[:], banks(2 * h + 1), rb[:, x], ALU.mult).then_inc(sem(p + "_up"), 1)
                        v.wait_ge(sem(p + "_up"), u + 1)
                        v.wait_ge(sem(p + "_silu"), u + 1)
                        v.tensor_tensor(tu[:], ts[:], tu[:], ALU.mult).then_inc(sem(p + "_prod"), 1)
                        v.wait_ge(sem(p + "_act_hi"), u + 1)
                        v.tensor_tensor(actl[:, s, x], tu[:], acth[:, s, x].bitcast(F32), ALU.subtract)\
                         .then_inc(sem(p + "_act_lo"), 1)
                    if more:
                        gu_lo(2 * i + 2 + s, s)
                down_dve(v, p, i, first)
                if more:
                    for s in range(2):
                        d_lo(2 * i + 2 + s, s)

            for s in range(2):
                gu_lo(s, s)
                d_lo(s, s)
            yield
            v.wait_ge(sem("rstd_rb"), RSTD[t + "_pre"])
            body(0, True, True)
            between(v)
            with v.Fori(1, FG - 1) as i:
                body(i, False, True)
            body(FG - 1, False, False)
            yield

        FFN_ACC = 16 * (FG - 1)

        def rope_tables_dve(v):
            n = [0]

            def step(ins):
                n[0] += 1
                ins.then_inc(sem("rope_step"), 1)
                v.wait_ge(sem("rope_step"), n[0])
            v.wait_ge(sem("pos_in"), 16)
            v.wait_ge(sem("turn_sq"), past("t0", "sq") + KT)
            step(v.tensor_copy(turns[:], sin[:].bitcast(I32)))
            step(v.tensor_scalar(ang[:], turns[:], cols[:, INVF:INVF + 1], None, ALU.mult))
            step(v.tensor_scalar(turns[:], ang[:], float(np.float32(1 / TWO_PI)), ROUND, ALU.mult, ALU.add))
            step(v.tensor_scalar(turns[:], turns[:], ROUND, None, ALU.subtract))
            for c in (C1, C2, C3):
                step(v.scalar_tensor_tensor(out=ang[:], in0=turns[:], scalar=-c, in1=ang[:], op0=ALU.mult, op1=ALU.add))
            step(v.tensor_scalar(ang[:], ang[:], PI_IN, -PI_IN, ALU.min, ALU.max))
            v.wait_ge(sem("rope_sin"), 2)
            step(v.tensor_tensor(cos[:], cos[:], cos[:], ALU.mult))
            step(v.tensor_scalar(cos[:], cos[:], -2.0, 1.0, ALU.mult, ALU.add))

        def rope_tables_act(act):
            act.wait_ge(sem("rope_step"), 8)
            act.activation(cos[:], ang[:], ACT.Sin, scale=0.5).then_inc(sem("rope_sin"), 1)
            act.activation(sin[:], ang[:], ACT.Sin).then_inc(sem("rope_sin"), 1)

        def proj_pe(pe, q, n, slot, bank, gate=None, free=None):
            pe.wait_ge(sem(q + "_w_lo"), n + 1)
            for h in range(NH2):
                if free:
                    free(h)
                x = slice(h * HALF, (h + 1) * HALF)
                for k in range(KT):
                    if gate and h == 0:
                        pe.wait_ge(sem("turn_lo"), past(gate, "lo") + k + 1)
                    pe.matmul(banks(bank + h), wh[:, slot, k, :], nh[:, k, x], start=(k == 0), stop=False)
                    pe.matmul(banks(bank + h), wh[:, slot, k, :], nl[:, k, x], start=False, stop=False)
                    mm = pe.matmul(banks(bank + h), wl[:, slot, k, :], nh[:, k, x], start=False, stop=(k == KT - 1))
                mm.then_inc(sem(q + "_mm"), 1)

        def w_hi(act, q, n, slot, used):
            act.wait_ge(sem(q + "_w_in"), 16 * n + 16)
            wait(act, q + "_mm", used)
            act.copy(wh[:, slot], raww[:]).then_inc(sem(q + "_w_hi"), 1)

        def w_lo(v, q, n, slot):
            v.wait_ge(sem(q + "_w_hi"), n + 1)
            v.tensor_tensor(wl[:, slot], raww[:], wh[:, slot].bitcast(F32), ALU.subtract).then_inc(sem(q + "_w_lo"), 1)

        def w_sp(sp, q, src, count):
            sp.dma_start(raww[:], src[0]).then_inc(sem(q + "_w_in"), 16)
            with sp.Fori(1, count) as n:
                sp.wait_ge(sem(q + "_w_lo"), n)
                sp.dma_start(raww[:], tile_of(src, n)).then_inc(sem(q + "_w_in"), 16)

        NT = sum(i + 1 for i in range(CH))

        def cnt(i, j):
            return sum(x + 1 for x in range(i)) + j

        def events(i):
            half = (i + 1) // 2
            nxt = [("score", i + 1, hh) for hh in range(4)] if i + 1 < CH else []
            blocks = [("block", i, j) for j in range(i + 1)]
            return nxt[:2] + blocks[:half] + nxt[2:] + blocks[half:]

        def probs(i, hh):
            return (pe1 if i % 2 else pe0)[:, hh, :]

        def att_pe(pe, g, first):
            for t in range(3):
                def free(h, t=t):
                    if t < 2:
                        wait(pe, "at_max", 32 * g)
                    else:
                        wait(pe, "at_t_lo", NT * g)
                proj_pe(pe, "at", 3 * g + t, t % 2, 2 * t, "t1" if first and t == 0 else None, free)
                if first and t == 1:
                    rstd_pe_cols(pe, "turn_sum", past("t1", "sum") + KT)
                    rstd_pe_rows(pe, "t1_pre")
                    pe.wait_ge(sem("rstd_rb"), RSTD["t1_pre"])
            for t in range(3):
                pe.wait_ge(sem("at_raw"), 6 * g + 2 * t + 2)
                if t == 0:
                    wait(pe, "at_ov_add", 16 * g)
                    if first:
                        pe.wait_ge(sem("rstd_rms"), RSTD["t1_pre"])
                else:
                    pe.wait_ge(sem("at_sin"), 3 * g + t)
                for h in range(NH2):
                    mm = pe.matmul(banks(6 + h), rot[:], qr[:, h * HALF:(h + 1) * HALF], start=True, stop=True)
                mm.then_inc(sem("at_rot"), 1)
            if first:
                pe.wait_ge(sem("v_w_lo"), 1)
                for c in range(CH):
                    if c >= 4:
                        pe.wait_ge(sem("v_read"), 2 * (c - 3))
                    x = slice(c * P, (c + 1) * P)
                    for k in range(KT):
                        o = psum[:, c % 4, 0:272]
                        pe.matmul(o, nh[:, k, x], vwh[:, k, :], start=(k == 0), stop=False)
                        pe.matmul(o, nh[:, k, x], vwl[:, k, :], start=False, stop=False)
                        mm = pe.matmul(o, nl[:, k, x], vwh[:, k, :], start=False, stop=(k == KT - 1))
                    mm.then_inc(sem("v_mm"), 1)

            def score(i, hh):
                n = 32 * g + 4 * i + hh
                if first and i == 0 and hh < 2:
                    pe.wait_ge(sem("v_read"), 2 * CH)
                wait(pe, "at_max", n - 1)
                b, w = 64 * (hh % 2), (i + 1) * P
                for c in range(0, w, 512):
                    o = psum[:, 2 * (n % 2 if isinstance(n, int) else hh % 2) + c // 512, 0:min(512, w - c)]
                    q = slice(i * P, (i + 1) * P)
                    ks = slice(c, min(c + 512, w))
                    pe.matmul(o, qh[b:b + 64, hh // 2, q], kh[b:b + 64, ks], start=True, stop=False)
                    pe.matmul(o, qh[b:b + 64, hh // 2, q], kl[b:b + 64, ks], start=False, stop=False)
                    mm = pe.matmul(o, ql[b:b + 64, hh // 2, q], kh[b:b + 64, ks], start=False, stop=True)
                mm.then_inc(sem("at_score"), 1)

            def turn(i, j):
                n = NT * g + cnt(i, j)
                if j == 0:
                    pe.wait_ge(sem("at_norm"), 32 * g + 4 * i + 4)
                wait(pe, "at_t_lo", n - 1)
                for hh in range(4):
                    mm = pe.transpose(psum[:, 4 + cnt(i, j) % 2, hh * P:(hh + 1) * P],
                                      probs(i, hh)[:, j * P:(j + 1) * P], ident[:])
                mm.then_inc(sem("at_t_mm"), 1)

            def values(i, j):
                n = NT * g + cnt(i, j)
                s = cnt(i, j) % 2
                pe.wait_ge(sem("at_t_lo"), n + 1)
                if j == 0:
                    wait(pe, "at_ov_add", 2 * (8 * g + i - 1))
                    pe.wait_ge(sem("at_v_lo"), g + 1)
                pe.matmul(banks(6 + i % 2), vg[:, j].rearrange("p a d -> p (a d)"),
                          pth[:, s].rearrange("p a d -> p (a d)"), start=(j == 0), stop=False)
                pe.matmul(banks(6 + i % 2), vg[:, j].rearrange("p a d -> p (a d)"),
                          ptl[:, s].rearrange("p a d -> p (a d)"), start=False, stop=(j == i))\
                  .then_inc(sem("at_pv"), 1)

            pe.wait_ge(sem("at_qk_lo"), 3 * g + 3)
            for hh in range(4):
                score(0, hh)
            last = None
            for i in range(CH):
                for kind, x, y in events(i):
                    if kind == "score":
                        score(x, y)
                    else:
                        turn(x, y)
                        if last:
                            values(*last)
                        last = (x, y)
            values(*last)

        def att_act(act, g, first, more):
            w_hi(act, "at", 3 * g + 2, 0, 6 * g + 2)
            if first:
                rstd_act(act, "t1_pre", D)
                act.wait_ge(sem("v_in"), 16)
                act.copy(vwh[:], vraw[:]).then_inc(sem("v_w_hi"), 1)
            for t in range(3):
                act.wait_ge(sem("at_sum"), 3 * g + t + 1)
                o = qh[:, t, :] if t < 2 else kh[:]
                act.copy(o, qt[:]).then_inc(sem("at_qk_hi"), 1)
            if more:
                w_hi(act, "at", 3 * g + 3, 0, 6 * g + 6)
                w_hi(act, "at", 3 * g + 4, 1, 6 * g + 6)
            if first:
                act.wait_ge(sem("v_read"), 2 * CH)
            wait(act, "at_pv", NT * g)
            act.copy(vg[:, :, 0, :], vall[:, :, bass.ds(g * HD, HD)]).then_inc(sem("at_v_hi"), 1)

            def soft(i, hh):
                n, c = 32 * g + 4 * i + hh, 4 * (i % 2) + hh
                act.wait_ge(sem("at_max"), n + 1)
                pr = probs(i, hh)[:, 0:(i + 1) * P]
                act.activation(pr, pr, ACT.Exp, bias=nmax[:, c:c + 1], scale=-1.0, accum_out=den[:, c:c + 1])\
                   .then_inc(sem("at_exp"), 1)

            for hh in range(4):
                soft(0, hh)
            for i in range(CH):
                for kind, x, y in events(i):
                    if kind == "score":
                        soft(x, y)
                    else:
                        n, s = NT * g + cnt(x, y), cnt(x, y) % 2
                        act.wait_ge(sem("at_t_mm"), n + 1)
                        wait(act, "at_pv", n - 1)
                        act.copy(pth[:, s].rearrange("p a d -> p (a d)"), banks(4 + s)).then_inc(sem("at_t_hi"), 1)
                act.wait_ge(sem("at_pv"), NT * g + cnt(i, i) + 1)
                wait(act, "at_ov_add", 2 * (8 * g + i))
                act.copy(ovt[:], psum[64:128, 6 + i % 2, :]).then_inc(sem("at_ov_lo"), 1)

        def att_dve(v, g, first, more):
            w_lo(v, "at", 3 * g + 2, 0)
            if first:
                rstd_dve(v, "t1_pre")
                v.wait_ge(sem("rstd_rb"), RSTD["t1_pre"])
            for t in range(3):
                n = 3 * g + t
                for h in range(NH2):
                    x = slice(h * HALF, (h + 1) * HALF)
                    v.wait_ge(sem("at_mm"), 2 * n + h + 1)
                    wait(v, "at_rot", n)
                    wait(v, "at_sum", n)
                    v.scalar_tensor_tensor(out=qr[:, x], in0=banks(2 * t + h), scalar=0.125 if t < 2 else 1.0,
                                           in1=rb[:, x], op0=ALU.mult, op1=ALU.mult).then_inc(sem("at_raw"), 1)
                v.wait_ge(sem("at_raw"), 2 * n + 2)
                wait(v, "at_qk_lo", n)
                v.tensor_tensor(qt[:], qr[:], cos[:], ALU.mult).then_inc(sem("at_cos"), 1)
                v.wait_ge(sem("at_rot"), n + 1)
                v.wait_ge(sem("at_cos"), n + 1)
                v.tensor_tensor(qr[:], banks(6, 2), sin[:], ALU.mult).then_inc(sem("at_sin"), 1)
                v.wait_ge(sem("at_sin"), n + 1)
                v.tensor_tensor(qt[:], qt[:], qr[:], ALU.add).then_inc(sem("at_sum"), 1)
                v.wait_ge(sem("at_qk_hi"), n + 1)
                ho, lo = (qh[:, t, :], ql[:, t, :]) if t < 2 else (kh[:], kl[:])
                v.tensor_tensor(lo, qt[:], ho.bitcast(F32), ALU.subtract).then_inc(sem("at_qk_lo"), 1)
            if first:
                v.wait_ge(sem("v_w_hi"), 1)
                v.tensor_tensor(vwl[:], vraw[:], vwh[:].bitcast(F32), ALU.subtract).then_inc(sem("v_w_lo"), 1)
                for c in range(CH):
                    v.wait_ge(sem("v_mm"), c + 1)
                    v.tensor_scalar(vall[:, c, :], psum[:, c % 4, 0:256], rc[:, c:c + 1], None, ALU.mult)\
                     .then_inc(sem("v_read"), 1)
                    v.tensor_scalar(dtr[:, c, :], psum[:, c % 4, 256:272], rc[:, c:c + 1], None, ALU.mult)\
                     .then_inc(sem("v_read"), 1)
            if more:
                w_lo(v, "at", 3 * g + 3, 0)
                w_lo(v, "at", 3 * g + 4, 1)
            v.wait_ge(sem("at_v_hi"), g + 1)
            v.tensor_tensor(vg[:, :, 1, :], vall[:, :, bass.ds(g * HD, HD)], vg[:, :, 0, :].bitcast(F32), ALU.subtract)\
             .then_inc(sem("at_v_lo"), 1)
            def soft(i, hh):
                n, c, w = 32 * g + 4 * i + hh, 4 * (i % 2) + hh, (i + 1) * P
                v.wait_ge(sem("at_score"), n + 1)
                wait(v, "at_norm", n - 3)
                v.sem_inc(sem("at_softmax_go"), 1)
                v.wait_ge(sem("mask_in"), 16)
                v.tensor_tensor_reduce(probs(i, hh)[:, 0:w], banks(2 * (hh % 2), 2)[:, 0:w], mask[:, S - w:S],
                                       -1.0, 3.0e38, ALU.add, ALU.min, nmax[:, c:c + 1]).then_inc(sem("at_max"), 1)

            def recip(i, hh):
                n, c = 32 * g + 4 * i + hh, 4 * (i % 2) + hh
                v.wait_ge(sem("at_exp"), n + 1)
                v.reciprocal(rden[:, c:c + 1], den[:, c:c + 1]).then_inc(sem("at_rden"), 1)

            for hh in range(4):
                soft(0, hh)
            for hh in range(4):
                recip(0, hh)
            for i in range(CH):
                todo = []
                for kind, x, y in events(i):
                    if kind == "score":
                        soft(x, y)
                        todo.append((x, y))
                    else:
                        for z in todo:
                            recip(*z)
                        todo = []
                        n, s = NT * g + cnt(x, y), cnt(x, y) % 2
                        v.wait_ge(sem("at_t_hi"), n + 1)
                        v.tensor_tensor(ptl[:, s].rearrange("p a d -> p (a d)"), banks(4 + s),
                                        pth[:, s].rearrange("p a d -> p (a d)").bitcast(F32), ALU.subtract)\
                         .then_inc(sem("at_t_lo"), 1)
                for z in todo:
                    recip(*z)
                v.wait_ge(sem("at_ov_lo"), 8 * g + i + 1)
                if i == 0:
                    wait(v, "att_out", 16 * g)
                for par in range(2):
                    ov = psum[0:64, 6 + i % 2, :].rearrange("p (t a q) -> p t a q", t=2, a=2)[:, :, par, :]
                    tv = ovt[:].rearrange("p (t a q) -> p t a q", t=2, a=2)[:, :, par, :]
                    v.tensor_tensor(attg[64 * par:64 * par + 64, :, i * P:(i + 1) * P], ov, tv, ALU.add)\
                     .then_inc(sem("at_ov_add"), 1)

        def att_pool(gp, g):
            def norm(i, hh):
                n, c = 32 * g + 4 * i + hh, 4 * (i % 2) + hh
                gp.wait_ge(sem("at_rden"), n + 1)
                gp.sem_inc(sem("at_norm_go"), 1)
                pr = probs(i, hh)[:, 0:(i + 1) * P]
                gp.tensor_scalar(pr, pr, rden[:, c:c + 1], 1.0, ALU.mult, ALU.mult).then_inc(sem("at_norm"), 1)
            for i in range(CH):
                for hh in range(4):
                    norm(i, hh)

        def xz_pe(pe):
            def tile(n, s):
                def free(h):
                    wait(pe, "xz_read", 2 * n - 2)
                proj_pe(pe, "xz", n, s, 2 * s, None, free)
            pe.wait_ge(sem("at_max"), 32 * KVH)
            for s in range(2):
                tile(s, s)
            with pe.Fori(1, (XBC_T + Z_T) // 2) as i:
                for s in range(2):
                    tile(2 * i + s, s)

        def xz_act(act):
            def tile(n, s, conv, more):
                if conv:
                    act.wait_ge(sem("xz_out"), n + 1)
                    act.activation(xbc[:, bass.ds(n, 1), :].rearrange("p a s -> p (a s)"), ct[:, s, :], ACT.Silu)\
                       .then_inc(sem("xz_silu"), 1)
                else:
                    act.wait_ge(sem("xz_read"), 2 * n + 2)
                    act.activation(zs[:, s, :], zt[:, s, :], ACT.Silu).then_inc(sem("z_silu"), 1)
                if more:
                    w_hi(act, "xz", n + 2, s, 2 * n + 2)
            w_hi(act, "xz", 0, 0, 0)
            w_hi(act, "xz", 1, 1, 0)
            for s in range(2):
                tile(s, s, True, True)
            with act.Fori(1, XBC_T // 2) as i:
                for s in range(2):
                    tile(2 * i + s, s, True, True)
            for i in range(Z_T // 2):
                for s in range(2):
                    if i:
                        act.wait_ge(sem(f"z_out{s}"), 16 * i)
                    tile(XBC_T + 2 * i + s, s, False, i + 1 < Z_T // 2)

        def xz_dve(v):
            def tile(n, s, conv, more):
                for h in range(NH2):
                    x = slice(h * HALF, (h + 1) * HALF)
                    v.wait_ge(sem("xz_mm"), 2 * n + h + 1)
                    if conv:
                        wait(v, "xz_out", n - 1)
                        o = cv[:, s, 3 + h * HALF:3 + (h + 1) * HALF]
                    else:
                        wait(v, "z_silu", n - XBC_T - 1)
                        o = zt[:, s, x]
                    v.tensor_tensor(o, banks(2 * s + h), rb[:, x], ALU.mult).then_inc(sem("xz_read"), 1)
                if conv:
                    v.wait_ge(sem("xz_read"), 2 * n + 2)
                    wait(v, "xz_silu", n - 1)
                    def col(j):
                        return cols[:, bass.ds(n + CONVW + 12 * j, 1)]
                    v.tensor_scalar(ct[:, s, :], cv[:, s, 3:3 + S], col(3), col(4), ALU.mult, ALU.add)\
                     .then_inc(sem("xz_tap"), 1)
                    for j in range(3):
                        v.wait_ge(sem("xz_tap"), 3 * n + j + 1)
                        v.scalar_tensor_tensor(out=ct[:, s, :], in0=cv[:, s, j:j + S], scalar=col(j), in1=ct[:, s, :],
                                               op0=ALU.mult, op1=ALU.add).then_inc(sem("xz_tap" if j < 2 else "xz_out"), 1)
                if more:
                    w_lo(v, "xz", n + 2, s)
            w_lo(v, "xz", 0, 0)
            w_lo(v, "xz", 1, 1)
            v.wait_ge(sem("att_out"), 16 * KVH)
            v.memset(cv[:, :, 0:3], 0.0).then_inc(sem("cv_zero"), 1)
            v.wait_ge(sem("cv_zero"), 1)
            for s in range(2):
                tile(s, s, True, True)
            with v.Fori(1, XBC_T // 2) as i:
                for s in range(2):
                    tile(2 * i + s, s, True, True)
            for i in range(Z_T // 2):
                for s in range(2):
                    tile(XBC_T + 2 * i + s, s, False, i + 1 < Z_T // 2)

        def flat(x):
            return x.rearrange("p a b -> p (a b)")

        def ssd_prep_dve(v):
            sm = small
            v.wait_ge(sem("xz_mm"), 2 * (XBC_T + Z_T))
            v.wait_ge(sem("arow_in"), 16)
            v.tensor_tensor(sm["dt_x"][:], dtr[:], arow[:, 0, :].unsqueeze(1).to_broadcast([P, CH, HEADS]), ALU.add)\
             .then_inc(sem("sp_x"), 1)
            v.wait_ge(sem("sp_x"), 1)
            v.tensor_scalar(sm["tmp"][:], sm["dt_x"][:], -1.0, None, ALU.mult).then_inc(sem("sp_neg"), 1)
            v.wait_ge(sem("sp_neg"), 1)
            v.tensor_tensor(sm["dt_abs"][:], sm["dt_x"][:], sm["tmp"][:], ALU.max).then_inc(sem("sp_abs"), 1)
            v.wait_ge(sem("sp_e"), 1)
            v.tensor_scalar(sm["dt_u"][:], sm["dt_e"][:], 1.0, None, ALU.add).then_inc(sem("sp_u"), 1)
            v.wait_ge(sem("sp_u"), 1)
            v.tensor_scalar(sm["tmp"][:], sm["dt_u"][:], 1.0, None, ALU.subtract).then_inc(sem("sp_t"), 1)
            v.reciprocal(sm["wend"][:], sm["dt_u"][:]).then_inc(sem("sp_t"), 1)
            v.wait_ge(sem("sp_t"), 2)
            v.tensor_tensor(sm["dt_c"][:], sm["dt_e"][:], sm["tmp"][:], ALU.subtract).then_inc(sem("sp_t"), 1)
            v.wait_ge(sem("sp_t"), 3)
            v.tensor_tensor(sm["dt_c"][:], sm["dt_c"][:], sm["wend"][:], ALU.mult).then_inc(sem("sp_t"), 1)
            v.wait_ge(sem("sp_ln"), 1)
            v.wait_ge(sem("sp_t"), 4)
            v.tensor_tensor(sm["dt_c"][:], sm["dt_c"][:], sm["dt_ln"][:], ALU.add).then_inc(sem("sp_t"), 1)
            v.wait_ge(sem("sp_t"), 5)
            v.scalar_tensor_tensor(out=flat(sm["dt"]), in0=flat(sm["dt_x"]), scalar=0.0, in1=flat(sm["dt_c"]),
                                   op0=ALU.max, op1=ALU.add).then_inc(sem("sp_t"), 1)
            v.wait_ge(sem("sp_t"), 6)
            v.wait_ge(sem("sp_a"), 1)
            v.scalar_tensor_tensor(out=sm["adt"][:], in0=sm["dt"][:], scalar=-1.0,
                                   in1=arow[:, 1, :].unsqueeze(1).to_broadcast([P, CH, HEADS]),
                                   op0=ALU.mult, op1=ALU.mult).then_inc(sem("sp_adt"), 1)
            v.wait_ge(sem("sp_cum"), 3)
            v.tensor_copy(flat(sm["acs"]), psum[:, 0, 0:P]).then_inc(sem("sp_acs"), 1)
            v.tensor_copy(flat(sm["cst"]), psum[:, 2, 0:P]).then_inc(sem("sp_cst"), 1)
            v.wait_ge(sem("sp_acs"), 1)
            v.tensor_tensor(flat(sm["tmp"]), psum[:, 1, 0:P], flat(sm["acs"]), ALU.subtract).then_inc(sem("sp_d"), 1)
            v.wait_ge(sem("sp_exp"), 3)
            v.tensor_tensor(sm["wend"][:], sm["wend"][:], sm["dt"][:], ALU.mult).then_inc(sem("sp_wend"), 1)
            v.memset(st[:], 0.0).then_inc(sem("sp_wend"), 1)
            v.wait_ge(sem("sp_wend"), 2)

        def ssd_prep_act(act):
            sm = small
            act.wait_ge(sem("sp_abs"), 1)
            act.activation(sm["dt_e"][:], sm["dt_abs"][:], ACT.Exp, scale=-1.0).then_inc(sem("sp_e"), 1)
            act.wait_ge(sem("sp_u"), 1)
            act.activation(sm["dt_ln"][:], sm["dt_u"][:], ACT.Ln).then_inc(sem("sp_ln"), 1)
            act.activation(arow[:, 1, :], arow[:, 1, :], ACT.Exp).then_inc(sem("sp_a"), 1)
            act.wait_ge(sem("sp_acs"), 1)
            act.activation(flat(sm["eac"]), flat(sm["acs"]), ACT.Exp).then_inc(sem("sp_exp"), 1)
            act.wait_ge(sem("sp_d"), 1)
            act.activation(flat(sm["wend"]), flat(sm["tmp"]), ACT.Exp).then_inc(sem("sp_exp"), 1)
            act.activation(flat(sm["chd"]), psum[:, 1, 0:P], ACT.Exp).then_inc(sem("sp_exp"), 1)

        def ssd_prep_pe(pe):
            pe.wait_ge(sem("sp_adt"), 1)
            pe.wait_ge(sem("xz_read"), 2 * (XBC_T + Z_T))
            f = flat(small["adt"])
            pe.matmul(psum[:, 0, 0:P], tri[:], f, start=True, stop=True).then_inc(sem("sp_cum"), 1)
            pe.matmul(psum[:, 1, 0:P], ones[:], f, start=True, stop=True).then_inc(sem("sp_cum"), 1)
            pe.matmul(psum[:, 2, 0:P], f, tri[:], start=True, stop=True).then_inc(sem("sp_cum"), 1)

        def row_of(t, c):
            return small[t][:, bass.ds(c, 1), :].rearrange("p a h -> p (a h)").unsqueeze(2).to_broadcast([P, HEADS, HD])

        def ssd_pe(pe, c):
            pe.wait_ge(sem("sd_xc"), c + 1)
            if isinstance(c, int) and c == 0:
                pe.wait_ge(sem("sp_exp"), 3)
                pe.wait_ge(sem("sp_wend"), 2)
            else:
                pe.wait_ge(sem("sd_st"), c)
                pe.wait_ge(sem("sd_yt"), c)
            for t in range(8):
                mm = pe.transpose(banks(0, 2)[:, t * P:(t + 1) * P], xc[:, t, :], ident[:])
            mm.then_inc(sem("sd_x_mm"), 1)
            for g in range(GROUPS):
                mm = pe.transpose(psum[:, 2, g * P:(g + 1) * P], xc[:, BC0 + g, :], ident[:])
            mm.then_inc(sem("sd_b_mm"), 1)
            for g in range(GROUPS):
                mm = pe.matmul(psum[:, 3, g * P:(g + 1) * P], xc[:, BC0 + g, :], xc[:, BC0 + 2 + g, :],
                               start=True, stop=True)
            mm.then_inc(sem("sd_cb_mm"), 1)
            wait(pe, "sd_y", c)
            for g in range(GROUPS):
                mm = pe.matmul(banks(6 + g), xc[:, BC0 + 2 + g, :], flat(st[:, 8 * g:8 * g + 8, :]),
                               start=True, stop=True)
            mm.then_inc(sem("sd_yo_mm"), 1)
            pe.wait_ge(sem("sd_xd"), c + 1)
            pe.wait_ge(sem("sd_mt"), 2 * c + 2)
            for e in range(HEADS):
                mm = pe.matmul(banks(4, 2)[:, e * HD:(e + 1) * HD], mt[:, e, :], xd[:, e, :], start=True, stop=True)
            mm.then_inc(sem("sd_yd_mm"), 1)
            pe.wait_ge(sem("sd_xw"), c + 1)
            pe.wait_ge(sem("sd_bt"), c + 1)
            for g in range(GROUPS):
                mm = pe.matmul(banks(g), bt[:, g, :], flat(xw[:, 8 * g:8 * g + 8, :]), start=True, stop=True)
            mm.then_inc(sem("sd_st_mm"), 1)
            pe.wait_ge(sem("sd_y"), c + 1)
            pe.wait_ge(sem("sd_cbm"), c + 1)
            for t in range(8):
                mm = pe.transpose(banks(2, 2)[:, t * P:(t + 1) * P], flat(ya[:, 2 * t:2 * t + 2, :]), ident[:])
            mm.then_inc(sem("sd_y_mm"), 1)

        def ssd_dve(v, c):
            v.wait_ge(sem("sd_rows_in"), 16 * c + 16)
            wait(v, "sd_exp", c)
            v.tensor_tensor(dec[:], rows[:], small["acs"][:, bass.ds(c, 1), :].rearrange("p a h -> p (a h)")
                            .unsqueeze(2).to_broadcast([P, HEADS, P]), ALU.subtract).then_inc(sem("sd_diff"), 1)
            v.wait_ge(sem("sd_diff"), c + 1)
            wait(v, "sd_mt", 2 * c)
            v.tensor_scalar(flat(dec), flat(dec), 0.0, None, ALU.min).then_inc(sem("sd_min"), 1)
            v.wait_ge(sem("sd_x_mm"), c + 1)
            xp = banks(0, 2).rearrange("p (h d) -> p h d", h=HEADS)
            wait(v, "sd_st_mm", c)
            v.tensor_tensor(xd[:], xp, row_of("dt", c), ALU.mult).then_inc(sem("sd_xd"), 1)
            v.tensor_tensor(xw[:], xp, row_of("wend", c), ALU.mult).then_inc(sem("sd_xw"), 1)
            v.wait_ge(sem("sd_cb_mm"), c + 1)
            v.tensor_tensor(cbm[:], psum[:, 3, 0:2 * P].rearrange("p (g l) -> p g l", g=GROUPS),
                            tri[:].unsqueeze(1).to_broadcast([P, GROUPS, P]), ALU.mult).then_inc(sem("sd_cbm"), 1)
            v.wait_ge(sem("sd_cbm"), c + 1)
            v.wait_ge(sem("sd_exp"), c + 1)
            wait(v, "sd_yd_mm", c)
            for g in range(GROUPS):
                v.tensor_tensor(mt[:, 8 * g:8 * g + 8, :], dec[:, 8 * g:8 * g + 8, :],
                                cbm[:, g, :].unsqueeze(1).to_broadcast([P, 8, P]), ALU.mult).then_inc(sem("sd_mt"), 1)
            v.tensor_tensor(hp[:], st[:], row_of("chd", c), ALU.mult).then_inc(sem("sd_hp"), 1)
            v.wait_ge(sem("sd_yo_mm"), c + 1)
            v.tensor_tensor(yo[:], banks(6, 2).rearrange("p (h d) -> p h d", h=HEADS), row_of("eac", c), ALU.mult)\
             .then_inc(sem("sd_yo"), 1)
            v.wait_ge(sem("sd_yo"), c + 1)
            v.wait_ge(sem("sd_yd_mm"), c + 1)
            wait(v, "sd_y_mm", c)
            v.tensor_tensor(flat(ya), banks(4, 2), flat(yo), ALU.add).then_inc(sem("sd_y"), 1)
            v.wait_ge(sem("sd_st_mm"), c + 1)
            v.wait_ge(sem("sd_hp"), c + 1)
            v.tensor_tensor(flat(st), banks(0, 2), flat(hp), ALU.add).then_inc(sem("sd_st"), 1)
            v.wait_ge(sem("sd_st"), c + 1)

        def ssd_act(act, c):
            act.wait_ge(sem("sd_min"), c + 1)
            act.activation(flat(dec), flat(dec), ACT.Exp).then_inc(sem("sd_exp"), 1)
            act.wait_ge(sem("sd_b_mm"), c + 1)
            wait(act, "sd_st_mm", c)
            act.copy(flat(bt), psum[:, 2, 0:2 * P]).then_inc(sem("sd_bt"), 1)
            act.wait_ge(sem("sd_y_mm"), c + 1)
            act.copy(yt[:, :, bass.ds(c * P, P)], banks(2, 2).rearrange("p (t l) -> p t l", t=8)).then_inc(sem("sd_yt"), 1)

        def ssd_pool(g, c):
            if isinstance(c, int) and c == 0:
                g.wait_ge(sem("xz_silu"), XBC_T)
                g.wait_ge(sem("xz_mm"), 2 * (XBC_T + Z_T))
            else:
                g.wait_ge(sem("sd_yo_mm"), c)
            g.tensor_copy(xc[:], xbc[:, :, bass.ds(c * P, P)]).then_inc(sem("sd_xc"), 1)

        def gate_dve(v):
            for t in range(8):
                g, s = t // 4, t % 2
                v.wait_ge(sem("gt_z_in" + str(s)), 16 * (t // 2 + 1))
                v.scalar_tensor_tensor(out=yt[:, t, :], in0=xbc[:, t, :], scalar=cols[:, DSK + t:DSK + t + 1],
                                       in1=yt[:, t, :], op0=ALU.mult, op1=ALU.add).then_inc(sem("gt_skip"), 1)
                v.wait_ge(sem("gt_skip"), t + 1)
                v.tensor_tensor(yt[:, t, :], yt[:, t, :], zr[:, s, :], ALU.mult).then_inc(sem("gt_z"), 1)
                if t >= 1:
                    gate_sum(v, t - 1)
            gate_sum(v, 7)
            for g in range(GROUPS):
                if g:
                    rstd_dve(v, f"gt{g}")
                v.wait_ge(sem("rstd_rb"), RSTD[f"gt{g}"])
                for t in range(4 * g, 4 * g + 4):
                    v.scalar_tensor_tensor(out=yt[:, t, :], in0=yt[:, t, :], scalar=cols[:, SSMN + t:SSMN + t + 1],
                                           in1=rb[:], op0=ALU.mult, op1=ALU.mult).then_inc(sem("gt_y"), 1)

        def gate_sum(v, t):
            v.wait_ge(sem("gt_sq"), t + 1)
            if t % 4 == 0:
                if t == 4:
                    v.wait_ge(sem("rstd_sum_cols"), RSTD["gt0"])
                v.tensor_copy(sqs[:], sq[:, t % 2, :]).then_inc(sem("gt_sum"), 1)
            else:
                v.wait_ge(sem("gt_sum"), t)
                v.tensor_tensor(sqs[:], sqs[:], sq[:, t % 2, :], ALU.add).then_inc(sem("gt_sum"), 1)
            if t == 7:
                rstd_dve(v, "gt0")

        def gate_act(act):
            for t in range(8):
                act.wait_ge(sem("gt_z"), t + 1)
                if t >= 2:
                    act.wait_ge(sem("gt_sum"), t - 1)
                act.activation(sq[:, t % 2, :], yt[:, t, :], ACT.Square).then_inc(sem("gt_sq"), 1)
            rstd_act(act, "gt0", 512)
            act.wait_ge(sem("gt_y"), 4)
            rstd_act(act, "gt1", 512)

        def gate_pe(pe):
            rstd_pe_cols(pe, "gt_sum", 4)
            rstd_pe_rows(pe, "gt0")
            rstd_pe_cols(pe, "gt_sum", 8)
            pe.wait_ge(sem("rstd_rb"), RSTD["gt0"])
            rstd_pe_rows(pe, "gt1")

        def out_sp(sp):
            sp.wait_ge(sem("xz_mm"), 2 * (XBC_T + Z_T))
            sp.dma_start(raww[:], a["w_out"][0]).then_inc(sem("wo_d_in"), 16)
            for s in range(2):
                sp.wait_ge(sem("gt_z"), 8)
                sp.dma_start(mixs[:, s, :], mixed[s]).then_inc(sem(f"wo_m_in{s}"), 16)
            with sp.Fori(1, MIX_T // 2) as i:
                sp.wait_ge(sem("wo_d_lo"), 2 * i - 1)
                sp.dma_start(raww[:], tile_of(a["w_out"], 2 * i - 1)).then_inc(sem("wo_d_in"), 16)
                for s in range(2):
                    sp.wait_ge(sem("wo_act_lo"), 2 * i - 1 + s)
                    sp.dma_start(mixs[:, s, :], tile_of(mixed, 2 * i + s)).then_inc(sem(f"wo_m_in{s}"), 16)
                sp.wait_ge(sem("wo_d_lo"), 2 * i)
                sp.dma_start(raww[:], tile_of(a["w_out"], 2 * i)).then_inc(sem("wo_d_in"), 16)
            sp.wait_ge(sem("wo_d_lo"), MIX_T - 1)
            sp.dma_start(raww[:], a["w_out"][MIX_T - 1]).then_inc(sem("wo_d_in"), 16)

        def out_act(act):
            def body(i, s):
                act.wait_ge(sem("wo_d_in"), 16 * (2 * i + s) + 16)
                wait(act, "wo_down_mm", 16 * i)
                act.copy(wh[:, s], raww[:]).then_inc(sem("wo_d_hi"), 1)
                act.wait_ge(sem(f"wo_m_in{s}"), 16 * i + 16)
                act.copy(acth[:, s, :], mixs[:, s, :]).then_inc(sem("wo_act_hi"), 1)
            act.wait_ge(sem("gt_y"), 8)
            for s in range(2):
                body(0, s)
            with act.Fori(1, MIX_T // 2) as i:
                for s in range(2):
                    body(i, s)

        def out_dve(v):
            def body(i, first):
                for s in range(2):
                    v.wait_ge(sem("wo_d_hi"), 2 * i + s + 1)
                    v.tensor_tensor(wl[:, s], raww[:], wh[:, s].bitcast(F32), ALU.subtract).then_inc(sem("wo_d_lo"), 1)
                    v.wait_ge(sem("wo_act_hi"), 2 * i + s + 1)
                    v.tensor_tensor(actl[:, s, :], mixs[:, s, :], acth[:, s, :].bitcast(F32), ALU.subtract)\
                     .then_inc(sem("wo_act_lo"), 1)
                down_dve(v, "wo", i, first)
            body(0, True)
            with v.Fori(1, MIX_T // 2) as i:
                body(i, False)

        def out_pe(pe):
            def body(i):
                pe.wait_ge(sem("wo_d_lo"), 2 * i + 2)
                pe.wait_ge(sem("wo_act_lo"), 2 * i + 2)
                for h in range(NH2):
                    down_pe(pe, "wo", i, h)
            pe.wait_ge(sem("rstd_rb"), RSTD["gt1"])
            body(0)
            with pe.Fori(1, MIX_T // 2) as i:
                body(i)

        WO_ACC = 16 * (MIX_T // 2 - 1)

        @block.sync
        def _(sp):
            sp.dma_start(cols[:], a["cols"]).then_inc(sem("consts_in"), 16)
            for n, t in enumerate((ident, tri, ones, rot)):
                sp.dma_start(t[:], a["squares"][n]).then_inc(sem("consts_in"), 16)
            for k in range(2):
                sp.dma_start(xs[:, k, :], a["x"][k]).then_inc(sem(f"turn_in{k}"), 16)
            sp.dma_start(rawg[:], a["gu1"][0]).then_inc(sem("f1_gu_in"), 16)
            sp.dma_start(raww[:], a["d1"][0]).then_inc(sem("f1_d_in"), 16)
            for k in range(2, KT):
                sp.wait_ge(sem("turn_lo"), past("t0", "lo") + k - 1)
                sp.wait_ge(sem("turn_sq"), past("t0", "sq") + k - 1)
                sp.dma_start(xs[:, k % 2, :], a["x"][k]).then_inc(sem(f"turn_in{k % 2}"), 16)
            sp.dma_start(sin[:].bitcast(I32), a["pos"]).then_inc(sem("pos_in"), 16)
            with sp.Fori(1, FT) as j:
                sp.wait_ge(sem("f1_gu_lo"), j)
                sp.dma_start(rawg[:], tile_of(a["gu1"], j)).then_inc(sem("f1_gu_in"), 16)
                sp.wait_ge(sem("f1_d_lo"), j)
                sp.dma_start(raww[:], tile_of(a["d1"], j)).then_inc(sem("f1_d_in"), 16)
            sp.wait_ge(sem("f1_d_lo"), FT)
            sp.dma_start(raww[:], a["w_att"][0]).then_inc(sem("at_w_in"), 16)
            sp.wait_ge(sem("rope_sin"), 2)
            turn_sp(sp, "t1", a["x"], x1, True)
            sp.wait_ge(sem("f1_gu_mm"), 4 * FG)
            sp.wait_ge(sem("turn_x"), past("t1", "x") + KT)
            sp.dma_start(vraw[:], a["w_v"]).then_inc(sem("v_in"), 16)
            sp.dma_start(mask[:], a["mask"]).then_inc(sem("mask_in"), 16)
            sp.wait_ge(sem("at_w_lo"), 1)
            sp.dma_start(raww[:], a["w_att"][1]).then_inc(sem("at_w_in"), 16)
            sp.wait_ge(sem("at_w_lo"), 2)
            sp.dma_start(raww[:], a["w_att"][2]).then_inc(sem("at_w_in"), 16)
            with sp.Fori(0, KVH - 1) as g:
                for t in range(2):
                    sp.wait_ge(sem("at_w_lo"), 3 * g + 3 + t)
                    sp.dma_start(raww[:], tile_of(a["w_att"], 3 * g + 3 + t)).then_inc(sem("at_w_in"), 16)
                sp.wait_ge(sem("at_ov_add"), 16 * g + 16)
                sp.dma_start(mixed[bass.ds(2 * g, 2)].rearrange("t p s -> p t s"), attg[:]).then_inc(sem("att_out"), 16)
                sp.wait_ge(sem("at_w_lo"), 3 * g + 5)
                sp.dma_start(raww[:], tile_of(a["w_att"], 3 * g + 5)).then_inc(sem("at_w_in"), 16)
            sp.wait_ge(sem("at_w_lo"), 3 * KVH)
            sp.dma_start(raww[:], a["w_xz"][0]).then_inc(sem("xz_w_in"), 16)
            sp.wait_ge(sem("at_ov_add"), 16 * KVH)
            sp.dma_start(mixed[2 * KVH - 2:2 * KVH].rearrange("t p s -> p t s"), attg[:]).then_inc(sem("att_out"), 16)
            with sp.Fori(1, XBC_T) as n:
                sp.wait_ge(sem("xz_w_lo"), n)
                sp.dma_start(raww[:], tile_of(a["w_xz"], n)).then_inc(sem("xz_w_in"), 16)
            for n in range(Z_T):
                if XBC_T + n < XBC_T + Z_T:
                    sp.wait_ge(sem("xz_w_lo"), XBC_T + n)
                    sp.dma_start(raww[:], a["w_xz"][XBC_T + n]).then_inc(sem("xz_w_in"), 16)
                if n >= 2:
                    sp.wait_ge(sem("z_silu"), n - 1)
                    sp.dma_start(zscr[n - 2], zs[:, n % 2, :]).then_inc(sem(f"z_out{n % 2}"), 16)
            for n in range(Z_T - 2, Z_T):
                sp.wait_ge(sem("z_silu"), n + 1)
                sp.dma_start(zscr[n], zs[:, n % 2, :]).then_inc(sem(f"z_out{n % 2}"), 16)
            sp.wait_ge(sem("xz_mm"), 2 * (XBC_T + Z_T))
            sp.dma_start(arow[:], a["head_rows"]).then_inc(sem("arow_in"), 16)
            sp.wait_ge(sem("sp_cst"), 1)
            sp.dma_start(cum, flat(small["cst"])).then_inc(sem("cum_out"), 16)
            sp.wait_ge(sem("cum_out"), 16)

            def rows_in(c):
                src = cum[bass.ds(c * HEADS, HEADS)] if not isinstance(c, int) else cum[c * HEADS:(c + 1) * HEADS]
                sp.dma_start(flat(rows), src.rearrange("h l -> (h l)").unsqueeze(0).to_broadcast([P, HEADS * P]))\
                  .then_inc(sem("sd_rows_in"), 16)
            rows_in(0)
            with sp.Fori(1, CH) as c:
                sp.wait_ge(sem("sd_diff"), c)
                rows_in(c)
            for s in range(2):
                sp.wait_ge(sem(f"z_out{s}"), 16 * (Z_T // 2))
            for t in range(8):
                if t >= 2:
                    sp.wait_ge(sem("gt_z"), t - 1)
                sp.dma_start(zr[:, t % 2, :], zscr[t]).then_inc(sem(f"gt_z_in{t % 2}"), 16)
            for t in range(8):
                sp.wait_ge(sem("gt_y"), t + 1)
                sp.dma_start(mixed[8 + t], yt[:, t, :]).then_inc(sem("gt_out"), 16)
            sp.wait_ge(sem("gt_out"), 16 * 8)
            sp.wait_ge(sem("att_out"), 16 * KVH)
            out_sp(sp)
            sp.dma_start(rawg[:], a["gu2"][0]).then_inc(sem("f2_gu_in"), 16)
            sp.wait_ge(sem("wo_d_lo"), MIX_T)
            sp.dma_start(raww[:], a["d2"][0]).then_inc(sem("f2_d_in"), 16)
            sp.wait_ge(sem("wo_act_lo"), MIX_T)
            turn_sp(sp, "t2", x1, x2, True)
            with sp.Fori(1, FT) as j:
                sp.wait_ge(sem("f2_gu_lo"), j)
                sp.dma_start(rawg[:], tile_of(a["gu2"], j)).then_inc(sem("f2_gu_in"), 16)
                sp.wait_ge(sem("f2_d_lo"), j)
                sp.dma_start(raww[:], tile_of(a["d2"], j)).then_inc(sem("f2_d_in"), 16)
            turn_sp(sp, "t3", x2, a["out"], False)

        @block.tensor
        def _(pe):
            pe.wait_ge(sem("consts_in"), 16 * 5)
            ffn_pe(pe, "f1", "t0")
            rstd_pe_cols(pe, "turn_a_sum", past("t1", "a_sum") + KT)
            rstd_pe_rows(pe, "t1_post")
            att_pe(pe, 0, True)
            with pe.Fori(1, KVH) as g:
                att_pe(pe, g, False)
            xz_pe(pe)
            ssd_prep_pe(pe)
            ssd_pe(pe, 0)
            with pe.Fori(1, CH) as c:
                ssd_pe(pe, c)
            gate_pe(pe)
            out_pe(pe)
            rstd_pe_cols(pe, "turn_a_sum", past("t2", "a_sum") + KT)
            rstd_pe_rows(pe, "t2_post")
            ffn_pe(pe, "f2", "t2")
            rstd_pe_cols(pe, "turn_a_sum", past("t3", "a_sum") + KT)
            rstd_pe_rows(pe, "t3_post")

        @block.scalar
        def _(act):
            act.wait_ge(sem("consts_in"), 16 * 5)
            turn_act(act, "t0", None, NORM_COLS["ffn1_pre"])
            f = ffn_act(act, "f1", "t0", rope_tables_act)
            next(f)
            rstd_act(act, "t0_pre", D)
            next(f)
            post_act(act, "t1", "f1_acc", FFN_ACC)
            rstd_act(act, "t1_post", D)
            turn_act(act, "t1", True, NORM_COLS["mix_pre"])
            w_hi(act, "at", 0, 0, 0)
            w_hi(act, "at", 1, 1, 0)
            att_act(act, 0, True, True)
            with act.Fori(1, KVH - 1) as g:
                att_act(act, g, False, True)
            att_act(act, KVH - 1, False, False)
            xz_act(act)
            ssd_prep_act(act)
            ssd_act(act, 0)
            with act.Fori(1, CH) as c:
                ssd_act(act, c)
            gate_act(act)
            out_act(act)
            post_act(act, "t2", "wo_acc", WO_ACC)
            rstd_act(act, "t2_post", D)
            turn_act(act, "t2", True, NORM_COLS["ffn2_pre"])
            f = ffn_act(act, "f2", "t2", lambda act: None)
            next(f)
            rstd_act(act, "t2_pre", D)
            next(f)
            post_act(act, "t3", "f2_acc", FFN_ACC)
            rstd_act(act, "t3_post", D)

        @block.vector
        def _(v):
            v.wait_ge(sem("consts_in"), 16 * 5)
            v.tensor_scalar(hcols[:], cols[:, 0:48], 0.5, None, ALU.mult).then_inc(sem("half_cols"), 1)
            v.wait_ge(sem("half_cols"), 1)
            turn_dve(v, "t0", None, NORM_COLS["ffn1_pre"])
            f = ffn_dve(v, "f1", "t0", rope_tables_dve)
            next(f)
            rstd_dve(v, "t0_pre")
            next(f)
            post_dve(v, "t1")
            rstd_dve(v, "t1_post")
            turn_dve(v, "t1", hcols[:, 8:16], NORM_COLS["mix_pre"])
            w_lo(v, "at", 0, 0)
            w_lo(v, "at", 1, 1)
            att_dve(v, 0, True, True)
            with v.Fori(1, KVH - 1) as g:
                att_dve(v, g, False, True)
            att_dve(v, KVH - 1, False, False)
            xz_dve(v)
            ssd_prep_dve(v)
            ssd_dve(v, 0)
            with v.Fori(1, CH) as c:
                ssd_dve(v, c)
            v.wait_ge(sem("sd_yt"), CH)
            gate_dve(v)
            out_dve(v)
            post_dve(v, "t2")
            rstd_dve(v, "t2_post")
            turn_dve(v, "t2", cols[:, 24:32], NORM_COLS["ffn2_pre"])
            f = ffn_dve(v, "f2", "t2", lambda v: None)
            next(f)
            rstd_dve(v, "t2_pre")
            next(f)
            post_dve(v, "t3")
            rstd_dve(v, "t3_post")
            turn_dve(v, "t3", hcols[:, 40:48], None)

        @block.gpsimd
        def _(g):
            turn_pool(g, "t0")
            turn_pool(g, "t1")
            att_pool(g, 0)
            with g.Fori(1, KVH) as i:
                att_pool(g, i)
            ssd_pool(g, 0)
            with g.Fori(1, CH) as c:
                ssd_pool(g, c)
            turn_pool(g, "t2")


def shape_constants():
    r = np.arange(P)
    ident = np.eye(P)
    tri = (r[:, None] <= r[None, :]) * 1.0
    rot = np.zeros((P, P))
    for b in (0, HD):
        for i in range(HD // 2):
            rot[b + HD // 2 + i, b + i] = -1.0
            rot[b + i, b + HD // 2 + i] = 1.0
    squares = np.stack([ident, tri, np.ones((P, P)), rot]).astype(np.float32)
    dist = r[:, None] + (S - P) - np.arange(S)[None, :]
    times = sum((((dist >= 0) & (dist % dil == 0) & (dist <= (win // dil) * dil)) * 1) for win, dil in ((128, 1), (512, 4), (2048, 16)))
    mask = np.where(times > 0, np.log(np.maximum(times, 1)), -1e30).astype(np.float32)
    inv = (10000.0 ** (-np.arange(0, HD, 2, dtype=np.float64) / HD)).astype(np.float32)
    return squares, mask, np.tile(inv, 4)


def kernel(**inputs):
    import concourse.bacc as bacc
    from concourse.bass_utils import run_bass_kernel_spmd

    x = {n: np.asarray(v) for n, v in inputs.items()}
    squares, mask, inv = shape_constants()

    def col_tiles(w, lo, n):
        w = w[:, lo:lo + n * P].reshape(KT, P, n, P)
        return np.ascontiguousarray(w.transpose(2, 1, 0, 3))

    def row_tiles(w):
        return np.ascontiguousarray(w.reshape(-1, P, KT, P))

    def cols_of(v):
        return v.reshape(-1, P).T

    w_in = x["w_in"][0]
    k0, v0, c0 = HEADS * HD, (HEADS + KVH) * HD, (HEADS + 2 * KVH) * HD
    z0 = c0 + XBC_T * P
    q_tiles = col_tiles(w_in, 0, 8)
    att = []
    for g in range(KVH):
        kg = w_in[:, k0 + g * HD:k0 + (g + 1) * HD]
        att += [q_tiles[2 * g], q_tiles[2 * g + 1], col_tiles(np.concatenate([kg, kg], 1), 0, 1)[0]]
    w_v = np.concatenate([w_in[:, v0:c0], w_in[:, z0 + Z_T * P:]], 1).reshape(KT, P, 272).transpose(1, 0, 2)
    arrays = {
        "x": np.ascontiguousarray(x["x"][0].T).reshape(KT, P, S),
        "pos": np.ascontiguousarray(np.broadcast_to(x["positions"], (P, S))),
        "squares": squares,
        "mask": mask,
        "cols": np.ascontiguousarray(np.concatenate(
            [cols_of(x[n][0]) for n in ("ffn1_pre_norm", "ffn1_post_norm", "mix_pre_norm", "mix_post_norm",
                                        "ffn2_pre_norm", "ffn2_post_norm")]
            + [cols_of(x["conv_w"][0, j]) for j in range(4)] + [cols_of(x["conv_b"][0])]
            + [cols_of(x["ssm_norm"][0]), cols_of(np.repeat(x["d_skip"][0], HD))]
            + [inv[:, None], np.full((P, 1), EPS, np.float32)], 1)),
        "head_rows": np.ascontiguousarray(np.broadcast_to(np.stack([x["dt_bias"][0], x["a_log"][0]]), (P, 2, HEADS))),
        "w_att": np.stack(att),
        "w_v": np.ascontiguousarray(w_v),
        "w_xz": col_tiles(w_in, c0, XBC_T + Z_T),
        "w_out": row_tiles(x["w_out"][0]),
    }
    for n in (1, 2):
        gate, up = (col_tiles(x[f"ffn{n}_w_{m}"][0], 0, FT) for m in ("gate", "up"))
        arrays[f"gu{n}"] = np.ascontiguousarray(np.stack([gate, up], 2))
        arrays[f"d{n}"] = row_tiles(x[f"ffn{n}_w_down"][0])
    nc = bacc.Bacc("TRN2", target_bir_lowering=False, num_devices=1)
    a = {n: nc.dram_tensor("in_" + n, v.shape, mybir.dt.from_np(v.dtype), kind="ExternalInput").ap()
         for n, v in arrays.items()}
    a["out"] = nc.dram_tensor("out_x", (KT, P, S), F32, kind="ExternalOutput").ap()
    build(nc, a)
    r = run_bass_kernel_spmd(nc, [{"in_" + n: v for n, v in arrays.items()}], core_ids=[0])
    y = r.results[0]["out_x"]
    return np.ascontiguousarray(y.reshape(D, S).T).reshape(x["x"].shape)
```

```python
from contextlib import ExitStack

import numpy as np

import concourse.bass as bass
from concourse import mybir

F32 = mybir.dt.float32
FR = mybir.dt.float32r
I32 = mybir.dt.int32
ALU = mybir.AluOpType
ACT = mybir.ActivationFunctionType

P = 128
S = 1024
D = 1024
KT = D // P
HALF = 512
NH2 = S // HALF
FF = 2816
FT = FF // P
FG = FT // 2
HD = 64
HEADS = 16
KVH = 4
CH = S // P
XBC_T = 12
Z_T = 8
BC0 = 8
MIX_T = 16
ATT_T = 8
GROUPS = 2
EPS = 1e-6
KB = 1024
NORM_COLS = {"ffn1_pre": 0, "ffn1_post": 8, "mix_pre": 16, "mix_post": 24, "ffn2_pre": 32, "ffn2_post": 40}
CONVW, CONVB, SSMN, DSK, INVF, EPSC = 48, 96, 108, 116, 124, 125
NCOLS = 126
TWO_PI = 2 * np.pi
C1 = 6.28125
C2 = float(np.float32(np.floor((TWO_PI - C1) * 2**22) / 2**22))
C3 = float(np.float32(TWO_PI - C1 - C2))
ROUND = 12582912.0
PI_IN = 3.1415925


FFN_COUNTS = {"gu_in": 16 * FT, "d_in": 16 * FT, "gu_hi": FT, "gu_lo": FT, "d_hi": FT, "d_lo": FT,
              "gu_mm": 2 * FT, "gate": 2 * FT, "up": 2 * FT, "silu": 2 * FT, "prod": 2 * FT,
              "act_hi": 2 * FT, "act_lo": 2 * FT, "down_mm": 16 * FG, "acc": 16 * FG}


def build(nc, a):
    with ExitStack() as ctx:
        sems = {}

        def sem(name):
            if name[:3] in ("f1_", "f2_"):
                name = "ff_" + name[3:]
            if name not in sems:
                sems[name] = ctx.enter_context(nc.semaphore(name))
            return sems[name]

        map_base = -(-nc.sbuf_base // 64) * 64

        def at(name, kb, shape, dt=F32):
            return nc.alloc_sbuf_tensor_at(name, shape, dt, offset=map_base + int(kb * KB))

        def wait(eng, name, value):
            if not isinstance(value, int) or value > 0:
                eng.wait_ge(sem(name), value + (FFN_COUNTS[name[3:]] if name[:3] == "f2_" else 0))

        nh = at("norm_hi", 0, [P, KT, S], FR)
        nl = at("norm_lo", 32, [P, KT, S], FR)
        acc = at("acc", 64, [P, KT, S])
        acth = at("act_hi", 96, [P, 2, S], FR)
        actl = at("act_lo", 104, [P, 2, S], FR)
        rawg = at("raw_gate_up", 112, [P, 2, KT, P])
        guh = at("gate_up_hi", 120, [P, 2, 2, KT, P], FR)
        gul = at("gate_up_lo", 136, [P, 2, 2, KT, P], FR)
        raww = at("raw_tile", 152, [P, KT, P])
        wh = at("tile_hi", 156, [P, 2, KT, P], FR)
        wl = at("tile_lo", 164, [P, 2, KT, P], FR)
        xs = at("x_stream", 172, [P, 2, S])
        sq = at("squares", 180, [P, 2, S])
        diag = at("rstd_diagonal", 180, [P, CH, P])
        sqa = at("result_squares", 172, [P, 4, HALF])
        tg = at("gate_scaled", 180, [P, HALF])
        ts = at("gate_silu", 182, [P, HALF])
        tu = at("up_scaled", 184, [P, HALF])
        sqs = at("square_sums", 188, [P, S])
        rb = at("rstd_rows", 192, [P, S])
        cos = at("cos", 196, [P, S])
        sin = at("sin", 200, [P, S])
        ident = at("ident", 204, [P, P])
        tri = at("tri", 204.5, [P, P])
        ones = at("ones", 205, [P, P])
        rot = at("rot", 205.5, [P, P])
        cols = at("cols", 206, [P, NCOLS])
        rc0 = at("rms_col", 206.5, [P, CH])
        rc = at("rstd_col", 206.53125, [P, CH])
        hcols = at("half_post_cols", 206.5625, [P, 48])
        ang = at("angle", 172, [P, S])
        turns = at("turns", 176, [P, S])
        qh = at("q_hi", 64, [P, 2, S], FR)
        ql = at("q_lo", 72, [P, 2, S], FR)
        kh = at("k_hi", 80, [P, S], FR)
        kl = at("k_lo", 84, [P, S], FR)
        vg = at("v_hi_lo", 88, [P, CH, 2, HD], FR)
        pe0 = at("probs_even", 92, [P, 4, 7 * P])
        pe1 = at("probs_odd", 106, [P, 4, 8 * P])
        pth = at("probs_t_hi", 122, [P, 2, 4, P], FR)
        ptl = at("probs_t_lo", 126, [P, 2, 4, P], FR)
        attg = at("att_group", 130, [P, 2, S])
        mask = at("mask", 138, [P, S])
        vall = at("v_all", 142, [P, CH, 256])
        dtr = at("dt_raw", 150, [P, CH, HEADS])
        nmax = at("neg_max", 150.5, [P, 8])
        den = at("denom", 150.53125, [P, 8])
        rden = at("denom_recip", 150.5625, [P, 8])
        qr = at("q_raw", 172, [P, S])
        qn = at("q_k_next", 176, [P, 3, S])
        ovt = at("out_lo_part", 188, [64, HALF])
        vraw = at("v_weights_raw", 92, [P, KT, 272])
        vwh = at("v_weights_hi", 101, [P, KT, 272], FR)
        vwl = at("v_weights_lo", 110, [P, KT, 272], FR)
        xbc = at("xbc", 64, [P, XBC_T, S])
        cv = at("conv_in", 112, [P, 2, S + 4])
        ct = at("conv_out", 121, [P, 2, S])
        zt = at("z_scaled", 129, [P, 2, S])
        zs = at("z_silu", 137, [P, 2, S])
        xc = at("xbc_chunk", 0, [P, XBC_T, P])
        mixs = at("mixed_stream", 6, [P, 2, S])
        dec = at("decay", 14, [P, HEADS, P])
        mt = at("mix_t", 22, [P, HEADS, P])
        xd = at("x_dt", 30, [P, HEADS, HD])
        xw = at("x_to_end", 34, [P, HEADS, HD])
        bt = at("b_tokens", 38, [P, GROUPS, P])
        cbm = at("cb_causal", 39, [P, GROUPS, P])
        st = at("state", 40, [P, HEADS, HD])
        yo = at("y_off", 44, [P, HEADS, HD])
        ya = at("y_tokens", 48, [P, HEADS, HD])
        hp = at("state_decayed", 52, [P, HEADS, HD])
        xt = at("x_tokens", 56, [P, HEADS, HD])
        yt = at("y_features", 112, [P, 8, S])
        small = {n: at(n, 172 + 0.5 * i, [P, CH, HEADS]) for i, n in enumerate(
            ["dt_x", "dt_abs", "dt_e", "dt_u", "dt_ln", "dt_c", "dt", "adt", "acs", "eac", "tmp", "wend", "chd", "cst"])}
        arow = at("a_row", 179, [P, 2, HEADS])
        rows = at("cum_rows", 180, [P, HEADS, P])
        zr = at("z_in", 172, [P, 2, S])
        gsq = at("gate_squares", 48, [P, 2, S])
        out_slots = [(wh, wl, acth, actl),
                     (at("tile_hi_odd", 14, [P, 2, KT, P], FR), at("tile_lo_odd", 22, [P, 2, KT, P], FR),
                      at("act_hi_odd", 30, [P, 2, S], FR), at("act_lo_odd", 38, [P, 2, S], FR))]

        psum = ctx.enter_context(nc.psum_tensor("psum", [P, 8, 512], F32))

        def banks(b, n=1):
            return psum[:, b:b + n, :].rearrange("p b n -> p (b n)")

        x1 = nc.dram_tensor("x1_scratch", (KT, P, S), F32).ap()
        x2 = nc.dram_tensor("x2_scratch", (KT, P, S), F32).ap()
        zscr = nc.dram_tensor("z_scratch", (Z_T, P, S), F32).ap()
        mixed = nc.dram_tensor("attention_scratch", (ATT_T, P, S), F32).ap()
        cum = nc.dram_tensor("cum_scratch", (P, P), F32).ap()

        def past(t, name):
            per = {"in": 16 * KT // 2, "out": 16 * KT, "a_sq": 2 * KT, "a_sum": 2 * KT}.get(name, KT)
            return per * (int(t[1]) if name in ("hi", "lo", "sq", "sum") else int(t[1]) - 1)

        RSTD = {t: n + 1 for n, t in enumerate(
            ("t0_pre", "t1_post", "t1_pre", "gt0", "gt1", "t2_post", "t2_pre", "t3_post"))}

        def tile_of(ap, n):
            return ap[bass.ds(n, 1)].rearrange("a p ... -> (a p) ...") if not isinstance(n, int) else ap[n]

        block = ctx.enter_context(nc.Block())

        def rstd_pe_cols(pe, ready, value, bank=6):
            pe.wait_ge(sem(ready), value)
            for c in range(CH):
                mm = pe.matmul(psum[:, bank, c:c + 1], sqs[:, c * P:(c + 1) * P], ones[:, 0:1], start=True, stop=True)
            mm.then_inc(sem("rstd_sum_cols"), 1)

        def rstd_act_rms(act, t, n, bank=6):
            act.wait_ge(sem("rstd_sum_cols"), RSTD[t])
            act.activation(rc0[:], psum[:, bank, 0:CH], ACT.Sqrt, bias=cols[:, EPSC:EPSC + 1], scale=1.0 / n)\
               .then_inc(sem("rstd_rms"), 1)

        def rstd_act_rows(act, t, bank=4):
            act.wait_ge(sem("rstd_row_mm"), RSTD[t])
            act.copy(rb[:], banks(bank, 2)).then_inc(sem("rstd_rb"), 1)

        def rstd_act(act, t, n):
            rstd_act_rms(act, t, n)
            rstd_act_rows(act, t)

        def rstd_dve(v, t):
            v.wait_ge(sem("rstd_rms"), RSTD[t])
            v.reciprocal(rc[:], rc0[:]).then_inc(sem("rstd_rc"), 1)
            v.wait_ge(sem("rstd_rc"), RSTD[t])
            v.tensor_tensor(diag[:], ident[:].unsqueeze(1).to_broadcast([P, CH, P]),
                            rc[:].unsqueeze(2).to_broadcast([P, CH, P]), ALU.mult).then_inc(sem("rstd_diag"), 1)

        def rstd_pe_rows(pe, t, bank=4):
            pe.wait_ge(sem("rstd_diag"), RSTD[t])
            for h in range(NH2):
                mm = pe.matmul(banks(bank + h), ones[:], diag[:, 4 * h:4 * h + 4, :].rearrange("p a b -> p (a b)"),
                               start=True, stop=True)
            mm.then_inc(sem("rstd_row_mm"), 1)

        def post_act(act, t, done, base):
            for h in range(NH2):
                for d in range(KT):
                    n = past(t, "a_sq") + h * KT + d
                    wait(act, done, base + h * KT + d + 1)
                    if h or d >= 4:
                        act.wait_ge(sem("turn_a_sum"), n - 3)
                    act.activation(sqa[:, d % 4, :], acc[:, d, h * HALF:(h + 1) * HALF], ACT.Square)\
                       .then_inc(sem("turn_a_sq"), 1)

        def turn_sp(sp, t, src, dst, after=lambda k: None):
            sp.wait_ge(sem("turn_a_sum"), past(t, "a_sum") + 2 * KT)
            for k in range(KT):
                if k >= 2:
                    sp.wait_ge(sem("turn_x"), past(t, "x") + k - 1)
                    sp.dma_start(dst[k - 2], acc[:, k - 2, :]).then_inc(sem("turn_out"), 16)
                sp.dma_start(xs[:, k % 2, :], src[k]).then_inc(sem(f"turn_in{k % 2}"), 16)
                after(k)
            for k in range(KT - 2, KT):
                sp.wait_ge(sem("turn_x"), past(t, "x") + k + 1)
                sp.dma_start(dst[k], acc[:, k, :]).then_inc(sem("turn_out"), 16)

        def turn_dve(v, t, post, pre, after=lambda k: None):
            def lo(k):
                v.wait_ge(sem("turn_hi"), past(t, "hi") + k + 1)
                v.scalar_tensor_tensor(out=nl[:, k, :], in0=acc[:, k, :], scalar=cols[:, pre + k:pre + k + 1],
                                       in1=nh[:, k, :].bitcast(F32), op0=ALU.mult, op1=ALU.subtract)\
                 .then_inc(sem("turn_lo"), 1)

            for k in range(KT):
                if post is not None:
                    v.wait_ge(sem("rstd_rb"), RSTD[t + "_post"])
                    v.tensor_tensor(acc[:, k, :], acc[:, k, :], rb[:], ALU.mult).then_inc(sem("turn_scaled"), 1)
                    v.wait_ge(sem(f"turn_in{k % 2}"), past(t, "in") + 16 * (k // 2 + 1))
                    v.wait_ge(sem("turn_scaled"), past(t, "scaled") + k + 1)
                    v.scalar_tensor_tensor(out=acc[:, k, :], in0=acc[:, k, :], scalar=post[:, k:k + 1],
                                           in1=xs[:, k % 2, :], op0=ALU.mult, op1=ALU.add).then_inc(sem("turn_x"), 1)
                if pre is not None and k >= 1:
                    lo(k - 1)
                    after(k - 1)
            if pre is not None:
                lo(KT - 1)
                after(KT - 1)

        def turn_act(act, t, post, pre, after=lambda k: None):
            for k in range(KT):
                if post is not None:
                    act.wait_ge(sem("turn_x"), past(t, "x") + k + 1)
                else:
                    act.wait_ge(sem(f"x_in{k}"), 16)
                act.activation(nh[:, k, :], acc[:, k, :], ACT.Copy, scale=cols[:, pre + k:pre + k + 1])\
                   .then_inc(sem("turn_hi"), 1)
                if k >= 2:
                    act.wait_ge(sem("turn_sum"), past(t, "sum") + k - 1)
                act.activation(sq[:, k % 2, :], acc[:, k, :], ACT.Square).then_inc(sem("turn_sq"), 1)
                after(k)

        def turn_pool(g, t):
            for k in range(KT):
                g.wait_ge(sem("turn_sq"), past(t, "sq") + k + 1)
                if k == 0:
                    g.tensor_copy(sqs[:], sq[:, 0, :]).then_inc(sem("turn_sum"), 1)
                else:
                    g.wait_ge(sem("turn_sum"), past(t, "sum") + k)
                    g.tensor_tensor(sqs[:], sqs[:], sq[:, k % 2, :], ALU.add).then_inc(sem("turn_sum"), 1)

        def ffn_sp(sp, p, wgu, wd, start):
            start(sp)
            sp.dma_start(rawg[:], wgu[0]).then_inc(sem(p + "_gu_in"), 16)
            sp.dma_start(raww[:], wd[0]).then_inc(sem(p + "_d_in"), 16)
            with sp.Fori(1, FT) as j:
                wait(sp, p + "_gu_lo", j)
                sp.dma_start(rawg[:], tile_of(wgu, j)).then_inc(sem(p + "_gu_in"), 16)
                wait(sp, p + "_d_lo", j)
                sp.dma_start(raww[:], tile_of(wd, j)).then_inc(sem(p + "_d_in"), 16)

        def ffn_pe(pe, p, t):
            def pair(bank, slot, m, k, h):
                o, x = banks(bank), slice(h * HALF, (h + 1) * HALF)
                pe.matmul(o, guh[:, slot, m, k, :], nh[:, k, x], start=(k == 0), stop=False)
                pe.matmul(o, guh[:, slot, m, k, :], nl[:, k, x], start=False, stop=False)
                return pe.matmul(o, gul[:, slot, m, k, :], nh[:, k, x], start=False, stop=(k == KT - 1))

            def body(i, first):
                for s in range(2):
                    wait(pe, p + "_gu_lo", 2 * i + s + 1)
                    if first and s == 0:
                        for k in range(KT):
                            pe.wait_ge(sem("turn_lo"), past(t, "lo") + k + 1)
                            for h in range(NH2):
                                for m in range(2):
                                    mm = pair(2 * h + m, s, m, k, h)
                        mm.then_inc(sem(p + "_gu_mm"), 2)
                        rstd_pe_cols(pe, "turn_sum", past(t, "sum") + KT)
                        rstd_pe_rows(pe, t + "_pre")
                        continue
                    for h in range(NH2):
                        u = 4 * i + 2 * s + h
                        wait(pe, p + "_up", u - 1)
                        for m in range(2):
                            for k in range(KT):
                                mm = pair(2 * h + m, s, m, k, h)
                        mm.then_inc(sem(p + "_gu_mm"), 1)
                wait(pe, p + "_d_lo", 2 * i + 2)
                for h in range(NH2):
                    wait(pe, p + "_act_lo", 4 * i + 3 + h)
                    if first and h == 0:
                        pe.wait_ge(sem("rstd_rb"), RSTD[t + "_pre"])
                    down_pe(pe, p, i, h)
            body(0, True)
            with pe.Fori(1, FG) as i:
                body(i, False)

        def down_pe(pe, p, i, h, slots=(wh, wl, acth, actl)):
            w_h, w_l, a_h, a_l = slots
            for d in range(KT):
                u = 16 * i + 8 * h + d
                wait(pe, p + "_acc", u - 3)
                o, x = banks(4 + d % 4), slice(h * HALF, (h + 1) * HALF)
                for s in range(2):
                    pe.matmul(o, w_h[:, s, d, :], a_h[:, s, x], start=(s == 0), stop=False)
                    pe.matmul(o, w_h[:, s, d, :], a_l[:, s, x], start=False, stop=False)
                    mm = pe.matmul(o, w_l[:, s, d, :], a_h[:, s, x], start=False, stop=(s == 1))
                mm.then_inc(sem(p + "_down_mm"), 1)

        def down_dve(v, p, i, first, last=False, t=None, between=lambda h, d: None):
            def square_sum(h, d):
                n = past(t, "a_sum") + h * KT + d
                x = slice(h * HALF, (h + 1) * HALF)
                v.wait_ge(sem("turn_a_sq"), n + 1)
                if d == 0:
                    v.tensor_copy(sqs[:, x], sqa[:, d % 4, :]).then_inc(sem("turn_a_sum"), 1)
                else:
                    v.wait_ge(sem("turn_a_sum"), n)
                    v.tensor_tensor(sqs[:, x], sqs[:, x], sqa[:, d % 4, :], ALU.add).then_inc(sem("turn_a_sum"), 1)

            for h in range(NH2):
                for d in range(KT):
                    between(h, d)
                    u = 16 * i + 8 * h + d
                    a_, b_ = acc[:, d, h * HALF:(h + 1) * HALF], banks(4 + d % 4)
                    wait(v, p + "_down_mm", u + 1)
                    if first:
                        v.tensor_copy(a_, b_).then_inc(sem(p + "_acc"), 1)
                    else:
                        wait(v, p + "_acc", u - 15)
                        v.tensor_tensor(a_, b_, a_, ALU.add).then_inc(sem(p + "_acc"), 1)
                    if last and d:
                        square_sum(h, d - 1)
                if last:
                    square_sum(h, KT - 1)

        def ffn_act(act, p, t, between):
            def gu_hi(j, s, used):
                wait(act, p + "_gu_in", 16 * j + 16)
                wait(act, p + "_gu_mm", used)
                act.copy(guh[:, s], rawg[:]).then_inc(sem(p + "_gu_hi"), 1)

            def d_hi(j, s, used):
                wait(act, p + "_d_in", 16 * j + 16)
                wait(act, p + "_down_mm", used)
                act.copy(wh[:, s], raww[:]).then_inc(sem(p + "_d_hi"), 1)

            def body(i, more):
                for s in range(2):
                    for h in range(NH2):
                        u = 4 * i + 2 * s + h
                        wait(act, p + "_gate", u + 1)
                        wait(act, p + "_prod", u)
                        act.activation(ts[:], tg[:], ACT.Silu).then_inc(sem(p + "_silu"), 1)
                        wait(act, p + "_prod", u + 1)
                        wait(act, p + "_down_mm", 16 * i - 8 + 8 * h)
                        act.copy(acth[:, s, h * HALF:(h + 1) * HALF], tu[:]).then_inc(sem(p + "_act_hi"), 1)
                    if more:
                        gu_hi(2 * i + 2 + s, s, 4 * i + 2 * s + 2)
                if more:
                    for s in range(2):
                        d_hi(2 * i + 2 + s, s, 16 * i + 16)

            yield lambda k: {0: lambda: gu_hi(0, 0, 0), 5: lambda: d_hi(0, 0, 0), 6: lambda: gu_hi(1, 1, 0),
                             7: lambda: d_hi(1, 1, 0)}.get(k, lambda: None)()
            body(0, True)
            between(act)
            with act.Fori(1, FG - 1) as i:
                body(i, True)
            body(FG - 1, False)
            yield

        def ffn_dve(v, p, t, t_next, between):
            def gu_lo(j, s):
                wait(v, p + "_gu_hi", j + 1)
                v.tensor_tensor(gul[:, s], rawg[:], guh[:, s].bitcast(F32), ALU.subtract).then_inc(sem(p + "_gu_lo"), 1)

            def d_lo(j, s):
                wait(v, p + "_d_hi", j + 1)
                v.tensor_tensor(wl[:, s], raww[:], wh[:, s].bitcast(F32), ALU.subtract).then_inc(sem(p + "_d_lo"), 1)

            def body(i, first, more):
                for s in range(2):
                    for h in range(NH2):
                        u = 4 * i + 2 * s + h
                        x = slice(h * HALF, (h + 1) * HALF)
                        wait(v, p + "_gu_mm", u + 1)
                        wait(v, p + "_silu", u)
                        v.tensor_tensor(tg[:], banks(2 * h), rb[:, x], ALU.mult).then_inc(sem(p + "_gate"), 1)
                        wait(v, p + "_act_lo", u)
                        v.tensor_tensor(tu[:], banks(2 * h + 1), rb[:, x], ALU.mult).then_inc(sem(p + "_up"), 1)
                        wait(v, p + "_up", u + 1)
                        wait(v, p + "_silu", u + 1)
                        v.tensor_tensor(tu[:], ts[:], tu[:], ALU.mult).then_inc(sem(p + "_prod"), 1)
                        wait(v, p + "_act_hi", u + 1)
                        v.tensor_tensor(actl[:, s, x], tu[:], acth[:, s, x].bitcast(F32), ALU.subtract)\
                         .then_inc(sem(p + "_act_lo"), 1)
                    if more and s == 0:
                        gu_lo(2 * i + 2, 0)
                down_dve(v, p, i, first, not more, t_next, 
                         lambda h, d: gu_lo(2 * i + 3, 1) if more and (h, d) == (1, 0) else None)
                if more:
                    for s in range(2):
                        d_lo(2 * i + 2 + s, s)

            yield lambda k: {0: lambda: gu_lo(0, 0), 5: lambda: d_lo(0, 0), 6: lambda: gu_lo(1, 1),
                             7: lambda: d_lo(1, 1)}.get(k, lambda: None)()
            v.wait_ge(sem("rstd_rb"), RSTD[t + "_pre"])
            body(0, True, True)
            between(v)
            with v.Fori(1, FG - 1) as i:
                body(i, False, True)
            body(FG - 1, False, False)
            yield

        FFN_ACC = 16 * (FG - 1)

        def rope_tables_dve(v):
            n = [0]

            def step(ins):
                n[0] += 1
                ins.then_inc(sem("rope_step"), 1)
                v.wait_ge(sem("rope_step"), n[0])
            v.wait_ge(sem("pos_in"), 16)
            step(v.tensor_copy(turns[:], sin[:].bitcast(I32)))
            step(v.tensor_scalar(ang[:], turns[:], cols[:, INVF:INVF + 1], None, ALU.mult))
            step(v.tensor_scalar(turns[:], ang[:], float(np.float32(1 / TWO_PI)), ROUND, ALU.mult, ALU.add))
            step(v.tensor_scalar(turns[:], turns[:], ROUND, None, ALU.subtract))
            for c in (C1, C2, C3):
                step(v.scalar_tensor_tensor(out=ang[:], in0=turns[:], scalar=-c, in1=ang[:], op0=ALU.mult, op1=ALU.add))
            step(v.tensor_scalar(ang[:], ang[:], PI_IN, -PI_IN, ALU.min, ALU.max))
            v.wait_ge(sem("rope_sin"), 2)
            step(v.tensor_tensor(cos[:], cos[:], cos[:], ALU.mult))
            step(v.tensor_scalar(cos[:], cos[:], -2.0, 1.0, ALU.mult, ALU.add))

        def rope_tables_act(act):
            act.wait_ge(sem("rope_step"), 8)
            act.activation(cos[:], ang[:], ACT.Sin, scale=0.5).then_inc(sem("rope_sin"), 1)
            act.activation(sin[:], ang[:], ACT.Sin).then_inc(sem("rope_sin"), 1)

        def proj_pe(pe, q, n, slot, bank, gate=None, free=None):
            pe.wait_ge(sem(q + "_w_lo"), n + 1)
            for h in range(NH2):
                if free:
                    free(h)
                x = slice(h * HALF, (h + 1) * HALF)
                for k in range(KT):
                    if gate and h == 0:
                        pe.wait_ge(sem("turn_lo"), past(gate, "lo") + k + 1)
                    pe.matmul(banks(bank + h), wh[:, slot, k, :], nh[:, k, x], start=(k == 0), stop=False)
                    pe.matmul(banks(bank + h), wh[:, slot, k, :], nl[:, k, x], start=False, stop=False)
                    mm = pe.matmul(banks(bank + h), wl[:, slot, k, :], nh[:, k, x], start=False, stop=(k == KT - 1))
                mm.then_inc(sem(q + "_mm"), 1)

        def w_hi(act, q, n, slot, used):
            act.wait_ge(sem(q + "_w_in"), 16 * n + 16)
            wait(act, q + "_mm", used)
            act.copy(wh[:, slot], raww[:]).then_inc(sem(q + "_w_hi"), 1)

        def w_lo(v, q, n, slot):
            v.wait_ge(sem(q + "_w_hi"), n + 1)
            v.tensor_tensor(wl[:, slot], raww[:], wh[:, slot].bitcast(F32), ALU.subtract).then_inc(sem(q + "_w_lo"), 1)

        def w_sp(sp, q, src, count):
            sp.dma_start(raww[:], src[0]).then_inc(sem(q + "_w_in"), 16)
            with sp.Fori(1, count) as n:
                sp.wait_ge(sem(q + "_w_lo"), n)
                sp.dma_start(raww[:], tile_of(src, n)).then_inc(sem(q + "_w_in"), 16)

        NT = sum(i + 1 for i in range(CH))
        AHEAD = 0.15
        PARTS = 4

        def cnt(i, j):
            return sum(x + 1 for x in range(i)) + j

        def att_events(more):
            def unit(i):
                items = [((j + 0.5) / (i + 1), ("block", i, j)) for j in range(i + 1)]
                if i + 1 < CH:
                    items += [(hh * 0.18, ("score", i + 1, hh)) for hh in range(4)]
                items = [e for _, e in sorted(items)]
                if i:
                    items.insert(items.index(("block", i, 0)) + 1, ("end", i - 1))
                return items

            base = [("score", 0, hh) for hh in range(4)] + [e for i in range(CH) for e in unit(i)]
            if not more:
                return [("v_split",)] + base
            parts = []
            for n in range(12):
                if n % 4 < 2:
                    parts += [("part", n, q) for q in range(PARTS - 1)]
                parts.append(("piece", n))
                if n in (0, 3):
                    parts.append(("w", 1 if n == 0 else 2))
            last_score = base.index(("score", CH - 1, 3))
            ev, done = [("w", 0), ("v_split",)], 0
            for k, e in enumerate(base):
                ev.append(e)
                if k >= 3:
                    due = min(len(parts), int(len(parts) * (AHEAD + (1 - AHEAD) * (k - 3) / (last_score - 6))))
                    ev += parts[done:due]
                    done = max(done, due)
                if k == last_score:
                    ev.append(("split",))
            return ev

        FIRST_GROUP = ([("piece", n) for n in range(8)] + [("w", 2)]
                       + [x for n in range(4) for x in (("v", 2 * n), ("piece", 8 + n), ("v", 2 * n + 1))])

        def probs(i, hh):
            return (pe1 if i % 2 else pe0)[:, hh, :]

        def piece_pe(pe, g, n, inc=1, part=None):
            t, rotated, h = n // 4, n % 4 >= 2, n % 2
            x = slice(h * HALF, (h + 1) * HALF)
            tiles = range(KT) if part is None else range(part * KT // PARTS, (part + 1) * KT // PARTS)
            if rotated or tiles[0] == 0:
                wait(pe, "pj_read", 12 * g + n)
            if rotated:
                mm = pe.matmul(banks(7), rot[:], qr[:, x], start=True, stop=True)
            else:
                if tiles[0] == 0:
                    pe.wait_ge(sem("at_w_lo"), 3 * g + t + 1)
                for k in tiles:
                    pe.matmul(banks(7), wh[:, t % 2, k, :], nh[:, k, x], start=(k == 0), stop=False)
                    pe.matmul(banks(7), wh[:, t % 2, k, :], nl[:, k, x], start=False, stop=False)
                    mm = pe.matmul(banks(7), wl[:, t % 2, k, :], nh[:, k, x], start=False, stop=(k == KT - 1))
            if rotated or tiles[-1] == KT - 1:
                mm.then_inc(sem("pj_mm"), inc)

        def first_group_pe(pe):
            pe.wait_ge(sem("at_w_lo"), 2)
            for k in range(KT):
                pe.wait_ge(sem("turn_lo"), past("t1", "lo") + k + 1)
                for t in range(2):
                    for h in range(NH2):
                        x = slice(h * HALF, (h + 1) * HALF)
                        o = banks(2 * t + h)
                        pe.matmul(o, wh[:, t, k, :], nh[:, k, x], start=(k == 0), stop=False)
                        pe.matmul(o, wh[:, t, k, :], nl[:, k, x], start=False, stop=False)
                        mm = pe.matmul(o, wl[:, t, k, :], nh[:, k, x], start=False, stop=(k == KT - 1))
            mm.then_inc(sem("pj_mm"), 2)
            rstd_pe_cols(pe, "turn_sum", past("t1", "sum") + KT)
            rstd_pe_rows(pe, "t1_pre")
            for e in FIRST_GROUP:
                if e[0] == "v":
                    v_pe(pe, e[1])
                elif e[0] == "piece" and e[1] not in (0, 1, 4, 5):
                    piece_pe(pe, 0, e[1], 3 if e[1] == 3 else 1)

        def v_pe(pe, c):
            if c == 0:
                pe.wait_ge(sem("v_w_lo"), 1)
                pe.wait_ge(sem("rstd_rb"), RSTD["t1_pre"])
            if c >= 2:
                pe.wait_ge(sem("v_read"), 2 * (c - 1))
            x = slice(c * P, (c + 1) * P)
            o = psum[:, 4 + c % 2, 0:272]
            for k in range(KT):
                pe.matmul(o, nh[:, k, x], vwh[:, k, :], start=(k == 0), stop=False)
                pe.matmul(o, nh[:, k, x], vwl[:, k, :], start=False, stop=False)
                mm = pe.matmul(o, nl[:, k, x], vwh[:, k, :], start=False, stop=(k == KT - 1))
            mm.then_inc(sem("v_mm"), 1)

        def att_pe(pe, g, first, more):
            def score(i, hh):
                n = 32 * g + 4 * i + hh
                if i == 0 and hh == 0:
                    pe.wait_ge(sem("at_qk_lo"), 3 * g + 3)
                    if first:
                        pe.wait_ge(sem("v_read"), 2 * CH)
                wait(pe, "at_max", n - 1)
                b, w = 64 * (hh % 2), (i + 1) * P
                for c in range(0, w, 512):
                    o = psum[:, 2 * (hh % 2) + c // 512, 0:min(512, w - c)]
                    q = slice(i * P, (i + 1) * P)
                    ks = slice(c, min(c + 512, w))
                    pe.matmul(o, qh[b:b + 64, hh // 2, q], kh[b:b + 64, ks], start=True, stop=False)
                    pe.matmul(o, qh[b:b + 64, hh // 2, q], kl[b:b + 64, ks], start=False, stop=False)
                    mm = pe.matmul(o, ql[b:b + 64, hh // 2, q], kh[b:b + 64, ks], start=False, stop=True)
                mm.then_inc(sem("at_score"), 1)

            def turn(i, j):
                n = NT * g + cnt(i, j)
                if j == 0:
                    pe.wait_ge(sem("at_norm"), 32 * g + 4 * i + 4)
                wait(pe, "at_t_lo", n - 1)
                for hh in range(4):
                    mm = pe.transpose(psum[:, 4 + cnt(i, j) % 2, hh * P:(hh + 1) * P],
                                      probs(i, hh)[:, j * P:(j + 1) * P], ident[:])
                mm.then_inc(sem("at_t_mm"), 1)

            def values(i, j):
                n = NT * g + cnt(i, j)
                s = cnt(i, j) % 2
                pe.wait_ge(sem("at_t_lo"), n + 1)
                if j == 0:
                    wait(pe, "at_ov_add", 2 * (8 * g + i))
                    pe.wait_ge(sem("at_v_lo"), g + 1)
                v_hl = vg[:, j].rearrange("p a d -> p (a d)")
                pe.matmul(banks(6), v_hl, pth[:, s].rearrange("p a d -> p (a d)"), start=(j == 0), stop=False)
                pe.matmul(banks(6), v_hl, ptl[:, s].rearrange("p a d -> p (a d)"), start=False, stop=(j == i))\
                  .then_inc(sem("at_pv"), 1)

            last = None
            for e in att_events(more):
                if e[0] == "score":
                    score(e[1], e[2])
                elif e[0] == "part":
                    piece_pe(pe, g + 1, e[1], 1, e[2])
                elif e[0] == "piece":
                    piece_pe(pe, g + 1, e[1], 1, PARTS - 1)
                elif e[0] == "block":
                    turn(e[1], e[2])
                    if last:
                        values(*last)
                    last = e[1:]
            values(*last)

        def att_w_hi(act, g, t):
            used = 12 * g + 2 if t == 2 else 12 * (g - 1) + (10 if t == 0 else 6)
            act.wait_ge(sem("at_w_in"), 16 * (3 * g + t) + 16)
            wait(act, "pj_mm", used)
            act.copy(wh[:, t % 2], raww[:]).then_inc(sem("at_w_hi"), 1)

        def first_group_act(act):
            act.wait_ge(sem("v_in"), 16)
            act.copy(vwh[:], vraw[:]).then_inc(sem("v_w_hi"), 1)
            att_w_hi(act, 0, 2)
            act.wait_ge(sem("turn_out"), past("t2", "out"))
            qk_split_act(act, 0)

        def qk_split_act(act, g):
            act.wait_ge(sem("at_sum"), 6 * g + 6)
            wait(act, "at_score", 32 * g)
            for t in (2, 0, 1):
                act.copy(qh[:, t, :] if t < 2 else kh[:], qn[:, t, :]).then_inc(sem("at_qk_hi"), 1)

        def qk_split_dve(v, g):
            for m, t in enumerate((2, 0, 1)):
                v.wait_ge(sem("at_qk_hi"), 3 * g + m + 1)
                ho, lo = (qh[:, t, :], ql[:, t, :]) if t < 2 else (kh[:], kl[:])
                v.tensor_tensor(lo, qn[:, t, :], ho.bitcast(F32), ALU.subtract).then_inc(sem("at_qk_lo"), 1)

        def att_act(act, g, first, more):
            def soft(i, hh):
                n, c = 32 * g + 4 * i + hh, 4 * (i % 2) + hh
                act.wait_ge(sem("at_max"), n + 1)
                pr = probs(i, hh)[:, 0:(i + 1) * P]
                act.activation(pr, pr, ACT.Exp, bias=nmax[:, c:c + 1], scale=-1.0, accum_out=den[:, c:c + 1])\
                   .then_inc(sem("at_exp"), 1)

            for e in att_events(more):
                if e[0] == "split":
                    qk_split_act(act, g + 1)
                elif e[0] == "v_split":
                    if first:
                        act.wait_ge(sem("v_read"), 2 * CH)
                    wait(act, "at_pv", NT * g)
                    act.copy(vg[:, :, 0, :], vall[:, :, bass.ds(g * HD, HD)]).then_inc(sem("at_v_hi"), 1)
                elif e[0] == "score":
                    soft(e[1], e[2])
                elif e[0] == "w":
                    att_w_hi(act, g + 1, e[1])
                elif e[0] == "block":
                    n, s = NT * g + cnt(*e[1:]), cnt(*e[1:]) % 2
                    act.wait_ge(sem("at_t_mm"), n + 1)
                    wait(act, "at_pv", n - 1)
                    act.copy(pth[:, s].rearrange("p a d -> p (a d)"), banks(4 + s)).then_inc(sem("at_t_hi"), 1)
                elif e[0] == "end":
                    unit_end_act(act, g, e[1])
            unit_end_act(act, g, CH - 1)

        def unit_end_act(act, g, i):
            act.wait_ge(sem("at_pv"), NT * g + cnt(i, i) + 1)
            wait(act, "at_ov_add", 2 * (8 * g + i))
            act.copy(ovt[:], psum[64:128, 6, :]).then_inc(sem("at_ov_lo"), 1)

        def unit_end_dve(v, g, i):
            v.wait_ge(sem("at_ov_lo"), 8 * g + i + 1)
            if i == 0:
                wait(v, "att_out", 16 * g)
            for par in range(2):
                ov = psum[0:64, 6, :].rearrange("p (t a q) -> p t a q", t=2, a=2)[:, :, par, :]
                tv = ovt[:].rearrange("p (t a q) -> p t a q", t=2, a=2)[:, :, par, :]
                v.tensor_tensor(attg[64 * par:64 * par + 64, :, i * P:(i + 1) * P], ov, tv, ALU.add)\
                 .then_inc(sem("at_ov_add"), 1)

        def piece_dve(v, g, n, bank=7):
            t, rotated, h = n // 4, n % 4 >= 2, n % 2
            x = slice(h * HALF, (h + 1) * HALF)
            m = 2 * (3 * g + t)
            v.wait_ge(sem("pj_mm"), 12 * g + n + 1)
            if rotated:
                v.wait_ge(sem("at_cos"), m + h + 1)
                v.tensor_tensor(qr[:, x], banks(bank), sin[:, x], ALU.mult).then_inc(sem("pj_read"), 1)
                v.wait_ge(sem("pj_read"), 12 * g + n + 1)
                v.tensor_tensor(qn[:, t, x], qn[:, t, x], qr[:, x], ALU.add).then_inc(sem("at_sum"), 1)
            else:
                wait(v, "at_sum", m)
                v.scalar_tensor_tensor(out=qr[:, x], in0=banks(bank), scalar=0.125 if t < 2 else 1.0,
                                       in1=rb[:, x], op0=ALU.mult, op1=ALU.mult).then_inc(sem("pj_read"), 1)

        def first_group_dve(v):
            rstd_dve(v, "t1_pre")
            v.wait_ge(sem("v_w_hi"), 1)
            v.tensor_tensor(vwl[:], vraw[:], vwh[:].bitcast(F32), ALU.subtract).then_inc(sem("v_w_lo"), 1)
            v.wait_ge(sem("rstd_rb"), RSTD["t1_pre"])
            for e in FIRST_GROUP:
                if e[0] == "w":
                    w_lo(v, "at", 2, 0)
                elif e[0] == "piece":
                    n = e[1]
                    piece_dve(v, 0, n, {0: 0, 1: 1, 4: 2, 5: 3}.get(n, 7))
                else:
                    c = e[1]
                    v.wait_ge(sem("v_mm"), c + 1)
                    o = psum[:, 4 + c % 2, :]
                    v.tensor_scalar(vall[:, c, :], o[:, 0:256], rc[:, c:c + 1], None, ALU.mult)\
                     .then_inc(sem("v_read"), 1)
                    v.tensor_scalar(dtr[:, c, :], o[:, 256:272], rc[:, c:c + 1], None, ALU.mult)\
                     .then_inc(sem("v_read"), 1)
            qk_split_dve(v, 0)

        def att_dve(v, g, first, more):
            def soft(i, hh):
                n, c, w = 32 * g + 4 * i + hh, 4 * (i % 2) + hh, (i + 1) * P
                v.wait_ge(sem("at_score"), n + 1)
                wait(v, "at_norm", n - 3)
                v.sem_inc(sem("at_softmax_go"), 1)
                v.wait_ge(sem("mask_in"), 16)
                v.tensor_tensor_reduce(probs(i, hh)[:, 0:w], banks(2 * (hh % 2), 2)[:, 0:w], mask[:, S - w:S],
                                       -1.0, 3.0e38, ALU.add, ALU.min, nmax[:, c:c + 1]).then_inc(sem("at_max"), 1)

            def recip(i, hh):
                n, c = 32 * g + 4 * i + hh, 4 * (i % 2) + hh
                v.wait_ge(sem("at_exp"), n + 1)
                v.reciprocal(rden[:, c:c + 1], den[:, c:c + 1]).then_inc(sem("at_rden"), 1)

            todo = []
            for e in att_events(more):
                if e[0] == "score":
                    if len(todo) > 1:
                        recip(*todo.pop(0))
                    soft(e[1], e[2])
                    todo.append(e[1:])
                    continue
                if e[0] not in ("w", "part"):
                    for z in todo:
                        recip(*z)
                    todo = []
                if e[0] == "split":
                    qk_split_dve(v, g + 1)
                elif e[0] == "v_split":
                    v.wait_ge(sem("at_v_hi"), g + 1)
                    v.tensor_tensor(vg[:, :, 1, :], vall[:, :, bass.ds(g * HD, HD)], vg[:, :, 0, :].bitcast(F32),
                                    ALU.subtract).then_inc(sem("at_v_lo"), 1)
                elif e[0] == "w":
                    w_lo(v, "at", 3 * (g + 1) + e[1], e[1] % 2)
                elif e[0] == "piece":
                    piece_dve(v, g + 1, e[1])
                elif e[0] == "block":
                    n, s = NT * g + cnt(*e[1:]), cnt(*e[1:]) % 2
                    v.wait_ge(sem("at_t_hi"), n + 1)
                    v.tensor_tensor(ptl[:, s].rearrange("p a d -> p (a d)"), banks(4 + s),
                                    pth[:, s].rearrange("p a d -> p (a d)").bitcast(F32), ALU.subtract)\
                     .then_inc(sem("at_t_lo"), 1)
                elif e[0] == "end":
                    unit_end_dve(v, g, e[1])
            unit_end_dve(v, g, CH - 1)

        def piece_pool(gp, g, n):
            t, h = n // 4, n % 2
            if n % 4 < 2:
                x = slice(h * HALF, (h + 1) * HALF)
                gp.wait_ge(sem("pj_read"), 12 * g + n + 1)
                wait(gp, "at_qk_lo", 3 * g)
                gp.tensor_tensor(qn[:, t, x], qr[:, x], cos[:, x], ALU.mult).then_inc(sem("at_cos"), 1)

        def att_pool(gp, g, more):
            def norm(i, hh):
                n, c = 32 * g + 4 * i + hh, 4 * (i % 2) + hh
                gp.wait_ge(sem("at_rden"), n + 1)
                gp.sem_inc(sem("at_norm_go"), 1)
                pr = probs(i, hh)[:, 0:(i + 1) * P]
                gp.tensor_scalar(pr, pr, rden[:, c:c + 1], 1.0, ALU.mult, ALU.mult).then_inc(sem("at_norm"), 1)
            for e in att_events(more):
                if e[0] == "score":
                    norm(e[1], e[2])
                elif e[0] == "piece":
                    piece_pool(gp, g + 1, e[1])

        def xz_pe(pe):
            def tile(n, s):
                def free(h):
                    wait(pe, "xz_read", 2 * n - 2)
                proj_pe(pe, "xz", n, s, 2 * s, None, free)
            pe.wait_ge(sem("at_max"), 32 * KVH)
            for s in range(2):
                tile(s, s)
            with pe.Fori(1, (XBC_T + 4) // 2) as i:
                for s in range(2):
                    tile(2 * i + s, s)
            ssd_prep_pe(pe)
            for n in range(XBC_T + 4, XBC_T + Z_T):
                tile(n, n % 2)

        def xz_act(act):
            def tile(n, s, conv, more):
                if conv:
                    act.wait_ge(sem("xz_out"), n + 1)
                    act.activation(xbc[:, bass.ds(n, 1), :].rearrange("p a s -> p (a s)"), ct[:, s, :], ACT.Silu)\
                       .then_inc(sem("xz_silu"), 1)
                else:
                    act.wait_ge(sem("xz_read"), 2 * n + 2)
                    act.activation(zs[:, s, :], zt[:, s, :], ACT.Silu).then_inc(sem("z_silu"), 1)
                if more:
                    w_hi(act, "xz", n + 2, s, 2 * n + 2)
            w_hi(act, "xz", 0, 0, 0)
            w_hi(act, "xz", 1, 1, 0)
            for s in range(2):
                tile(s, s, True, True)
            with act.Fori(1, XBC_T // 2) as i:
                for s in range(2):
                    tile(2 * i + s, s, True, True)
            for i in range(Z_T // 2):
                for s in range(2):
                    if i:
                        act.wait_ge(sem(f"z_out{s}"), 16 * i)
                    tile(XBC_T + 2 * i + s, s, False, i + 1 < Z_T // 2)
                    if (i, s) == (0, 0):
                        ssd_prep_act_steps(act)
                    elif (i, s) == (2, 1):
                        ssd_prep_act_sums(act)

        def xz_dve(v):
            def tile(n, s, conv, more):
                for h in range(NH2):
                    x = slice(h * HALF, (h + 1) * HALF)
                    v.wait_ge(sem("xz_mm"), 2 * n + h + 1)
                    if conv:
                        wait(v, "xz_out", n - 1)
                        o = cv[:, s, 3 + h * HALF:3 + (h + 1) * HALF]
                    else:
                        wait(v, "z_silu", n - XBC_T - 1)
                        o = zt[:, s, x]
                    v.tensor_tensor(o, banks(2 * s + h), rb[:, x], ALU.mult).then_inc(sem("xz_read"), 1)
                if conv:
                    v.wait_ge(sem("xz_read"), 2 * n + 2)
                    wait(v, "xz_silu", n - 1)
                    def col(j):
                        return cols[:, bass.ds(n + CONVW + 12 * j, 1)]
                    v.tensor_scalar(ct[:, s, :], cv[:, s, 3:3 + S], col(3), col(4), ALU.mult, ALU.add)\
                     .then_inc(sem("xz_tap"), 1)
                    for j in range(3):
                        v.wait_ge(sem("xz_tap"), 3 * n + j + 1)
                        v.scalar_tensor_tensor(out=ct[:, s, :], in0=cv[:, s, j:j + S], scalar=col(j), in1=ct[:, s, :],
                                               op0=ALU.mult, op1=ALU.add).then_inc(sem("xz_tap" if j < 2 else "xz_out"), 1)
                if more:
                    w_lo(v, "xz", n + 2, s)
            w_lo(v, "xz", 0, 0)
            w_lo(v, "xz", 1, 1)
            v.wait_ge(sem("att_out"), 16 * KVH)
            v.memset(cv[:, :, 0:3], 0.0).then_inc(sem("cv_zero"), 1)
            v.wait_ge(sem("cv_zero"), 1)
            for s in range(2):
                tile(s, s, True, True)
            with v.Fori(1, XBC_T // 2) as i:
                for s in range(2):
                    tile(2 * i + s, s, True, True)
            for i in range(Z_T // 2):
                for s in range(2):
                    tile(XBC_T + 2 * i + s, s, False, i + 1 < Z_T // 2)
                    if (i, s) == (0, 0):
                        ssd_prep_dve_steps(v)
                    elif (i, s) == (2, 1):
                        ssd_prep_dve_sums(v)

        def flat(x):
            return x.rearrange("p a b -> p (a b)")

        def ssd_prep_dve_steps(v):
            sm = small
            v.wait_ge(sem("arow_in"), 16)
            v.tensor_tensor(sm["dt_x"][:], dtr[:], arow[:, 0, :].unsqueeze(1).to_broadcast([P, CH, HEADS]), ALU.add)\
             .then_inc(sem("sp_x"), 1)
            v.wait_ge(sem("sp_x"), 1)
            v.tensor_scalar(sm["tmp"][:], sm["dt_x"][:], -1.0, None, ALU.mult).then_inc(sem("sp_neg"), 1)
            v.wait_ge(sem("sp_neg"), 1)
            v.tensor_tensor(sm["dt_abs"][:], sm["dt_x"][:], sm["tmp"][:], ALU.max).then_inc(sem("sp_abs"), 1)
            v.wait_ge(sem("sp_e"), 1)
            v.tensor_scalar(sm["dt_u"][:], sm["dt_e"][:], 1.0, None, ALU.add).then_inc(sem("sp_u"), 1)
            v.wait_ge(sem("sp_u"), 1)
            v.tensor_scalar(sm["tmp"][:], sm["dt_u"][:], 1.0, None, ALU.subtract).then_inc(sem("sp_t"), 1)
            v.reciprocal(sm["wend"][:], sm["dt_u"][:]).then_inc(sem("sp_t"), 1)
            v.wait_ge(sem("sp_t"), 2)
            v.tensor_tensor(sm["dt_c"][:], sm["dt_e"][:], sm["tmp"][:], ALU.subtract).then_inc(sem("sp_t"), 1)
            v.wait_ge(sem("sp_t"), 3)
            v.tensor_tensor(sm["dt_c"][:], sm["dt_c"][:], sm["wend"][:], ALU.mult).then_inc(sem("sp_t"), 1)
            v.wait_ge(sem("sp_ln"), 1)
            v.wait_ge(sem("sp_t"), 4)
            v.tensor_tensor(sm["dt_c"][:], sm["dt_c"][:], sm["dt_ln"][:], ALU.add).then_inc(sem("sp_t"), 1)
            v.wait_ge(sem("sp_t"), 5)
            v.scalar_tensor_tensor(out=flat(sm["dt"]), in0=flat(sm["dt_x"]), scalar=0.0, in1=flat(sm["dt_c"]),
                                   op0=ALU.max, op1=ALU.add).then_inc(sem("sp_t"), 1)
            v.wait_ge(sem("sp_t"), 6)
            v.wait_ge(sem("sp_a"), 1)
            v.scalar_tensor_tensor(out=sm["adt"][:], in0=sm["dt"][:], scalar=-1.0,
                                   in1=arow[:, 1, :].unsqueeze(1).to_broadcast([P, CH, HEADS]),
                                   op0=ALU.mult, op1=ALU.mult).then_inc(sem("sp_adt"), 1)

        def ssd_prep_dve_sums(v):
            sm = small
            v.wait_ge(sem("sp_cum"), 3)
            v.tensor_copy(flat(sm["cst"]), psum[:, 7, 0:P]).then_inc(sem("sp_cst"), 1)
            v.tensor_copy(flat(sm["acs"]), psum[:, 4, 0:P]).then_inc(sem("sp_acs"), 1)
            v.wait_ge(sem("sp_acs"), 1)
            v.tensor_tensor(flat(sm["tmp"]), psum[:, 5, 0:P], flat(sm["acs"]), ALU.subtract).then_inc(sem("sp_d"), 1)
            v.wait_ge(sem("sp_exp"), 3)
            v.tensor_tensor(sm["wend"][:], sm["wend"][:], sm["dt"][:], ALU.mult).then_inc(sem("sp_wend"), 1)

        def ssd_prep_act_steps(act):
            sm = small
            act.wait_ge(sem("sp_abs"), 1)
            act.activation(sm["dt_e"][:], sm["dt_abs"][:], ACT.Exp, scale=-1.0).then_inc(sem("sp_e"), 1)
            act.wait_ge(sem("sp_u"), 1)
            act.activation(sm["dt_ln"][:], sm["dt_u"][:], ACT.Ln).then_inc(sem("sp_ln"), 1)
            act.activation(arow[:, 1, :], arow[:, 1, :], ACT.Exp).then_inc(sem("sp_a"), 1)

        def ssd_prep_act_sums(act):
            sm = small
            act.wait_ge(sem("sp_acs"), 1)
            act.activation(flat(sm["eac"]), flat(sm["acs"]), ACT.Exp).then_inc(sem("sp_exp"), 1)
            act.wait_ge(sem("sp_d"), 1)
            act.activation(flat(sm["wend"]), flat(sm["tmp"]), ACT.Exp).then_inc(sem("sp_exp"), 1)
            act.activation(flat(sm["chd"]), psum[:, 5, 0:P], ACT.Exp).then_inc(sem("sp_exp"), 1)

        def ssd_prep_pe(pe):
            pe.wait_ge(sem("sp_adt"), 1)
            f = flat(small["adt"])
            pe.matmul(psum[:, 4, 0:P], tri[:], f, start=True, stop=True).then_inc(sem("sp_cum"), 1)
            pe.matmul(psum[:, 5, 0:P], ones[:], f, start=True, stop=True).then_inc(sem("sp_cum"), 1)
            pe.matmul(psum[:, 7, 0:P], f, tri[:], start=True, stop=True).then_inc(sem("sp_cum"), 1)

        def row_of(t, c):
            return small[t][:, bass.ds(c, 1), :].rearrange("p a h -> p (a h)").unsqueeze(2).to_broadcast([P, HEADS, HD])

        def prepare_pe(pe, c):
            if isinstance(c, int) and c == 0:
                pe.wait_ge(sem("xz_read"), 2 * (XBC_T + Z_T))
            pe.wait_ge(sem("sd_xc"), c + 1)
            wait(pe, "sd_xt", c)
            for t in range(8):
                mm = pe.transpose(banks(0, 2)[:, t * P:(t + 1) * P], xc[:, t, :], ident[:])
            mm.then_inc(sem("sd_x_mm"), 1)
            wait(pe, "sd_cbm", c)
            for g in range(GROUPS):
                mm = pe.matmul(psum[:, 3, g * P:(g + 1) * P], xc[:, BC0 + g, :], xc[:, BC0 + 2 + g, :],
                               start=True, stop=True)
            mm.then_inc(sem("sd_cb_mm"), 1)
            wait(pe, "sd_bt", c)
            for g in range(GROUPS):
                mm = pe.transpose(psum[:, 2, g * P:(g + 1) * P], xc[:, BC0 + g, :], ident[:])
            mm.then_inc(sem("sd_b_mm"), 1)

        def outputs_pe(pe, c):
            if isinstance(c, int) and c == 0:
                pe.wait_ge(sem("sd_zero"), 1)
                pe.wait_ge(sem("sp_exp"), 3)
            wait(pe, "sd_st", c)
            for g in range(GROUPS):
                mm = pe.matmul(banks(6 + g), xc[:, BC0 + 2 + g, :], flat(st[:, 8 * g:8 * g + 8, :]),
                               start=True, stop=True)
            mm.then_inc(sem("sd_yo_mm"), 1)
            pe.wait_ge(sem("sd_xd"), c + 1)
            pe.wait_ge(sem("sd_mt"), 2 * c + 2)
            wait(pe, "sd_yt", c)
            for e in range(HEADS):
                mm = pe.matmul(banks(4, 2)[:, e * HD:(e + 1) * HD], mt[:, e, :], xd[:, e, :], start=True, stop=True)
            mm.then_inc(sem("sd_yd_mm"), 1)

        def state_pe(pe, c):
            pe.wait_ge(sem("sd_xw"), c + 1)
            pe.wait_ge(sem("sd_bt"), c + 1)
            pe.wait_ge(sem("sd_yo"), c + 1)
            for g in range(GROUPS):
                mm = pe.matmul(banks(6 + g), bt[:, g, :], flat(xw[:, 8 * g:8 * g + 8, :]), start=True, stop=True)
            mm.then_inc(sem("sd_st_mm"), 1)
            pe.wait_ge(sem("sd_y"), c + 1)
            for t in range(8):
                mm = pe.transpose(banks(4, 2)[:, t * P:(t + 1) * P], flat(ya[:, 2 * t:2 * t + 2, :]), ident[:])
            mm.then_inc(sem("sd_y_mm"), 1)

        def ssd_pe(pe):
            def step(c):
                outputs_pe(pe, c - 1)
                prepare_pe(pe, c)
                state_pe(pe, c - 1)
            prepare_pe(pe, 0)
            step(1)
            with pe.Fori(2, CH) as c:
                step(c)
            outputs_pe(pe, CH - 1)
            state_pe(pe, CH - 1)

        def ssd_dve(v):
            def diff(c):
                v.wait_ge(sem("sd_rows_in"), 16 * c + 16)
                wait(v, "sd_mt", 2 * c)
                v.tensor_tensor(dec[:], rows[:], small["acs"][:, bass.ds(c, 1), :].rearrange("p a h -> p (a h)")
                                .unsqueeze(2).to_broadcast([P, HEADS, P]), ALU.subtract).then_inc(sem("sd_diff"), 1)

            def x_and_cb(c):
                v.wait_ge(sem("sd_xt"), c + 1)
                wait(v, "sd_yd_mm", c)
                v.tensor_tensor(xd[:], xt[:], row_of("dt", c), ALU.mult).then_inc(sem("sd_xd"), 1)
                v.wait_ge(sem("sd_cb_mm"), c + 1)
                v.tensor_tensor(cbm[:], psum[:, 3, 0:2 * P].rearrange("p (g l) -> p g l", g=GROUPS),
                                tri[:].unsqueeze(1).to_broadcast([P, GROUPS, P]), ALU.mult).then_inc(sem("sd_cbm"), 1)

            def mix(c):
                v.wait_ge(sem("sd_exp"), c + 1)
                v.wait_ge(sem("sd_cbm"), c + 1)
                for g in range(GROUPS):
                    v.tensor_tensor(mt[:, 8 * g:8 * g + 8, :], dec[:, 8 * g:8 * g + 8, :],
                                    cbm[:, g, :].unsqueeze(1).to_broadcast([P, 8, P]), ALU.mult)\
                     .then_inc(sem("sd_mt"), 1)

            def output(c):
                v.wait_ge(sem("sd_yo_mm"), c + 1)
                v.tensor_tensor(yo[:], banks(6, 2).rearrange("p (h d) -> p h d", h=HEADS), row_of("eac", c), ALU.mult)\
                 .then_inc(sem("sd_yo"), 1)
                v.wait_ge(sem("sd_yo"), c + 1)
                v.wait_ge(sem("sd_yd_mm"), c + 1)
                wait(v, "sd_y_mm", c)
                v.tensor_tensor(flat(ya), banks(4, 2), flat(yo), ALU.add).then_inc(sem("sd_y"), 1)

            def state(c):
                v.wait_ge(sem("sd_st_mm"), c + 1)
                v.wait_ge(sem("sd_hp"), c + 1)
                v.tensor_tensor(flat(st), banks(6, 2), flat(hp), ALU.add).then_inc(sem("sd_st"), 1)

            def step(c):
                output(c - 1)
                x_and_cb(c)
                state(c - 1)
                mix(c)

            v.wait_ge(sem("xz_mm"), 2 * (XBC_T + Z_T))
            diff(0)
            v.memset(st[:], 0.0).then_inc(sem("sd_zero"), 1)
            x_and_cb(0)
            mix(0)
            diff(1)
            step(1)
            diff(2)
            out_w_lo(v, 0)
            with v.Fori(2, CH - 1) as c:
                step(c)
                diff(c + 1)
            step(CH - 1)
            out_w_lo(v, 1)
            output(CH - 1)
            state(CH - 1)

        def ssd_act(act):
            def features(c):
                wait(act, "sd_yo_mm", c)
                act.copy(xc[:], xbc[:, :, bass.ds(c * P, P)]).then_inc(sem("sd_xc"), 1)

            def prepare(c):
                act.wait_ge(sem("sd_diff"), c + 1)
                act.activation(flat(dec), flat(dec), ACT.Relu, scale=-1.0).then_inc(sem("sd_held"), 1)
                act.wait_ge(sem("sd_held"), c + 1)
                act.activation(flat(dec), flat(dec), ACT.Exp, scale=-1.0).then_inc(sem("sd_exp"), 1)
                act.wait_ge(sem("sd_x_mm"), c + 1)
                wait(act, "sd_xd", c)
                wait(act, "sd_xw", c)
                act.copy(flat(xt), banks(0, 2)).then_inc(sem("sd_xt"), 1)
                act.wait_ge(sem("sd_b_mm"), c + 1)
                wait(act, "sd_st_mm", c)
                act.copy(flat(bt), psum[:, 2, 0:2 * P]).then_inc(sem("sd_bt"), 1)

            def output(c):
                act.wait_ge(sem("sd_y_mm"), c + 1)
                act.copy(yt[:, :, bass.ds(c * P, P)], banks(4, 2).rearrange("p (t l) -> p t l", t=8))\
                   .then_inc(sem("sd_yt"), 1)

            def step(c):
                features(c)
                prepare(c)
                output(c - 1)

            act.wait_ge(sem("xz_silu"), XBC_T)
            act.wait_ge(sem("xz_mm"), 2 * (XBC_T + Z_T))
            features(0)
            prepare(0)
            step(1)
            out_w_hi(act, 0)
            with act.Fori(2, CH) as c:
                step(c)
            out_w_hi(act, 1)
            output(CH - 1)

        def ssd_pool(g):
            def decayed(c):
                wait(g, "sd_st", c)
                g.tensor_tensor(hp[:], st[:], row_of("chd", c), ALU.mult).then_inc(sem("sd_hp"), 1)

            def to_end(c):
                g.wait_ge(sem("sd_xt"), c + 1)
                wait(g, "sd_st_mm", c)
                g.tensor_tensor(xw[:], xt[:], row_of("wend", c), ALU.mult).then_inc(sem("sd_xw"), 1)

            g.wait_ge(sem("sd_zero"), 1)
            g.wait_ge(sem("sp_exp"), 3)
            g.wait_ge(sem("sp_wend"), 1)
            to_end(0)
            decayed(0)
            to_end(1)
            with g.Fori(2, CH) as c:
                decayed(c - 1)
                to_end(c)
            decayed(CH - 1)

        OUT_PAIRS = MIX_T // 2

        def out_w_hi(act, n):
            i, s = n // 2, n % 2
            act.wait_ge(sem("wo_d_in"), 16 * n + 16)
            wait(act, "wo_down_mm", 16 * (i - 1))
            act.copy(out_slots[i % 2][0][:, s], raww[:]).then_inc(sem("wo_d_hi"), 1)

        def out_w_lo(v, n):
            w_h, w_l = out_slots[n // 2 % 2][:2]
            v.wait_ge(sem("wo_d_hi"), n + 1)
            v.tensor_tensor(w_l[:, n % 2], raww[:], w_h[:, n % 2].bitcast(F32), ALU.subtract)\
             .then_inc(sem("wo_d_lo"), 1)

        def mixed_tile(n):
            return mixs[:, n % 2, :] if n < ATT_T else yt[:, n - ATT_T, :]

        def out_a_hi(act, n):
            i, s = n // 2, n % 2
            if n < ATT_T:
                act.wait_ge(sem(f"wo_m_in{s}"), 16 * i + 16)
            else:
                act.wait_ge(sem("gt_y"), n - ATT_T + 1)
            wait(act, "wo_down_mm", 16 * (i - 1))
            act.copy(out_slots[i % 2][2][:, s, :], mixed_tile(n)).then_inc(sem("wo_act_hi"), 1)

        def out_a_lo(v, n):
            a_h, a_l = out_slots[n // 2 % 2][2:]
            v.wait_ge(sem("wo_act_hi"), n + 1)
            v.tensor_tensor(a_l[:, n % 2, :], mixed_tile(n), a_h[:, n % 2, :].bitcast(F32), ALU.subtract)\
             .then_inc(sem("wo_act_lo"), 1)

        def out_sp(sp):
            def z(t):
                if t >= 2:
                    sp.wait_ge(sem("gt_z"), t - 1)
                sp.dma_start(zr[:, t % 2, :], zscr[t]).then_inc(sem(f"gt_z_in{t % 2}"), 16)

            def w(n):
                sp.wait_ge(sem("wo_d_lo"), n)
                sp.dma_start(raww[:], a["w_out"][n]).then_inc(sem("wo_d_in"), 16)

            def m(n):
                sp.wait_ge(sem("wo_act_lo"), n - 1)
                sp.dma_start(mixs[:, n % 2, :], mixed[n]).then_inc(sem(f"wo_m_in{n % 2}"), 16)

            for s in range(2):
                sp.wait_ge(sem(f"z_out{s}"), 16 * (Z_T // 2))
            for n in ("sd_yo", "sd_hp", "sd_xw"):
                sp.wait_ge(sem(n), CH)
            for f, n in ((z, 0), (z, 1), (w, 2), (m, 2), (m, 3), (z, 2), (w, 3), (z, 3), (z, 4), (m, 4), (z, 5), (w, 4),
                         (z, 6), (m, 5), (z, 7), (w, 5), (m, 6), (w, 6), (m, 7)):
                f(n)
            for n in range(7, MIX_T):
                w(n)

        def out_pe(pe):
            for i in range(OUT_PAIRS):
                pe.wait_ge(sem("wo_d_lo"), 2 * i + 2)
                pe.wait_ge(sem("wo_act_lo"), 2 * i + 2)
                if i == 0:
                    pe.wait_ge(sem("sd_yt"), CH)
                    pe.wait_ge(sem("sd_st"), CH)
                for h in range(NH2):
                    down_pe(pe, "wo", i, h, out_slots[i % 2])
                    if (i, h) == (1, 0):
                        rstd_pe_cols(pe, "gt_sum", 4, 2)
                    elif (i, h) == (2, 0):
                        rstd_pe_rows(pe, "gt0", 0)
                        rstd_pe_cols(pe, "gt_sum", 8, 2)
                    elif (i, h) == (3, 0):
                        pe.wait_ge(sem("rstd_rb"), RSTD["gt0"])
                        rstd_pe_rows(pe, "gt1", 0)

        def out_act(act):
            def square(t):
                act.wait_ge(sem("gt_z"), t + 1)
                if t >= 2:
                    act.wait_ge(sem("gt_sum"), t - 1)
                act.activation(gsq[:, t % 2, :], yt[:, t, :], ACT.Square).then_inc(sem("gt_sq"), 1)

            act.wait_ge(sem("sd_y_mm"), CH)
            act.wait_ge(sem("sd_st"), CH)
            for n in range(2):
                out_a_hi(act, n)
            for f, n in ((out_w_hi, 2), (out_a_hi, 2), (square, 0), (out_w_hi, 3), (out_a_hi, 3), (square, 1),
                         (square, 2), (square, 3), (out_w_hi, 4), (out_a_hi, 4), (square, 4), (square, 5),
                         (out_w_hi, 5), (out_a_hi, 5), (square, 6), (square, 7)):
                f(act, n) if f is not square else f(n)
            rstd_act_rms(act, "gt0", 512, 2)
            for n in (6, 7):
                out_w_hi(act, n)
                out_a_hi(act, n)
            rstd_act_rows(act, "gt0", 0)
            rstd_act_rms(act, "gt1", 512, 2)
            for n in (8, 9):
                out_w_hi(act, n)
                out_a_hi(act, n)
            act.wait_ge(sem("gt_y"), 4)
            rstd_act_rows(act, "gt1", 0)
            for n in range(10, MIX_T):
                out_w_hi(act, n)
                out_a_hi(act, n)

        def out_dve(v):
            def skip(t):
                v.scalar_tensor_tensor(out=yt[:, t, :], in0=xbc[:, t, :], scalar=cols[:, DSK + t:DSK + t + 1],
                                       in1=yt[:, t, :], op0=ALU.mult, op1=ALU.add).then_inc(sem("gt_skip"), 1)

            def normed(t):
                v.wait_ge(sem("rstd_rb"), RSTD[f"gt{t // 4}"])
                v.wait_ge(sem("gt_z"), t + 1)
                v.scalar_tensor_tensor(out=yt[:, t, :], in0=yt[:, t, :], scalar=cols[:, SSMN + t:SSMN + t + 1],
                                       in1=rb[:], op0=ALU.mult, op1=ALU.mult).then_inc(sem("gt_y"), 1)

            v.wait_ge(sem("sd_yt"), CH)
            for n in range(2):
                out_a_lo(v, n)
            skip(0)
            for i in range(OUT_PAIRS):
                def between(h, d):
                    if i == 0 and h == 0:
                        if d + 1 < KT:
                            skip(d + 1)
                        v.wait_ge(sem("gt_skip"), d + 1)
                    if i + 1 < OUT_PAIRS:
                        step = {(0, 2): (out_w_lo, 0), (0, 6): (out_a_lo, 0), (1, 2): (out_w_lo, 1),
                                (1, 5): (out_a_lo, 1)}.get((h, d))
                        if step:
                            step[0](v, 2 * i + 2 + step[1])
                    if i == 2 and h == 1 and d in (0, 2, 3, 4):
                        normed((0, 2, 3, 4).index(d))
                    if i == 3 and h == 1 and d % 2 == 0:
                        normed(4 + d // 2)
                    if (i, h, d) in ((2, 0, 0), (3, 0, 0)):
                        rstd_dve(v, f"gt{i - 2}")
                down_dve(v, "wo", i, i == 0, i == OUT_PAIRS - 1, "t2", between)

        def gate_pool(g):
            def total(t):
                g.wait_ge(sem("gt_sq"), t + 1)
                if t % 4 == 0:
                    if t == 4:
                        g.wait_ge(sem("rstd_sum_cols"), RSTD["gt0"])
                    g.tensor_copy(sqs[:], gsq[:, t % 2, :]).then_inc(sem("gt_sum"), 1)
                else:
                    g.wait_ge(sem("gt_sum"), t)
                    g.tensor_tensor(sqs[:], sqs[:], gsq[:, t % 2, :], ALU.add).then_inc(sem("gt_sum"), 1)
            for t in range(8):
                s = t % 2
                g.wait_ge(sem("gt_skip"), t + 1)
                g.wait_ge(sem(f"gt_z_in{s}"), 16 * (t // 2 + 1))
                g.tensor_tensor(yt[:, t, :], yt[:, t, :], zr[:, s, :], ALU.mult).then_inc(sem("gt_z"), 1)
                if t:
                    total(t - 1)
            total(7)

        WO_ACC = 16 * (OUT_PAIRS - 1)

        @block.sync
        def _(sp):
            sp.dma_start(cols[:], a["cols"]).then_inc(sem("consts_in"), 16)
            for n, t in enumerate((ident, tri, ones, rot)):
                sp.dma_start(t[:], a["squares"][n]).then_inc(sem("consts_in"), 16)
            for k in range(4):
                sp.dma_start(acc[:, k, :], a["x"][k]).then_inc(sem(f"x_in{k}"), 16)
            sp.dma_start(rawg[:], a["gu1"][0]).then_inc(sem("f1_gu_in"), 16)
            for k in range(4, KT):
                sp.dma_start(acc[:, k, :], a["x"][k]).then_inc(sem(f"x_in{k}"), 16)
            sp.dma_start(raww[:], a["d1"][0]).then_inc(sem("f1_d_in"), 16)
            sp.dma_start(sin[:].bitcast(I32), a["pos"]).then_inc(sem("pos_in"), 16)
            with sp.Fori(1, FT) as j:
                wait(sp, "f1_gu_lo", j)
                sp.dma_start(rawg[:], tile_of(a["gu1"], j)).then_inc(sem("f1_gu_in"), 16)
                wait(sp, "f1_d_lo", j)
                sp.dma_start(raww[:], tile_of(a["d1"], j)).then_inc(sem("f1_d_in"), 16)
            wait(sp, "f1_d_lo", FT)
            sp.dma_start(raww[:], a["w_att"][0]).then_inc(sem("at_w_in"), 16)

            def second_tile(k):
                if k == 3:
                    sp.wait_ge(sem("at_w_lo"), 1)
                    sp.dma_start(raww[:], a["w_att"][1]).then_inc(sem("at_w_in"), 16)
            turn_sp(sp, "t1", a["x"], x1, second_tile)
            sp.wait_ge(sem("turn_out"), past("t2", "out"))
            sp.wait_ge(sem("turn_lo"), past("t2", "lo"))
            sp.wait_ge(sem("turn_sq"), past("t2", "sq"))
            sp.dma_start(vraw[:], a["w_v"]).then_inc(sem("v_in"), 16)
            sp.dma_start(mask[:], a["mask"]).then_inc(sem("mask_in"), 16)
            sp.wait_ge(sem("at_w_lo"), 2)
            sp.dma_start(raww[:], a["w_att"][2]).then_inc(sem("at_w_in"), 16)
            sp.wait_ge(sem("at_w_lo"), 3)
            sp.dma_start(raww[:], a["w_att"][3]).then_inc(sem("at_w_in"), 16)

            def group_weights(g, tiles):
                for t in tiles:
                    sp.wait_ge(sem("at_w_lo"), 3 * g + 3 + t)
                    sp.dma_start(raww[:], tile_of(a["w_att"], 3 * g + 3 + t)).then_inc(sem("at_w_in"), 16)

            def group_out(g):
                sp.wait_ge(sem("at_ov_add"), 16 * g + 16)
                sp.dma_start(mixed[bass.ds(2 * g, 2)].rearrange("t p s -> p t s"), attg[:]).then_inc(sem("att_out"), 16)

            with sp.Fori(0, KVH - 2) as g:
                group_weights(g, (1, 2, 3))
                group_out(g)
            group_weights(KVH - 2, (1, 2))
            sp.wait_ge(sem("at_w_lo"), 3 * KVH)
            sp.dma_start(raww[:], a["w_xz"][0]).then_inc(sem("xz_w_in"), 16)
            sp.wait_ge(sem("at_qk_lo"), 3 * KVH)
            sp.dma_start(arow[:], a["head_rows"]).then_inc(sem("arow_in"), 16)
            group_out(KVH - 2)
            group_out(KVH - 1)
            with sp.Fori(1, XBC_T) as n:
                sp.wait_ge(sem("xz_w_lo"), n)
                sp.dma_start(raww[:], tile_of(a["w_xz"], n)).then_inc(sem("xz_w_in"), 16)
            for n in range(Z_T):
                if XBC_T + n < XBC_T + Z_T:
                    sp.wait_ge(sem("xz_w_lo"), XBC_T + n)
                    sp.dma_start(raww[:], a["w_xz"][XBC_T + n]).then_inc(sem("xz_w_in"), 16)
                if n >= 2:
                    sp.wait_ge(sem("z_silu"), n - 1)
                    sp.dma_start(zscr[n - 2], zs[:, n % 2, :]).then_inc(sem(f"z_out{n % 2}"), 16)
            for n in range(Z_T - 2, Z_T):
                sp.wait_ge(sem("z_silu"), n + 1)
                sp.dma_start(zscr[n], zs[:, n % 2, :]).then_inc(sem(f"z_out{n % 2}"), 16)
            sp.wait_ge(sem("sp_cst"), 1)
            sp.dma_start(cum, flat(small["cst"])).then_inc(sem("cum_out"), 16)
            sp.wait_ge(sem("cum_out"), 16)

            def rows_in(c):
                src = cum[bass.ds(c * HEADS, HEADS)] if not isinstance(c, int) else cum[c * HEADS:(c + 1) * HEADS]
                sp.dma_start(flat(rows), src.rearrange("h l -> (h l)").unsqueeze(0).to_broadcast([P, HEADS * P]))\
                  .then_inc(sem("sd_rows_in"), 16)
            rows_in(0)
            sp.wait_ge(sem("xz_w_lo"), XBC_T + Z_T)
            sp.dma_start(raww[:], a["w_out"][0]).then_inc(sem("wo_d_in"), 16)
            sp.wait_ge(sem("xz_mm"), 2 * (XBC_T + Z_T))
            sp.wait_ge(sem("att_out"), 16 * KVH)
            for s in range(2):
                sp.dma_start(mixs[:, s, :], mixed[s]).then_inc(sem(f"wo_m_in{s}"), 16)
            with sp.Fori(1, CH) as c:
                sp.wait_ge(sem("sd_diff"), c)
                rows_in(c)
            sp.wait_ge(sem("wo_d_lo"), 1)
            sp.dma_start(raww[:], a["w_out"][1]).then_inc(sem("wo_d_in"), 16)
            out_sp(sp)
            sp.wait_ge(sem("wo_act_lo"), MIX_T)
            sp.dma_start(rawg[:], a["gu2"][0]).then_inc(sem("f2_gu_in"), 16)
            sp.wait_ge(sem("wo_d_lo"), MIX_T)
            sp.dma_start(raww[:], a["d2"][0]).then_inc(sem("f2_d_in"), 16)
            sp.wait_ge(sem("turn_out"), past("t2", "out"))
            turn_sp(sp, "t2", x1, x2)
            with sp.Fori(1, FT) as j:
                wait(sp, "f2_gu_lo", j)
                sp.dma_start(rawg[:], tile_of(a["gu2"], j)).then_inc(sem("f2_gu_in"), 16)
                wait(sp, "f2_d_lo", j)
                sp.dma_start(raww[:], tile_of(a["d2"], j)).then_inc(sem("f2_d_in"), 16)
            sp.wait_ge(sem("turn_out"), past("t3", "out"))
            turn_sp(sp, "t3", x2, a["out"])
            sp.wait_ge(sem("turn_out"), past("t3", "out") + 16 * KT)

        @block.tensor
        def _(pe):
            pe.wait_ge(sem("consts_in"), 16 * 5)
            ffn_pe(pe, "f1", "t0")
            rstd_pe_cols(pe, "turn_a_sum", past("t1", "a_sum") + 2 * KT)
            rstd_pe_rows(pe, "t1_post")
            first_group_pe(pe)
            att_pe(pe, 0, True, True)
            with pe.Fori(1, KVH - 1) as g:
                att_pe(pe, g, False, True)
            att_pe(pe, KVH - 1, False, False)
            xz_pe(pe)
            ssd_pe(pe)
            out_pe(pe)
            rstd_pe_cols(pe, "turn_a_sum", past("t2", "a_sum") + 2 * KT)
            rstd_pe_rows(pe, "t2_post")
            ffn_pe(pe, "f2", "t2")
            rstd_pe_cols(pe, "turn_a_sum", past("t3", "a_sum") + 2 * KT)
            rstd_pe_rows(pe, "t3_post")

        @block.scalar
        def _(act):
            act.wait_ge(sem("consts_in"), 16 * 5)
            f = ffn_act(act, "f1", "t0", rope_tables_act)
            turn_act(act, "t0", None, NORM_COLS["ffn1_pre"], next(f))
            rstd_act(act, "t0_pre", D)
            next(f)
            post_act(act, "t1", "f1_acc", FFN_ACC)
            rstd_act(act, "t1_post", D)
            turn_act(act, "t1", True, NORM_COLS["mix_pre"], lambda k: att_w_hi(act, 0, k) if k < 2 else None)
            rstd_act(act, "t1_pre", D)
            first_group_act(act)
            att_act(act, 0, True, True)
            with act.Fori(1, KVH - 1) as g:
                att_act(act, g, False, True)
            att_act(act, KVH - 1, False, False)
            xz_act(act)
            ssd_act(act)
            out_act(act)
            post_act(act, "t2", "wo_acc", WO_ACC)
            rstd_act(act, "t2_post", D)
            f = ffn_act(act, "f2", "t2", lambda act: None)
            turn_act(act, "t2", True, NORM_COLS["ffn2_pre"], next(f))
            rstd_act(act, "t2_pre", D)
            next(f)
            post_act(act, "t3", "f2_acc", FFN_ACC)
            rstd_act(act, "t3_post", D)

        @block.vector
        def _(v):
            v.wait_ge(sem("consts_in"), 16 * 5)
            v.tensor_scalar(hcols[:], cols[:, 0:48], 0.5, None, ALU.mult).then_inc(sem("half_cols"), 1)
            v.wait_ge(sem("half_cols"), 1)
            f = ffn_dve(v, "f1", "t0", "t1", rope_tables_dve)
            turn_dve(v, "t0", None, NORM_COLS["ffn1_pre"], next(f))
            rstd_dve(v, "t0_pre")
            next(f)
            rstd_dve(v, "t1_post")
            turn_dve(v, "t1", hcols[:, 8:16], NORM_COLS["mix_pre"], lambda k: w_lo(v, "at", k, k) if k < 2 else None)
            first_group_dve(v)
            att_dve(v, 0, True, True)
            with v.Fori(1, KVH - 1) as g:
                att_dve(v, g, False, True)
            att_dve(v, KVH - 1, False, False)
            xz_dve(v)
            ssd_dve(v)
            out_dve(v)
            rstd_dve(v, "t2_post")
            f = ffn_dve(v, "f2", "t2", "t3", lambda v: None)
            turn_dve(v, "t2", cols[:, 24:32], NORM_COLS["ffn2_pre"], next(f))
            rstd_dve(v, "t2_pre")
            next(f)
            rstd_dve(v, "t3_post")
            turn_dve(v, "t3", hcols[:, 40:48], None)

        @block.gpsimd
        def _(g):
            turn_pool(g, "t0")
            turn_pool(g, "t1")
            for n in range(12):
                piece_pool(g, 0, n)
            att_pool(g, 0, True)
            with g.Fori(1, KVH - 1) as i:
                att_pool(g, i, True)
            att_pool(g, KVH - 1, False)
            ssd_pool(g)
            gate_pool(g)
            turn_pool(g, "t2")


def shape_constants():
    r = np.arange(P)
    ident = np.eye(P)
    tri = (r[:, None] <= r[None, :]) * 1.0
    rot = np.zeros((P, P))
    for b in (0, HD):
        for i in range(HD // 2):
            rot[b + HD // 2 + i, b + i] = -1.0
            rot[b + i, b + HD // 2 + i] = 1.0
    squares = np.stack([ident, tri, np.ones((P, P)), rot]).astype(np.float32)
    dist = r[:, None] + (S - P) - np.arange(S)[None, :]
    times = sum((((dist >= 0) & (dist % dil == 0) & (dist <= (win // dil) * dil)) * 1) for win, dil in ((128, 1), (512, 4), (2048, 16)))
    mask = np.where(times > 0, np.log(np.maximum(times, 1)), -1e30).astype(np.float32)
    inv = (10000.0 ** (-np.arange(0, HD, 2, dtype=np.float64) / HD)).astype(np.float32)
    return squares, mask, np.tile(inv, 4)


def kernel(**inputs):
    import concourse.bacc as bacc
    from concourse.bass_utils import run_bass_kernel_spmd

    x = {n: np.asarray(v) for n, v in inputs.items()}
    squares, mask, inv = shape_constants()

    def col_tiles(w, lo, n):
        w = w[:, lo:lo + n * P].reshape(KT, P, n, P)
        return np.ascontiguousarray(w.transpose(2, 1, 0, 3))

    def row_tiles(w):
        return np.ascontiguousarray(w.reshape(-1, P, KT, P))

    def cols_of(v):
        return v.reshape(-1, P).T

    w_in = x["w_in"][0]
    k0, v0, c0 = HEADS * HD, (HEADS + KVH) * HD, (HEADS + 2 * KVH) * HD
    z0 = c0 + XBC_T * P
    q_tiles = col_tiles(w_in, 0, 8)
    att = []
    for g in range(KVH):
        kg = w_in[:, k0 + g * HD:k0 + (g + 1) * HD]
        att += [q_tiles[2 * g], q_tiles[2 * g + 1], col_tiles(np.concatenate([kg, kg], 1), 0, 1)[0]]
    w_v = np.concatenate([w_in[:, v0:c0], w_in[:, z0 + Z_T * P:]], 1).reshape(KT, P, 272).transpose(1, 0, 2)
    arrays = {
        "x": np.ascontiguousarray(x["x"][0].T).reshape(KT, P, S),
        "pos": np.ascontiguousarray(np.broadcast_to(x["positions"], (P, S))),
        "squares": squares,
        "mask": mask,
        "cols": np.ascontiguousarray(np.concatenate(
            [cols_of(x[n][0]) for n in ("ffn1_pre_norm", "ffn1_post_norm", "mix_pre_norm", "mix_post_norm",
                                        "ffn2_pre_norm", "ffn2_post_norm")]
            + [cols_of(x["conv_w"][0, j]) for j in range(4)] + [cols_of(x["conv_b"][0])]
            + [cols_of(x["ssm_norm"][0]), cols_of(np.repeat(x["d_skip"][0], HD))]
            + [inv[:, None], np.full((P, 1), EPS, np.float32)], 1)),
        "head_rows": np.ascontiguousarray(np.broadcast_to(np.stack([x["dt_bias"][0], x["a_log"][0]]), (P, 2, HEADS))),
        "w_att": np.stack(att),
        "w_v": np.ascontiguousarray(w_v),
        "w_xz": col_tiles(w_in, c0, XBC_T + Z_T),
        "w_out": row_tiles(x["w_out"][0]),
    }
    for n in (1, 2):
        gate, up = (col_tiles(x[f"ffn{n}_w_{m}"][0], 0, FT) for m in ("gate", "up"))
        arrays[f"gu{n}"] = np.ascontiguousarray(np.stack([gate, up], 2))
        arrays[f"d{n}"] = row_tiles(x[f"ffn{n}_w_down"][0])
    nc = bacc.Bacc("TRN2", target_bir_lowering=False, num_devices=1)
    a = {n: nc.dram_tensor("in_" + n, v.shape, mybir.dt.from_np(v.dtype), kind="ExternalInput").ap()
         for n, v in arrays.items()}
    a["out"] = nc.dram_tensor("out_x", (KT, P, S), F32, kind="ExternalOutput").ap()
    build(nc, a)
    r = run_bass_kernel_spmd(nc, [{"in_" + n: v for n, v in arrays.items()}], core_ids=[0])
    y = r.results[0]["out_x"]
    return np.ascontiguousarray(y.reshape(D, S).T).reshape(x["x"].shape)
```

```python
from contextlib import ExitStack

import numpy as np

import concourse.bass as bass
from concourse import mybir

F32 = mybir.dt.float32
FR = mybir.dt.float32r
I32 = mybir.dt.int32
ALU = mybir.AluOpType
ACT = mybir.ActivationFunctionType

P = 128
S = 1024
D = 1024
KT = D // P
HALF = 512
NH2 = S // HALF
FF = 2816
FT = FF // P
FG = FT // 2
HD = 64
HEADS = 16
KVH = 4
CH = S // P
XBC_T = 12
Z_T = 8
BC0 = 8
MIX_T = 16
ATT_T = 8
STAGED = 4
GROUPS = 2
EPS = 1e-6
KB = 1024
NORM_COLS = {"ffn1_pre": 0, "ffn1_post": 8, "mix_pre": 16, "mix_post": 24, "ffn2_pre": 32, "ffn2_post": 40}
CONVW, CONVB, SSMN, DSK, INVF, EPSC = 48, 96, 108, 116, 124, 125
NCOLS = 126
TWO_PI = 2 * np.pi
C1 = 6.28125
C2 = float(np.float32(np.floor((TWO_PI - C1) * 2**22) / 2**22))
C3 = float(np.float32(TWO_PI - C1 - C2))
ROUND = 12582912.0
PI_IN = 3.1415925


FFN_COUNTS = {"gu_in": 16 * FT, "d_in": 16 * FT, "gu_hi": FT, "gu_lo": FT, "d_hi": FT, "d_lo": FT,
              "gu_mm": 2 * FT, "gate": 2 * FT, "up": 2 * FT, "silu": 2 * FT, "prod": 2 * FT,
              "act_hi": 2 * FT, "act_lo": 2 * FT, "down_mm": 16 * FG, "acc": 16 * FG}


def build(nc, a):
    with ExitStack() as ctx:
        sems = {}

        def sem(name):
            if name[:3] in ("f1_", "f2_"):
                name = "ff_" + name[3:]
            if name not in sems:
                sems[name] = ctx.enter_context(nc.semaphore(name))
            return sems[name]

        map_base = -(-nc.sbuf_base // 64) * 64

        def at(name, kb, shape, dt=F32):
            return nc.alloc_sbuf_tensor_at(name, shape, dt, offset=map_base + int(kb * KB))

        def wait(eng, name, value):
            if not isinstance(value, int) or value > 0:
                eng.wait_ge(sem(name), value + (FFN_COUNTS[name[3:]] if name[:3] == "f2_" else 0))

        nh = at("norm_hi", 0, [P, KT, S], FR)
        nl = at("norm_lo", 32, [P, KT, S], FR)
        acc = at("acc", 64, [P, KT, S])
        acth = at("act_hi", 96, [P, 2, S], FR)
        actl = at("act_lo", 104, [P, 2, S], FR)
        rawg = at("raw_gate_up", 112, [P, 2, KT, P])
        guh = at("gate_up_hi", 120, [P, 2, 2, KT, P], FR)
        gul = at("gate_up_lo", 136, [P, 2, 2, KT, P], FR)
        raww = at("raw_tile", 152, [P, KT, P])
        wh = at("tile_hi", 156, [P, 2, KT, P], FR)
        wl = at("tile_lo", 164, [P, 2, KT, P], FR)
        xs = at("x_stream", 172, [P, 2, S])
        sq = at("squares", 180, [P, 2, S])
        diag = at("rstd_diagonal", 180, [P, CH, P])
        sqa = at("result_squares", 172, [P, 4, HALF])
        tg = at("gate_scaled", 180, [P, HALF])
        ts = at("gate_silu", 182, [P, HALF])
        tu = at("up_scaled", 184, [P, HALF])
        sqs = at("square_sums", 188, [P, S])
        rb = at("rstd_rows", 192, [P, S])
        cos = at("cos", 196, [P, S])
        sin = at("sin", 200, [P, S])
        ident = at("ident", 204, [P, P])
        tri = at("tri", 204.5, [P, P])
        ones = at("ones", 205, [P, P])
        rot = at("rot", 205.5, [P, P])
        cols = at("cols", 206, [P, NCOLS])
        rc0 = at("rms_col", 206.5, [P, CH])
        rc = at("rstd_col", 206.53125, [P, CH])
        hcols = at("half_post_cols", 206.5625, [P, 48])
        ang = at("angle", 172, [P, S])
        turns = at("turns", 176, [P, S])
        qh = at("q_hi", 64, [P, 2, S], FR)
        ql = at("q_lo", 72, [P, 2, S], FR)
        kh = at("k_hi", 80, [P, S], FR)
        kl = at("k_lo", 84, [P, S], FR)
        vg = at("v_hi_lo", 88, [P, CH, 2, HD], FR)
        pe0 = at("probs_even", 92, [P, 4, 7 * P])
        pe1 = at("probs_odd", 106, [P, 4, 8 * P])
        pth = at("probs_t_hi", 122, [P, 2, 4, P], FR)
        ptl = at("probs_t_lo", 126, [P, 2, 4, P], FR)
        attg = at("att_group", 130, [P, 2, S])
        mask = at("mask", 138, [P, S])
        vall = at("v_all", 142, [P, CH, 256])
        dtr = at("dt_raw", 151, [P, CH, HEADS])
        nmax = at("neg_max", 151.5, [P, 8])
        den = at("denom", 151.53125, [P, 8])
        rden = at("denom_recip", 151.5625, [P, 8])
        qr = at("q_raw", 172, [P, S])
        qn = at("q_k_next", 176, [P, 3, S])
        ovt = at("out_lo_part", 189, [64, HALF])
        vraw = at("v_weights_raw", 92, [P, KT, 272])
        vwh = at("v_weights_hi", 101, [P, KT, 272], FR)
        vwl = at("v_weights_lo", 110, [P, KT, 272], FR)
        xbc = at("xbc", 64, [P, XBC_T, S])
        cv = at("conv_in", 112, [P, 2, S + 4])
        ct = at("conv_out", 121, [P, 3, S])
        zt = at("z_scaled", 133, [P, 2, S])
        stg = at("staged_conv_in", 172, [P, STAGED, S + 4])
        zs = at("z_silu", 172, [P, 2, S])
        xc = at("xbc_chunk", 0, [P, XBC_T, P])
        mixs = at("mixed_stream", 6, [P, 2, S])
        dec = at("decay", 14, [P, HEADS, P])
        mt = at("mix_t", 22, [P, HEADS, P])
        xd = at("x_dt", 30, [P, HEADS, HD])
        xw = at("x_to_end", 34, [P, HEADS, HD])
        bt = at("b_tokens", 38, [P, GROUPS, P])
        cbm = at("cb_causal", 39, [P, GROUPS, P])
        st = at("state", 40, [P, HEADS, HD])
        yo = at("y_off", 44, [P, HEADS, HD])
        ya = at("y_tokens", 48, [P, HEADS, HD])
        hp = at("state_decayed", 52, [P, HEADS, HD])
        xt = at("x_tokens", 56, [P, HEADS, HD])
        yt = at("y_features", 112, [P, 8, S])
        small = {n: at(n, 144 + 0.5 * i, [P, CH, HEADS]) for i, n in enumerate(
            ["dt_x", "dt_abs", "dt_e", "dt_u", "dt_ln", "dt_c", "dt", "adt", "acs", "eac", "tmp", "wend", "chd", "cst"])}
        arow = at("a_row", 151.625, [P, 2, HEADS])
        rows = at("cum_rows", 180, [P, HEADS, P])
        zr = at("z_in", 172, [P, 2, S])
        gsq = at("gate_squares", 48, [P, 2, S])
        out_slots = [(wh, wl, acth, actl),
                     (at("tile_hi_odd", 14, [P, 2, KT, P], FR), at("tile_lo_odd", 22, [P, 2, KT, P], FR),
                      at("act_hi_odd", 30, [P, 2, S], FR), at("act_lo_odd", 38, [P, 2, S], FR))]

        psum = ctx.enter_context(nc.psum_tensor("psum", [P, 8, 512], F32))

        def banks(b, n=1):
            return psum[:, b:b + n, :].rearrange("p b n -> p (b n)")

        x1 = nc.dram_tensor("x1_scratch", (KT, P, S), F32).ap()
        x2 = nc.dram_tensor("x2_scratch", (KT, P, S), F32).ap()
        zscr = nc.dram_tensor("z_scratch", (Z_T, P, S), F32).ap()
        mixed = nc.dram_tensor("attention_scratch", (ATT_T, P, S), F32).ap()
        cum = nc.dram_tensor("cum_scratch", (P, P), F32).ap()

        def past(t, name):
            per = {"in": 16 * KT // 2, "out": 16 * KT, "a_sq": 2 * KT, "a_sum": 2 * KT, "sum": KT - 1}.get(name, KT)
            return per * (int(t[1]) if name in ("hi", "lo", "sq", "sum") else int(t[1]) - 1)

        RSTD = {t: n + 1 for n, t in enumerate(
            ("t0_pre", "t1_post", "t1_pre", "gt0", "gt1", "t2_post", "t2_pre", "t3_post"))}

        def tile_of(ap, n):
            return ap[bass.ds(n, 1)].rearrange("a p ... -> (a p) ...") if not isinstance(n, int) else ap[n]

        block = ctx.enter_context(nc.Block())

        def rstd_pe_cols(pe, ready, value, bank=6):
            pe.wait_ge(sem(ready), value)
            for c in range(CH):
                mm = pe.matmul(psum[:, bank, c:c + 1], sqs[:, c * P:(c + 1) * P], ones[:, 0:1], start=True, stop=True)
            mm.then_inc(sem("rstd_sum_cols"), 1)

        def rstd_act_rms(act, t, n, bank=6):
            act.wait_ge(sem("rstd_sum_cols"), RSTD[t])
            act.activation(rc0[:], psum[:, bank, 0:CH], ACT.Sqrt, bias=cols[:, EPSC:EPSC + 1], scale=1.0 / n)\
               .then_inc(sem("rstd_rms"), 1)

        def rstd_act_rows(act, t, bank=4):
            act.wait_ge(sem("rstd_row_mm"), RSTD[t])
            act.copy(rb[:], banks(bank, 2)).then_inc(sem("rstd_rb"), 1)

        def rstd_act(act, t, n):
            rstd_act_rms(act, t, n)
            rstd_act_rows(act, t)

        def rstd_dve(v, t):
            v.wait_ge(sem("rstd_rms"), RSTD[t])
            v.reciprocal(rc[:], rc0[:]).then_inc(sem("rstd_rc"), 1)
            v.wait_ge(sem("rstd_rc"), RSTD[t])
            v.tensor_tensor(diag[:], ident[:].unsqueeze(1).to_broadcast([P, CH, P]),
                            rc[:].unsqueeze(2).to_broadcast([P, CH, P]), ALU.mult).then_inc(sem("rstd_diag"), 1)

        def rstd_pe_rows(pe, t, bank=4):
            pe.wait_ge(sem("rstd_diag"), RSTD[t])
            for h in range(NH2):
                mm = pe.matmul(banks(bank + h), ones[:], diag[:, 4 * h:4 * h + 4, :].rearrange("p a b -> p (a b)"),
                               start=True, stop=True)
            mm.then_inc(sem("rstd_row_mm"), 1)

        def post_act(act, t, done, base):
            for h in range(NH2):
                for d in range(KT):
                    n = past(t, "a_sq") + h * KT + d
                    wait(act, done, base + h * KT + d + 1)
                    if h or d >= 4:
                        act.wait_ge(sem("turn_a_sum"), n - 3)
                    act.activation(sqa[:, d % 4, :], acc[:, d, h * HALF:(h + 1) * HALF], ACT.Square)\
                       .then_inc(sem("turn_a_sq"), 1)

        def turn_sp(sp, t, src, dst, after=lambda k: None):
            sp.wait_ge(sem("turn_a_sum"), past(t, "a_sum") + 2 * KT)
            for k in range(KT):
                if k >= 2:
                    sp.wait_ge(sem("turn_x"), past(t, "x") + k - 1)
                    sp.dma_start(dst[k - 2], acc[:, k - 2, :]).then_inc(sem("turn_out"), 16)
                sp.dma_start(xs[:, k % 2, :], src[k]).then_inc(sem(f"turn_in{k % 2}"), 16)
                after(k)
            for k in range(KT - 2, KT):
                sp.wait_ge(sem("turn_x"), past(t, "x") + k + 1)
                sp.dma_start(dst[k], acc[:, k, :]).then_inc(sem("turn_out"), 16)

        scaled = [0]

        def turn_dve(v, t, post, pre, after=lambda k: None):
            def lo(k):
                v.wait_ge(sem("turn_hi"), past(t, "hi") + k + 1)
                v.scalar_tensor_tensor(out=nl[:, k, :], in0=acc[:, k, :], scalar=cols[:, pre + k:pre + k + 1],
                                       in1=nh[:, k, :].bitcast(F32), op0=ALU.mult, op1=ALU.subtract)\
                 .then_inc(sem("turn_lo"), 1)

            for k in range(KT):
                if post is not None:
                    if k in POOL_TILES[t]:
                        v.wait_ge(sem("turn_scaled_pool"), POOL_BEFORE[t] + POOL_TILES[t].index(k) + 1)
                    else:
                        scaled[0] += 1
                        v.wait_ge(sem("rstd_rb"), RSTD[t + "_post"])
                        v.tensor_tensor(acc[:, k, :], acc[:, k, :], rb[:], ALU.mult).then_inc(sem("turn_scaled"), 1)
                        v.wait_ge(sem("turn_scaled"), scaled[0])
                    v.wait_ge(sem(f"turn_in{k % 2}"), past(t, "in") + 16 * (k // 2 + 1))
                    v.scalar_tensor_tensor(out=acc[:, k, :], in0=acc[:, k, :], scalar=post[:, k:k + 1],
                                           in1=xs[:, k % 2, :], op0=ALU.mult, op1=ALU.add).then_inc(sem("turn_x"), 1)
                if pre is not None and k >= 1:
                    lo(k - 1)
                    after(k - 1)
            if pre is not None:
                lo(KT - 1)
                after(KT - 1)

        def turn_act(act, t, post, pre, after=lambda k: None):
            for k in range(KT):
                if post is not None:
                    act.wait_ge(sem("turn_x"), past(t, "x") + k + 1)
                else:
                    act.wait_ge(sem(f"x_in{k}"), 16)
                act.activation(nh[:, k, :], acc[:, k, :], ACT.Copy, scale=cols[:, pre + k:pre + k + 1])\
                   .then_inc(sem("turn_hi"), 1)
                if k >= 3:
                    act.wait_ge(sem("turn_sum"), past(t, "sum") + k - 2)
                act.activation(sq[:, k % 2, :] if k else sqs[:], acc[:, k, :], ACT.Square).then_inc(sem("turn_sq"), 1)
                after(k)

        POOL_TILES = {"t1": (1, 3), "t2": (1, 3), "t3": (1, 3, 5)}
        POOL_BEFORE = {"t1": 0, "t2": 2, "t3": 4}

        def turn_pool_scale(g, t):
            g.wait_ge(sem("rstd_rb"), RSTD[t + "_post"])
            for k in POOL_TILES[t]:
                g.tensor_tensor(acc[:, k, :], acc[:, k, :], rb[:], ALU.mult).then_inc(sem("turn_scaled_pool"), 1)

        def turn_pool(g, t):
            for k in range(1, KT):
                g.wait_ge(sem("turn_sq"), past(t, "sq") + k + 1)
                wait(g, "turn_sum", past(t, "sum") + k - 1)
                g.tensor_tensor(sqs[:], sqs[:], sq[:, k % 2, :], ALU.add).then_inc(sem("turn_sum"), 1)

        def ffn_sp(sp, p, wgu, wd, start):
            start(sp)
            sp.dma_start(rawg[:], wgu[0]).then_inc(sem(p + "_gu_in"), 16)
            sp.dma_start(raww[:], wd[0]).then_inc(sem(p + "_d_in"), 16)
            with sp.Fori(1, FT) as j:
                wait(sp, p + "_gu_lo", j)
                sp.dma_start(rawg[:], tile_of(wgu, j)).then_inc(sem(p + "_gu_in"), 16)
                wait(sp, p + "_d_lo", j)
                sp.dma_start(raww[:], tile_of(wd, j)).then_inc(sem(p + "_d_in"), 16)

        def ffn_pe(pe, p, t):
            def pair(bank, slot, m, k, h):
                o, x = banks(bank), slice(h * HALF, (h + 1) * HALF)
                pe.matmul(o, guh[:, slot, m, k, :], nh[:, k, x], start=(k == 0), stop=False)
                pe.matmul(o, guh[:, slot, m, k, :], nl[:, k, x], start=False, stop=False)
                return pe.matmul(o, gul[:, slot, m, k, :], nh[:, k, x], start=False, stop=(k == KT - 1))

            def body(i, first):
                for s in range(2):
                    wait(pe, p + "_gu_lo", 2 * i + s + 1)
                    if first and s == 0:
                        for k in range(KT):
                            pe.wait_ge(sem("turn_lo"), past(t, "lo") + k + 1)
                            for h in range(NH2):
                                for m in range(2):
                                    mm = pair(2 * h + m, s, m, k, h)
                        mm.then_inc(sem(p + "_gu_mm"), 2)
                        if t == "t0":
                            pe.wait_ge(sem("consts_in"), 16 * 4)
                        rstd_pe_cols(pe, "turn_sum", past(t, "sum") + KT - 1)
                        rstd_pe_rows(pe, t + "_pre")
                        continue
                    for h in range(NH2):
                        u = 4 * i + 2 * s + h
                        wait(pe, p + "_up", u - 1)
                        for m in range(2):
                            for k in range(KT):
                                mm = pair(2 * h + m, s, m, k, h)
                        mm.then_inc(sem(p + "_gu_mm"), 1)
                wait(pe, p + "_d_lo", 2 * i + 2)
                for h in range(NH2):
                    wait(pe, p + "_act_lo", 4 * i + 3 + h)
                    if first and h == 0:
                        pe.wait_ge(sem("rstd_rb"), RSTD[t + "_pre"])
                    down_pe(pe, p, i, h)
            body(0, True)
            with pe.Fori(1, FG) as i:
                body(i, False)

        def down_pe(pe, p, i, h, slots=(wh, wl, acth, actl)):
            w_h, w_l, a_h, a_l = slots
            for d in range(KT):
                u = 16 * i + 8 * h + d
                wait(pe, p + "_acc", u - 3)
                o, x = banks(4 + d % 4), slice(h * HALF, (h + 1) * HALF)
                for s in range(2):
                    pe.matmul(o, w_h[:, s, d, :], a_h[:, s, x], start=(s == 0), stop=False)
                    pe.matmul(o, w_h[:, s, d, :], a_l[:, s, x], start=False, stop=False)
                    mm = pe.matmul(o, w_l[:, s, d, :], a_h[:, s, x], start=False, stop=(s == 1))
                mm.then_inc(sem(p + "_down_mm"), 1)

        def down_dve(v, p, i, first, last=False, t=None, between=lambda h, d: None):
            def square_sum(h, d):
                n = past(t, "a_sum") + h * KT + d
                x = slice(h * HALF, (h + 1) * HALF)
                v.wait_ge(sem("turn_a_sq"), n + 1)
                if d == 0:
                    v.tensor_copy(sqs[:, x], sqa[:, d % 4, :]).then_inc(sem("turn_a_sum"), 1)
                else:
                    v.wait_ge(sem("turn_a_sum"), n)
                    v.tensor_tensor(sqs[:, x], sqs[:, x], sqa[:, d % 4, :], ALU.add).then_inc(sem("turn_a_sum"), 1)

            for h in range(NH2):
                for d in range(KT):
                    between(h, d)
                    u = 16 * i + 8 * h + d
                    a_, b_ = acc[:, d, h * HALF:(h + 1) * HALF], banks(4 + d % 4)
                    wait(v, p + "_down_mm", u + 1)
                    if first:
                        v.tensor_copy(a_, b_).then_inc(sem(p + "_acc"), 1)
                    else:
                        wait(v, p + "_acc", u - 15)
                        v.tensor_tensor(a_, b_, a_, ALU.add).then_inc(sem(p + "_acc"), 1)
                    if last and d:
                        square_sum(h, d - 1)
                if last:
                    square_sum(h, KT - 1)

        START = -1

        def ffn_act(act, p, t, between):
            def gu_hi(j, s, used):
                wait(act, p + "_gu_in", 16 * j + 16)
                wait(act, p + "_gu_mm", used)
                act.copy(guh[:, s], rawg[:]).then_inc(sem(p + "_gu_hi"), 1)

            def d_hi(j, s, used):
                wait(act, p + "_d_in", 16 * j + 16)
                wait(act, p + "_down_mm", used)
                act.copy(wh[:, s], raww[:]).then_inc(sem(p + "_d_hi"), 1)

            def body(i, more):
                for s in range(2):
                    for h in range(NH2):
                        u = 4 * i + 2 * s + h
                        wait(act, p + "_gate", u + 1)
                        wait(act, p + "_prod", u)
                        act.activation(ts[:], tg[:], ACT.Silu).then_inc(sem(p + "_silu"), 1)
                        wait(act, p + "_prod", u + 1)
                        wait(act, p + "_down_mm", 16 * i - 8 + 8 * h)
                        act.copy(acth[:, s, h * HALF:(h + 1) * HALF], tu[:]).then_inc(sem(p + "_act_hi"), 1)
                    if more:
                        gu_hi(2 * i + 2 + s, s, 4 * i + 2 * s + 2)
                if more:
                    for s in range(2):
                        d_hi(2 * i + 2 + s, s, 16 * i + 16)

            yield lambda k: {START: lambda: gu_hi(0, 0, 0), 5: lambda: d_hi(0, 0, 0), 6: lambda: gu_hi(1, 1, 0),
                             7: lambda: d_hi(1, 1, 0)}.get(k, lambda: None)()
            body(0, True)
            between(act)
            with act.Fori(1, FG - 1) as i:
                body(i, True)
            body(FG - 1, False)
            yield

        def ffn_dve(v, p, t, t_next, between):
            def gu_lo(j, s):
                wait(v, p + "_gu_hi", j + 1)
                v.tensor_tensor(gul[:, s], rawg[:], guh[:, s].bitcast(F32), ALU.subtract).then_inc(sem(p + "_gu_lo"), 1)

            def d_lo(j, s):
                wait(v, p + "_d_hi", j + 1)
                v.tensor_tensor(wl[:, s], raww[:], wh[:, s].bitcast(F32), ALU.subtract).then_inc(sem(p + "_d_lo"), 1)

            def body(i, first, more):
                for s in range(2):
                    for h in range(NH2):
                        u = 4 * i + 2 * s + h
                        x = slice(h * HALF, (h + 1) * HALF)
                        wait(v, p + "_gu_mm", u + 1)
                        wait(v, p + "_silu", u)
                        v.tensor_tensor(tg[:], banks(2 * h), rb[:, x], ALU.mult).then_inc(sem(p + "_gate"), 1)
                        wait(v, p + "_act_lo", u)
                        v.tensor_tensor(tu[:], banks(2 * h + 1), rb[:, x], ALU.mult).then_inc(sem(p + "_up"), 1)
                        wait(v, p + "_up", u + 1)
                        wait(v, p + "_silu", u + 1)
                        v.tensor_tensor(tu[:], ts[:], tu[:], ALU.mult).then_inc(sem(p + "_prod"), 1)
                        wait(v, p + "_act_hi", u + 1)
                        v.tensor_tensor(actl[:, s, x], tu[:], acth[:, s, x].bitcast(F32), ALU.subtract)\
                         .then_inc(sem(p + "_act_lo"), 1)
                    if more and s == 0:
                        gu_lo(2 * i + 2, 0)
                down_dve(v, p, i, first, not more, t_next, 
                         lambda h, d: gu_lo(2 * i + 3, 1) if more and (h, d) == (1, 0) else None)
                if more:
                    for s in range(2):
                        d_lo(2 * i + 2 + s, s)

            yield lambda k: {START: lambda: gu_lo(0, 0), 5: lambda: d_lo(0, 0), 6: lambda: gu_lo(1, 1),
                             7: lambda: d_lo(1, 1)}.get(k, lambda: None)()
            v.wait_ge(sem("rstd_rb"), RSTD[t + "_pre"])
            body(0, True, True)
            between(v)
            with v.Fori(1, FG - 1) as i:
                body(i, False, True)
            body(FG - 1, False, False)
            yield

        FFN_ACC = 16 * (FG - 1)

        def rope_tables_dve(v):
            n = [0]

            def step(ins):
                n[0] += 1
                ins.then_inc(sem("rope_step"), 1)
                v.wait_ge(sem("rope_step"), n[0])
            v.wait_ge(sem("pos_in"), 16)
            step(v.tensor_copy(turns[:], sin[:].bitcast(I32)))
            step(v.tensor_scalar(ang[:], turns[:], cols[:, INVF:INVF + 1], None, ALU.mult))
            step(v.tensor_scalar(turns[:], ang[:], float(np.float32(1 / TWO_PI)), ROUND, ALU.mult, ALU.add))
            step(v.tensor_scalar(turns[:], turns[:], ROUND, None, ALU.subtract))
            for c in (C1, C2, C3):
                step(v.scalar_tensor_tensor(out=ang[:], in0=turns[:], scalar=-c, in1=ang[:], op0=ALU.mult, op1=ALU.add))
            step(v.tensor_scalar(ang[:], ang[:], PI_IN, -PI_IN, ALU.min, ALU.max))
            v.wait_ge(sem("rope_sin"), 2)
            step(v.tensor_tensor(cos[:], cos[:], cos[:], ALU.mult))
            step(v.tensor_scalar(cos[:], cos[:], -2.0, 1.0, ALU.mult, ALU.add))

        def rope_tables_act(act):
            act.wait_ge(sem("rope_step"), 8)
            act.activation(cos[:], ang[:], ACT.Sin, scale=0.5).then_inc(sem("rope_sin"), 1)
            act.activation(sin[:], ang[:], ACT.Sin).then_inc(sem("rope_sin"), 1)

        def proj_pe(pe, q, n, slot, bank, gate=None, free=None):
            pe.wait_ge(sem(q + "_w_lo"), n)
            for h in range(NH2):
                if free:
                    free(h)
                x = slice(h * HALF, (h + 1) * HALF)
                for k in range(KT):
                    if gate and h == 0:
                        pe.wait_ge(sem("turn_lo"), past(gate, "lo") + k + 1)
                    pe.matmul(banks(bank + h), wh[:, slot, k, :], nh[:, k, x], start=(k == 0), stop=False)
                    pe.matmul(banks(bank + h), wh[:, slot, k, :], nl[:, k, x], start=False, stop=False)
                    mm = pe.matmul(banks(bank + h), wl[:, slot, k, :], nh[:, k, x], start=False, stop=(k == KT - 1))
                mm.then_inc(sem(q + "_mm"), 1)

        def w_hi(act, q, n, slot, used):
            act.wait_ge(sem(q + "_w_in"), 16 * n)
            wait(act, q + "_mm", used)
            act.copy(wh[:, slot], raww[:]).then_inc(sem(q + "_w_hi"), 1)

        def w_lo(v, q, n, slot):
            v.wait_ge(sem(q + "_w_hi"), n + 1 if q == "at" else n)
            v.tensor_tensor(wl[:, slot], raww[:], wh[:, slot].bitcast(F32), ALU.subtract).then_inc(sem(q + "_w_lo"), 1)

        NT = sum(i + 1 for i in range(CH))
        SCORE_WEIGHT, TAIL = 0.5, 0.5
        PARTS = 8

        def cnt(i, j):
            return sum(x + 1 for x in range(i)) + j

        def att_events(more):
            def unit(i):
                items = [((j + 0.5) / (i + 1), ("block", i, j)) for j in range(i + 1)]
                if i + 1 < CH:
                    items += [(hh * 0.10, ("score", i + 1, hh)) for hh in range(4)]
                items = [e for _, e in sorted(items)]
                if i:
                    items.insert(items.index(("block", i, 0)) + 1, ("end", i - 1))
                return items

            base = [("score", 0, hh) for hh in range(4)] + [e for i in range(CH) for e in unit(i)]
            parts = []
            if more:
                for n in range(12):
                    if n % 4 < 2:
                        parts += [("part", n, q) for q in range(PARTS - 1)]
                    parts.append(("piece", n))
                    if n in (0, 3, 10):
                        parts.append(("w", {0: 1, 3: 2, 10: 3}[n]))
            else:
                for n in range(2 * STAGED):
                    parts += [("xpart", n, q) for q in range(PARTS)]
                    if n % 2 == 0:
                        parts.append(("xw", n // 2 + 1))
                    elif n == 2 * STAGED - 1:
                        parts.append(("xw", STAGED + 1))
            weight = {"score": SCORE_WEIGHT, "block": 1.0, "end": 0.0}
            total = sum(weight[e[0]] for e in base) - SCORE_WEIGHT * 4 - TAIL
            done, past_weight = PARTS, 0.0
            ev = parts[:done] + [("v_split",)]
            for k, e in enumerate(base):
                ev.append(e)
                if k >= 3:
                    due = min(len(parts), int(len(parts) * past_weight / total))
                    ev += parts[done:due]
                    done = max(done, due)
                    past_weight += weight[e[0]]
                if more and done == len(parts) and ("split",) not in ev and ("score", CH - 1, 3) in ev:
                    ev.append(("split",))
            return ev

        FIRST_GROUP = ([("piece", 0), ("w", 2), ("piece", 1), ("k", 0), ("piece", 2), ("piece", 3), ("piece", 4),
                        ("piece", 5), ("k", 1), ("piece", 6), ("piece", 7), ("piece", 8), ("piece", 9), ("v_w",),
                        ("piece", 10), ("v", 0), ("piece", 11)] + [("v", 1), ("w", 3)] + [("v", n) for n in range(2, CH)])
        IN_BANK = {0: 0, 1: 1, 4: 2, 5: 3, 8: 0, 9: 1}

        def probs(i, hh):
            return (pe1 if i % 2 else pe0)[:, hh, :]

        def piece_pe(pe, g, n, inc=1, part=None):
            t, rotated, h = n // 4, n % 4 >= 2, n % 2
            x = slice(h * HALF, (h + 1) * HALF)
            tiles = range(KT) if part is None else range(part * KT // PARTS, (part + 1) * KT // PARTS)
            if rotated or tiles[0] == 0:
                wait(pe, "pj_read", 12 * g + n)
            if rotated:
                mm = pe.matmul(banks(7), rot[:], qr[:, x], start=True, stop=True)
            else:
                if tiles[0] == 0:
                    pe.wait_ge(sem("at_w_lo"), 3 * g + t + 1)
                for k in tiles:
                    pe.matmul(banks(7), wh[:, t % 2, k, :], nh[:, k, x], start=(k == 0), stop=False)
                    pe.matmul(banks(7), wh[:, t % 2, k, :], nl[:, k, x], start=False, stop=False)
                    mm = pe.matmul(banks(7), wl[:, t % 2, k, :], nh[:, k, x], start=False, stop=(k == KT - 1))
            if rotated or tiles[-1] == KT - 1:
                mm.then_inc(sem("pj_mm"), inc)

        def staged_pe(pe, n, part):
            t, x = n // 2, slice(n % 2 * HALF, (n % 2 + 1) * HALF)
            if part == 0:
                if n == 0:
                    pe.wait_ge(sem("pj_read"), 12 * KVH)
                wait(pe, "xz_read", n)
                if t == 0:
                    pe.wait_ge(sem("at_w_lo"), 3 * KVH + 1)
                else:
                    pe.wait_ge(sem("xz_w_lo"), t)
            for k in range(part * KT // PARTS, (part + 1) * KT // PARTS):
                pe.matmul(banks(7), wh[:, t % 2, k, :], nh[:, k, x], start=(k == 0), stop=False)
                pe.matmul(banks(7), wh[:, t % 2, k, :], nl[:, k, x], start=False, stop=False)
                mm = pe.matmul(banks(7), wl[:, t % 2, k, :], nh[:, k, x], start=False, stop=(k == KT - 1))
            if part == PARTS - 1:
                mm.then_inc(sem("xz_mm"), 1)

        def first_group_pe(pe):
            pe.wait_ge(sem("at_w_lo"), 2)
            for k in range(KT):
                pe.wait_ge(sem("turn_lo"), past("t1", "lo") + k + 1)
                for t in range(2):
                    for h in range(NH2):
                        x = slice(h * HALF, (h + 1) * HALF)
                        o = banks(2 * t + h)
                        pe.matmul(o, wh[:, t, k, :], nh[:, k, x], start=(k == 0), stop=False)
                        pe.matmul(o, wh[:, t, k, :], nl[:, k, x], start=False, stop=False)
                        mm = pe.matmul(o, wl[:, t, k, :], nh[:, k, x], start=False, stop=(k == KT - 1))
            mm.then_inc(sem("pj_mm"), 2)
            rstd_pe_cols(pe, "turn_sum", past("t1", "sum") + KT - 1)
            rstd_pe_rows(pe, "t1_pre")
            for e in FIRST_GROUP:
                if e[0] == "v":
                    v_pe(pe, e[1])
                elif e[0] == "k":
                    h = e[1]
                    pe.wait_ge(sem("at_w_lo"), 3)
                    pe.wait_ge(sem("pj_read"), h + 1)
                    for k in range(KT):
                        x = slice(h * HALF, (h + 1) * HALF)
                        pe.matmul(banks(h), wh[:, 0, k, :], nh[:, k, x], start=(k == 0), stop=False)
                        pe.matmul(banks(h), wh[:, 0, k, :], nl[:, k, x], start=False, stop=False)
                        mm = pe.matmul(banks(h), wl[:, 0, k, :], nh[:, k, x], start=False, stop=(k == KT - 1))
                    mm.then_inc(sem("k_first_mm"), 1)
                elif e[0] == "piece" and e[1] not in IN_BANK:
                    piece_pe(pe, 0, e[1], 3 if e[1] in (3, 7) else 1)

        def v_pe(pe, c):
            if c == 0:
                pe.wait_ge(sem("v_w_lo"), 1)
                pe.wait_ge(sem("rstd_rb"), RSTD["t1_pre"])
            if c >= 2:
                pe.wait_ge(sem("v_read"), 2 * (c - 1))
            x = slice(c * P, (c + 1) * P)
            o = psum[:, 4 + c % 2, 0:272]
            for k in range(KT):
                pe.matmul(o, nh[:, k, x], vwh[:, k, :], start=(k == 0), stop=False)
                pe.matmul(o, nh[:, k, x], vwl[:, k, :], start=False, stop=False)
                mm = pe.matmul(o, nl[:, k, x], vwh[:, k, :], start=False, stop=(k == KT - 1))
            mm.then_inc(sem("v_mm"), 1)

        def att_pe(pe, g, first, more):
            def score(i, hh):
                n = 32 * g + 4 * i + hh
                if i == 0 and hh == 0:
                    pe.wait_ge(sem("at_qk_lo"), 3 * g + 3)
                    if first:
                        pe.wait_ge(sem("v_read"), 2 * CH)
                wait(pe, "at_max", n - 1)
                b, w = 64 * (hh % 2), (i + 1) * P
                for c in range(0, w, 512):
                    o = psum[:, 2 * (hh % 2) + c // 512, 0:min(512, w - c)]
                    q = slice(i * P, (i + 1) * P)
                    ks = slice(c, min(c + 512, w))
                    pe.matmul(o, qh[b:b + 64, hh // 2, q], kh[b:b + 64, ks], start=True, stop=False)
                    pe.matmul(o, qh[b:b + 64, hh // 2, q], kl[b:b + 64, ks], start=False, stop=False)
                    mm = pe.matmul(o, ql[b:b + 64, hh // 2, q], kh[b:b + 64, ks], start=False, stop=True)
                mm.then_inc(sem("at_score"), 1)

            def turn(i, j):
                n = NT * g + cnt(i, j)
                if j == 0:
                    pe.wait_ge(sem("at_norm"), 32 * g + 4 * i + 4)
                wait(pe, "at_t_lo", n - 1)
                for hh in range(4):
                    mm = pe.transpose(psum[:, 4 + cnt(i, j) % 2, hh * P:(hh + 1) * P],
                                      probs(i, hh)[:, j * P:(j + 1) * P], ident[:])
                mm.then_inc(sem("at_t_mm"), 1)

            def values(i, j):
                n = NT * g + cnt(i, j)
                s = cnt(i, j) % 2
                pe.wait_ge(sem("at_t_lo"), n + 1)
                if j == 0:
                    wait(pe, "at_ov_add", 2 * (8 * g + i))
                    pe.wait_ge(sem("at_v_lo"), g + 1)
                v_hl = vg[:, j].rearrange("p a d -> p (a d)")
                pe.matmul(banks(6), v_hl, pth[:, s].rearrange("p a d -> p (a d)"), start=(j == 0), stop=False)
                pe.matmul(banks(6), v_hl, ptl[:, s].rearrange("p a d -> p (a d)"), start=False, stop=(j == i))\
                  .then_inc(sem("at_pv"), 1)

            last = due = None
            for e in att_events(more):
                if due and e[0] not in ("part", "xpart", "piece", "w", "xw"):
                    values(*due)
                    due = None
                if e[0] == "score":
                    score(e[1], e[2])
                elif e[0] == "xpart":
                    staged_pe(pe, e[1], e[2])
                elif e[0] == "part":
                    piece_pe(pe, g + 1, e[1], 1, e[2])
                elif e[0] == "piece":
                    piece_pe(pe, g + 1, e[1], 1, PARTS - 1)
                elif e[0] == "block":
                    turn(e[1], e[2])
                    due, last = last, e[1:]
                if due and e[0] in ("part", "xpart", "piece"):
                    values(*due)
                    due = None
            if due:
                values(*due)
            values(*last)

        def first_w_hi(act, t):
            act.wait_ge(sem("at_first_in"), 16)
            act.copy(wh[:, t], rawg[:, t]).then_inc(sem("at_w_hi"), 1)

        def first_w_lo(v, t):
            v.wait_ge(sem("at_w_hi"), t + 1)
            v.tensor_tensor(wl[:, t], rawg[:, t], wh[:, t].bitcast(F32), ALU.subtract).then_inc(sem("at_w_lo"), 1)

        def att_w_hi(act, g, t):
            used = {1: 12 * (g - 1) + 6, 2: 12 * g + 2, 3: 12 * g + 10}[t]
            act.wait_ge(sem("at_w_in"), 16 * (3 * g + t - 1))
            wait(act, "pj_mm", used)
            act.copy(wh[:, t % 3 % 2], raww[:]).then_inc(sem("at_w_hi"), 1)

        def first_group_act(act):
            att_w_hi(act, 0, 2)
            act.wait_ge(sem("v_in"), 16)
            act.copy(vwh[:], vraw[:]).then_inc(sem("v_w_hi"), 1)
            att_w_hi(act, 0, 3)
            act.wait_ge(sem("turn_out"), past("t2", "out"))
            qk_split_act(act, 0)

        def qk_split_act(act, g):
            act.wait_ge(sem("at_sum"), 6 * g + 6)
            wait(act, "at_score", 32 * g)
            for t in (2, 0, 1):
                act.copy(qh[:, t, :] if t < 2 else kh[:], qn[:, t, :]).then_inc(sem("at_qk_hi"), 1)

        def qk_split_dve(v, g):
            for m, t in enumerate((2, 0, 1)):
                v.wait_ge(sem("at_qk_hi"), 3 * g + m + 1)
                ho, lo = (qh[:, t, :], ql[:, t, :]) if t < 2 else (kh[:], kl[:])
                v.tensor_tensor(lo, qn[:, t, :], ho.bitcast(F32), ALU.subtract).then_inc(sem("at_qk_lo"), 1)

        def att_act(act, g, first, more):
            def soft(i, hh):
                n, c = 32 * g + 4 * i + hh, 4 * (i % 2) + hh
                act.wait_ge(sem("at_max"), n + 1)
                pr = probs(i, hh)[:, 0:(i + 1) * P]
                act.activation(pr, pr, ACT.Exp, bias=nmax[:, c:c + 1], scale=-1.0, accum_out=den[:, c:c + 1])\
                   .then_inc(sem("at_exp"), 1)

            for e in att_events(more):
                if e[0] == "split":
                    qk_split_act(act, g + 1)
                elif e[0] == "v_split":
                    if first:
                        act.wait_ge(sem("v_read"), 2 * CH)
                    wait(act, "at_pv", NT * g)
                    act.copy(vg[:, :, 0, :], vall[:, :, bass.ds(g * HD, HD)]).then_inc(sem("at_v_hi"), 1)
                elif e[0] == "score":
                    soft(e[1], e[2])
                elif e[0] == "w":
                    att_w_hi(act, g + 1, e[1])
                elif e[0] == "xw":
                    if e[1] < 2:
                        act.wait_ge(sem("pj_mm"), 12 * KVH)
                    w_hi(act, "xz", e[1], e[1] % 2, 2 * e[1] - 2)
                elif e[0] == "block":
                    n, s = NT * g + cnt(*e[1:]), cnt(*e[1:]) % 2
                    act.wait_ge(sem("at_t_mm"), n + 1)
                    wait(act, "at_pv", n - 1)
                    act.copy(pth[:, s].rearrange("p a d -> p (a d)"), banks(4 + s)).then_inc(sem("at_t_hi"), 1)
                elif e[0] == "end":
                    unit_end_act(act, g, e[1])
            unit_end_act(act, g, CH - 1)

        def unit_end_act(act, g, i):
            act.wait_ge(sem("at_pv"), NT * g + cnt(i, i) + 1)
            wait(act, "at_ov_add", 2 * (8 * g + i))
            act.copy(ovt[:], psum[64:128, 6, :]).then_inc(sem("at_ov_lo"), 1)

        def unit_end_dve(v, g, i):
            v.wait_ge(sem("at_ov_lo"), 8 * g + i + 1)
            if i == 0:
                wait(v, "att_out", 16 * g)
            for par in range(2):
                ov = psum[0:64, 6, :].rearrange("p (t a q) -> p t a q", t=2, a=2)[:, :, par, :]
                tv = ovt[:].rearrange("p (t a q) -> p t a q", t=2, a=2)[:, :, par, :]
                v.tensor_tensor(attg[64 * par:64 * par + 64, :, i * P:(i + 1) * P], ov, tv, ALU.add)\
                 .then_inc(sem("at_ov_add"), 1)

        def piece_dve(v, g, n, bank=7):
            t, rotated, h = n // 4, n % 4 >= 2, n % 2
            x = slice(h * HALF, (h + 1) * HALF)
            m = 2 * (3 * g + t)
            v.wait_ge(sem("pj_mm"), 12 * g + n + 1)
            if rotated:
                v.wait_ge(sem("at_cos"), m + h + 1)
                v.tensor_tensor(qr[:, x], banks(bank), sin[:, x], ALU.mult).then_inc(sem("pj_read"), 1)
                v.wait_ge(sem("pj_read"), 12 * g + n + 1)
                v.tensor_tensor(qn[:, t, x], qn[:, t, x], qr[:, x], ALU.add).then_inc(sem("at_sum"), 1)
            else:
                wait(v, "at_sum", m)
                v.scalar_tensor_tensor(out=qr[:, x], in0=banks(bank), scalar=0.125 if t < 2 else 1.0,
                                       in1=rb[:, x], op0=ALU.mult, op1=ALU.mult).then_inc(sem("pj_read"), 1)

        def first_group_dve(v):
            rstd_dve(v, "t1_pre")
            v.wait_ge(sem("rstd_rb"), RSTD["t1_pre"])
            for e in FIRST_GROUP:
                if e[0] == "w":
                    w_lo(v, "at", e[1], e[1] % 3 % 2)
                elif e[0] == "v_w":
                    v.wait_ge(sem("v_w_hi"), 1)
                    v.tensor_tensor(vwl[:], vraw[:], vwh[:].bitcast(F32), ALU.subtract).then_inc(sem("v_w_lo"), 1)
                elif e[0] == "piece":
                    n = e[1]
                    if n in (8, 9):
                        v.wait_ge(sem("k_first_mm"), n - 7)
                    piece_dve(v, 0, n, IN_BANK.get(n, 7))
                elif e[0] == "v":
                    c = e[1]
                    v.wait_ge(sem("v_mm"), c + 1)
                    o = psum[:, 4 + c % 2, :]
                    v.tensor_scalar(vall[:, c, :], o[:, 0:256], rc[:, c:c + 1], None, ALU.mult)\
                     .then_inc(sem("v_read"), 1)
                    v.tensor_scalar(dtr[:, c, :], o[:, 256:272], rc[:, c:c + 1], None, ALU.mult)\
                     .then_inc(sem("v_read"), 1)
            qk_split_dve(v, 0)

        def att_dve(v, g, first, more):
            def soft(i, hh):
                n, c, w = 32 * g + 4 * i + hh, 4 * (i % 2) + hh, (i + 1) * P
                v.wait_ge(sem("at_score"), n + 1)
                wait(v, "at_norm", n - 3)
                v.sem_inc(sem("at_softmax_go"), 1)
                v.wait_ge(sem("mask_in"), 16)
                v.tensor_tensor_reduce(probs(i, hh)[:, 0:w], banks(2 * (hh % 2), 2)[:, 0:w], mask[:, S - w:S],
                                       -1.0, 3.0e38, ALU.add, ALU.min, nmax[:, c:c + 1]).then_inc(sem("at_max"), 1)

            def recip(i, hh):
                n, c = 32 * g + 4 * i + hh, 4 * (i % 2) + hh
                v.wait_ge(sem("at_exp"), n + 1)
                v.reciprocal(rden[:, c:c + 1], den[:, c:c + 1]).then_inc(sem("at_rden"), 1)

            todo = []
            for k, e in enumerate(att_events(more)):
                while todo and (todo[0][0] + 2 <= k or e[0] == "block" and e[2] == 0 and e[1] == todo[0][1]):
                    recip(*todo.pop(0)[1:])
                if e[0] == "score":
                    soft(e[1], e[2])
                    todo.append((k, *e[1:]))
                if e[0] == "split":
                    qk_split_dve(v, g + 1)
                elif e[0] == "v_split":
                    v.wait_ge(sem("at_v_hi"), g + 1)
                    v.tensor_tensor(vg[:, :, 1, :], vall[:, :, bass.ds(g * HD, HD)], vg[:, :, 0, :].bitcast(F32),
                                    ALU.subtract).then_inc(sem("at_v_lo"), 1)
                elif e[0] == "w":
                    w_lo(v, "at", 3 * (g + 1) + e[1], e[1] % 3 % 2)
                elif e[0] == "xw":
                    w_lo(v, "xz", e[1], e[1] % 2)
                elif e[0] == "xpart" and e[2] == PARTS - 1:
                    n = e[1]
                    if n == 0:
                        v.wait_ge(sem("at_qk_lo"), 3 * KVH)
                    v.wait_ge(sem("xz_mm"), n + 1)
                    v.tensor_tensor(stg[:, n // 2, 3 + n % 2 * HALF:3 + (n % 2 + 1) * HALF], banks(7),
                                    rb[:, n % 2 * HALF:(n % 2 + 1) * HALF], ALU.mult).then_inc(sem("xz_read"), 1)
                elif e[0] == "piece":
                    piece_dve(v, g + 1, e[1])
                elif e[0] == "block":
                    n, s = NT * g + cnt(*e[1:]), cnt(*e[1:]) % 2
                    v.wait_ge(sem("at_t_hi"), n + 1)
                    v.tensor_tensor(ptl[:, s].rearrange("p a d -> p (a d)"), banks(4 + s),
                                    pth[:, s].rearrange("p a d -> p (a d)").bitcast(F32), ALU.subtract)\
                     .then_inc(sem("at_t_lo"), 1)
                elif e[0] == "end":
                    unit_end_dve(v, g, e[1])
            unit_end_dve(v, g, CH - 1)

        def piece_pool(gp, g, n):
            t, h = n // 4, n % 2
            if n % 4 < 2:
                x = slice(h * HALF, (h + 1) * HALF)
                gp.wait_ge(sem("pj_read"), 12 * g + n + 1)
                wait(gp, "at_qk_lo", 3 * g)
                gp.tensor_tensor(qn[:, t, x], qr[:, x], cos[:, x], ALU.mult).then_inc(sem("at_cos"), 1)

        def att_pool(gp, g, more):
            def norm(i, hh):
                n, c = 32 * g + 4 * i + hh, 4 * (i % 2) + hh
                gp.wait_ge(sem("at_rden"), n + 1)
                gp.sem_inc(sem("at_norm_go"), 1)
                pr = probs(i, hh)[:, 0:(i + 1) * P]
                gp.tensor_scalar(pr, pr, rden[:, c:c + 1], 1.0, ALU.mult, ALU.mult).then_inc(sem("at_norm"), 1)
            for e in att_events(more):
                if e[0] == "score":
                    norm(e[1], e[2])
                elif e[0] == "piece":
                    piece_pool(gp, g + 1, e[1])

        def xz_pe(pe):
            def tile(n, s):
                def free(h):
                    wait(pe, "xz_read", 2 * n - 2)
                proj_pe(pe, "xz", n, s, 2 * s, None, free)
            pe.wait_ge(sem("at_max"), 32 * KVH)
            with pe.Fori(STAGED // 2, (XBC_T + 4) // 2) as i:
                for s in range(2):
                    tile(2 * i + s, s)
            ssd_prep_pe(pe)
            for n in range(XBC_T + 4, XBC_T + Z_T):
                tile(n, n % 2)

        def conv_threes(eng, tile, staged):
            def three(i):
                for s in range(2):
                    tile(2 * i + s, s, 3 * (i - STAGED // 2) + s)
                staged(i - STAGED // 2, 3 * (i - STAGED // 2) + 2)
            three(STAGED // 2)
            with eng.Fori(STAGED // 2 + 1, XBC_T // 2) as i:
                three(i)

        def xz_act(act):
            def silu(m, q, slot):
                act.wait_ge(sem("xz_out"), q + 1)
                act.activation(xbc[:, bass.ds(m, 1), :].rearrange("p a s -> p (a s)"), ct[:, slot, :], ACT.Silu)\
                   .then_inc(sem("xz_silu"), 1)

            def tile(n, s, q):
                silu(n, q, s)
                w_hi(act, "xz", n + 2, s, 2 * n + 2)

            conv_threes(act, tile, lambda m, q: silu(m, q, 2))
            for n in range(XBC_T, XBC_T + Z_T):
                m, s = n - XBC_T, n % 2
                if m >= 2:
                    act.wait_ge(sem(f"z_out{s}"), 16 * (m // 2))
                act.wait_ge(sem("xz_read"), 2 * n + 2)
                act.activation(zs[:, s, :], zt[:, s, :], ACT.Silu).then_inc(sem("z_silu"), 1)
                if n + 2 < XBC_T + Z_T:
                    w_hi(act, "xz", n + 2, s, 2 * n + 2)
                if m == 0:
                    ssd_prep_act_steps(act)
                elif m == 5:
                    ssd_prep_act_sums(act)

        def xz_dve(v):
            def conv(src, m, q, slot):
                wait(v, "xz_silu", q - 2)
                def col(j):
                    return cols[:, bass.ds(m + CONVW + 12 * j, 1)]
                v.tensor_scalar(ct[:, slot, :], src(3), col(3), col(4), ALU.mult, ALU.add).then_inc(sem("xz_tap"), 1)
                for j in range(3):
                    v.wait_ge(sem("xz_tap"), 3 * q + j + 1)
                    v.scalar_tensor_tensor(out=ct[:, slot, :], in0=src(j), scalar=col(j), in1=ct[:, slot, :],
                                           op0=ALU.mult, op1=ALU.add).then_inc(sem("xz_tap" if j < 2 else "xz_out"), 1)

            def tile(n, s, q):
                wait(v, "xz_out", q - 2)
                for h in range(NH2):
                    v.wait_ge(sem("xz_mm"), 2 * n + h + 1)
                    v.tensor_tensor(cv[:, s, 3 + h * HALF:3 + (h + 1) * HALF], banks(2 * s + h),
                                    rb[:, h * HALF:(h + 1) * HALF], ALU.mult).then_inc(sem("xz_read"), 1)
                v.wait_ge(sem("xz_read"), 2 * n + 2)
                conv(lambda j: cv[:, s, j:j + S], n, q, s)
                w_lo(v, "xz", n + 2, s)

            def staged(m, q):
                conv(lambda j: stg[:, bass.ds(m, 1), j:j + S].rearrange("p a s -> p (a s)"), m, q, 2)

            v.wait_ge(sem("att_out"), 16 * KVH)
            v.memset(cv[:, :, 0:3], 0.0).then_inc(sem("cv_zero"), 1)
            v.memset(stg[:, :, 0:3], 0.0).then_inc(sem("cv_zero"), 1)
            v.wait_ge(sem("cv_zero"), 2)
            conv_threes(v, tile, staged)
            for n in range(XBC_T, XBC_T + Z_T):
                m, s = n - XBC_T, n % 2
                wait(v, "z_silu", m - 1)
                for h in range(NH2):
                    v.wait_ge(sem("xz_mm"), 2 * n + h + 1)
                    v.tensor_tensor(zt[:, s, h * HALF:(h + 1) * HALF], banks(2 * s + h),
                                    rb[:, h * HALF:(h + 1) * HALF], ALU.mult).then_inc(sem("xz_read"), 1)
                if n + 2 < XBC_T + Z_T:
                    w_lo(v, "xz", n + 2, s)
                if m == 0:
                    ssd_prep_dve_steps(v)
                elif m == 5:
                    ssd_prep_dve_sums(v)

        def flat(x):
            return x.rearrange("p a b -> p (a b)")

        def ssd_prep_dve_steps(v):
            sm = small
            v.wait_ge(sem("arow_in"), 16)
            v.tensor_tensor(sm["dt_x"][:], dtr[:], arow[:, 0, :].unsqueeze(1).to_broadcast([P, CH, HEADS]), ALU.add)\
             .then_inc(sem("sp_x"), 1)
            v.wait_ge(sem("sp_x"), 1)
            v.tensor_scalar(sm["tmp"][:], sm["dt_x"][:], -1.0, None, ALU.mult).then_inc(sem("sp_neg"), 1)
            v.wait_ge(sem("sp_neg"), 1)
            v.tensor_tensor(sm["dt_abs"][:], sm["dt_x"][:], sm["tmp"][:], ALU.max).then_inc(sem("sp_abs"), 1)
            v.wait_ge(sem("sp_e"), 1)
            v.tensor_scalar(sm["dt_u"][:], sm["dt_e"][:], 1.0, None, ALU.add).then_inc(sem("sp_u"), 1)
            v.wait_ge(sem("sp_u"), 1)
            v.tensor_scalar(sm["tmp"][:], sm["dt_u"][:], 1.0, None, ALU.subtract).then_inc(sem("sp_t"), 1)
            v.reciprocal(sm["wend"][:], sm["dt_u"][:]).then_inc(sem("sp_t"), 1)
            v.wait_ge(sem("sp_t"), 2)
            v.tensor_tensor(sm["dt_c"][:], sm["dt_e"][:], sm["tmp"][:], ALU.subtract).then_inc(sem("sp_t"), 1)
            v.wait_ge(sem("sp_t"), 3)
            v.tensor_tensor(sm["dt_c"][:], sm["dt_c"][:], sm["wend"][:], ALU.mult).then_inc(sem("sp_t"), 1)
            v.wait_ge(sem("sp_ln"), 1)
            v.wait_ge(sem("sp_t"), 4)
            v.tensor_tensor(sm["dt_c"][:], sm["dt_c"][:], sm["dt_ln"][:], ALU.add).then_inc(sem("sp_t"), 1)
            v.wait_ge(sem("sp_t"), 5)
            v.scalar_tensor_tensor(out=flat(sm["dt"]), in0=flat(sm["dt_x"]), scalar=0.0, in1=flat(sm["dt_c"]),
                                   op0=ALU.max, op1=ALU.add).then_inc(sem("sp_t"), 1)
            v.wait_ge(sem("sp_t"), 6)
            v.wait_ge(sem("sp_a"), 1)
            v.scalar_tensor_tensor(out=sm["adt"][:], in0=sm["dt"][:], scalar=-1.0,
                                   in1=arow[:, 1, :].unsqueeze(1).to_broadcast([P, CH, HEADS]),
                                   op0=ALU.mult, op1=ALU.mult).then_inc(sem("sp_adt"), 1)

        def ssd_prep_dve_sums(v):
            sm = small
            v.wait_ge(sem("sp_cum"), 3)
            v.tensor_copy(flat(sm["cst"]), psum[:, 7, 0:P]).then_inc(sem("sp_cst"), 1)
            v.tensor_copy(flat(sm["acs"]), psum[:, 4, 0:P]).then_inc(sem("sp_acs"), 1)
            v.wait_ge(sem("sp_acs"), 1)
            v.tensor_tensor(flat(sm["tmp"]), psum[:, 5, 0:P], flat(sm["acs"]), ALU.subtract).then_inc(sem("sp_d"), 1)
            v.wait_ge(sem("sp_exp"), 3)
            v.tensor_tensor(sm["wend"][:], sm["wend"][:], sm["dt"][:], ALU.mult).then_inc(sem("sp_wend"), 1)

        def ssd_prep_act_steps(act):
            sm = small
            act.wait_ge(sem("sp_abs"), 1)
            act.activation(sm["dt_e"][:], sm["dt_abs"][:], ACT.Exp, scale=-1.0).then_inc(sem("sp_e"), 1)
            act.wait_ge(sem("sp_u"), 1)
            act.activation(sm["dt_ln"][:], sm["dt_u"][:], ACT.Ln).then_inc(sem("sp_ln"), 1)
            act.activation(arow[:, 1, :], arow[:, 1, :], ACT.Exp).then_inc(sem("sp_a"), 1)

        def ssd_prep_act_sums(act):
            sm = small
            act.wait_ge(sem("sp_acs"), 1)
            act.activation(flat(sm["eac"]), flat(sm["acs"]), ACT.Exp).then_inc(sem("sp_exp"), 1)
            act.wait_ge(sem("sp_d"), 1)
            act.activation(flat(sm["wend"]), flat(sm["tmp"]), ACT.Exp).then_inc(sem("sp_exp"), 1)
            act.activation(flat(sm["chd"]), psum[:, 5, 0:P], ACT.Exp).then_inc(sem("sp_exp"), 1)

        def ssd_prep_pe(pe):
            pe.wait_ge(sem("sp_adt"), 1)
            f = flat(small["adt"])
            pe.matmul(psum[:, 4, 0:P], tri[:], f, start=True, stop=True).then_inc(sem("sp_cum"), 1)
            pe.matmul(psum[:, 5, 0:P], ones[:], f, start=True, stop=True).then_inc(sem("sp_cum"), 1)
            pe.matmul(psum[:, 7, 0:P], f, tri[:], start=True, stop=True).then_inc(sem("sp_cum"), 1)

        def row_of(t, c):
            return small[t][:, bass.ds(c, 1), :].rearrange("p a h -> p (a h)").unsqueeze(2).to_broadcast([P, HEADS, HD])

        def prepare_pe(pe, c):
            if isinstance(c, int) and c == 0:
                pe.wait_ge(sem("xz_read"), 2 * (XBC_T + Z_T))
            pe.wait_ge(sem("sd_xc"), c + 1)
            wait(pe, "sd_xt", c)
            for t in range(8):
                mm = pe.transpose(banks(0, 2)[:, t * P:(t + 1) * P], xc[:, t, :], ident[:])
            mm.then_inc(sem("sd_x_mm"), 1)
            wait(pe, "sd_cbm", c)
            for g in range(GROUPS):
                mm = pe.matmul(psum[:, 3, g * P:(g + 1) * P], xc[:, BC0 + g, :], xc[:, BC0 + 2 + g, :],
                               start=True, stop=True)
            mm.then_inc(sem("sd_cb_mm"), 1)
            wait(pe, "sd_bt", c)
            for g in range(GROUPS):
                mm = pe.transpose(psum[:, 2, g * P:(g + 1) * P], xc[:, BC0 + g, :], ident[:])
            mm.then_inc(sem("sd_b_mm"), 1)

        def outputs_pe(pe, c):
            if isinstance(c, int) and c == 0:
                pe.wait_ge(sem("sd_zero"), 1)
                pe.wait_ge(sem("sp_exp"), 3)
            wait(pe, "sd_st", c)
            for g in range(GROUPS):
                mm = pe.matmul(banks(6 + g), xc[:, BC0 + 2 + g, :], flat(st[:, 8 * g:8 * g + 8, :]),
                               start=True, stop=True)
            mm.then_inc(sem("sd_yo_mm"), 1)
            pe.wait_ge(sem("sd_xd"), c + 1)
            pe.wait_ge(sem("sd_mt"), 2 * c + 2)
            wait(pe, "sd_yt", c)
            for e in range(HEADS):
                mm = pe.matmul(banks(4, 2)[:, e * HD:(e + 1) * HD], mt[:, e, :], xd[:, e, :], start=True, stop=True)
            mm.then_inc(sem("sd_yd_mm"), 1)

        def state_pe(pe, c):
            pe.wait_ge(sem("sd_xw"), c + 1)
            pe.wait_ge(sem("sd_bt"), c + 1)
            pe.wait_ge(sem("sd_yo"), c + 1)
            for g in range(GROUPS):
                mm = pe.matmul(banks(6 + g), bt[:, g, :], flat(xw[:, 8 * g:8 * g + 8, :]), start=True, stop=True)
            mm.then_inc(sem("sd_st_mm"), 1)
            pe.wait_ge(sem("sd_y"), c + 1)
            for t in range(8):
                mm = pe.transpose(banks(4, 2)[:, t * P:(t + 1) * P], flat(ya[:, 2 * t:2 * t + 2, :]), ident[:])
            mm.then_inc(sem("sd_y_mm"), 1)

        def ssd_pe(pe):
            def step(c):
                outputs_pe(pe, c - 1)
                prepare_pe(pe, c)
                state_pe(pe, c - 1)
            prepare_pe(pe, 0)
            step(1)
            with pe.Fori(2, CH) as c:
                step(c)
            outputs_pe(pe, CH - 1)
            state_pe(pe, CH - 1)

        def ssd_dve(v):
            def diff(c):
                v.wait_ge(sem("sd_rows_in"), 16 * c + 16)
                wait(v, "sd_mt", 2 * c)
                v.tensor_tensor(dec[:], rows[:], small["acs"][:, bass.ds(c, 1), :].rearrange("p a h -> p (a h)")
                                .unsqueeze(2).to_broadcast([P, HEADS, P]), ALU.subtract).then_inc(sem("sd_diff"), 1)

            def x_and_cb(c):
                v.wait_ge(sem("sd_xt"), c + 1)
                wait(v, "sd_yd_mm", c)
                v.tensor_tensor(xd[:], xt[:], row_of("dt", c), ALU.mult).then_inc(sem("sd_xd"), 1)
                v.wait_ge(sem("sd_cb_mm"), c + 1)
                v.tensor_tensor(cbm[:], psum[:, 3, 0:2 * P].rearrange("p (g l) -> p g l", g=GROUPS),
                                tri[:].unsqueeze(1).to_broadcast([P, GROUPS, P]), ALU.mult).then_inc(sem("sd_cbm"), 1)

            def mix(c):
                v.wait_ge(sem("sd_exp"), c + 1)
                v.wait_ge(sem("sd_cbm"), c + 1)
                for g in range(GROUPS):
                    v.tensor_tensor(mt[:, 8 * g:8 * g + 8, :], dec[:, 8 * g:8 * g + 8, :],
                                    cbm[:, g, :].unsqueeze(1).to_broadcast([P, 8, P]), ALU.mult)\
                     .then_inc(sem("sd_mt"), 1)

            def output(c):
                v.wait_ge(sem("sd_yo_mm"), c + 1)
                v.tensor_tensor(yo[:], banks(6, 2).rearrange("p (h d) -> p h d", h=HEADS), row_of("eac", c), ALU.mult)\
                 .then_inc(sem("sd_yo"), 1)
                v.wait_ge(sem("sd_yo"), c + 1)
                v.wait_ge(sem("sd_yd_mm"), c + 1)
                wait(v, "sd_y_mm", c)
                v.tensor_tensor(flat(ya), banks(4, 2), flat(yo), ALU.add).then_inc(sem("sd_y"), 1)

            def state(c):
                v.wait_ge(sem("sd_st_mm"), c + 1)
                v.wait_ge(sem("sd_hp"), c + 1)
                v.tensor_tensor(flat(st), banks(6, 2), flat(hp), ALU.add).then_inc(sem("sd_st"), 1)

            def step(c):
                output(c - 1)
                x_and_cb(c)
                state(c - 1)
                mix(c)

            v.wait_ge(sem("xz_mm"), 2 * (XBC_T + Z_T))
            diff(0)
            v.memset(st[:], 0.0).then_inc(sem("sd_zero"), 1)
            x_and_cb(0)
            mix(0)
            diff(1)
            step(1)
            diff(2)
            out_w_lo(v, 0)
            with v.Fori(2, CH - 1) as c:
                step(c)
                diff(c + 1)
            step(CH - 1)
            out_w_lo(v, 1)
            output(CH - 1)
            state(CH - 1)

        def ssd_act(act):
            def features(c):
                wait(act, "sd_yo_mm", c)
                act.copy(xc[:], xbc[:, :, bass.ds(c * P, P)]).then_inc(sem("sd_xc"), 1)

            def prepare(c):
                act.wait_ge(sem("sd_diff"), c + 1)
                act.activation(flat(dec), flat(dec), ACT.Relu, scale=-1.0).then_inc(sem("sd_held"), 1)
                act.wait_ge(sem("sd_held"), c + 1)
                act.activation(flat(dec), flat(dec), ACT.Exp, scale=-1.0).then_inc(sem("sd_exp"), 1)
                act.wait_ge(sem("sd_x_mm"), c + 1)
                wait(act, "sd_xd", c)
                wait(act, "sd_xw", c)
                act.copy(flat(xt), banks(0, 2)).then_inc(sem("sd_xt"), 1)
                act.wait_ge(sem("sd_b_mm"), c + 1)
                wait(act, "sd_st_mm", c)
                act.copy(flat(bt), psum[:, 2, 0:2 * P]).then_inc(sem("sd_bt"), 1)

            def output(c):
                act.wait_ge(sem("sd_y_mm"), c + 1)
                act.copy(yt[:, :, bass.ds(c * P, P)], banks(4, 2).rearrange("p (t l) -> p t l", t=8))\
                   .then_inc(sem("sd_yt"), 1)

            def step(c):
                features(c)
                prepare(c)
                output(c - 1)

            act.wait_ge(sem("xz_silu"), XBC_T)
            act.wait_ge(sem("xz_mm"), 2 * (XBC_T + Z_T))
            features(0)
            prepare(0)
            step(1)
            out_w_hi(act, 0)
            with act.Fori(2, CH) as c:
                step(c)
            out_w_hi(act, 1)
            output(CH - 1)

        def ssd_pool(g):
            def decayed(c):
                wait(g, "sd_st", c)
                g.tensor_tensor(hp[:], st[:], row_of("chd", c), ALU.mult).then_inc(sem("sd_hp"), 1)

            def to_end(c):
                g.wait_ge(sem("sd_xt"), c + 1)
                wait(g, "sd_st_mm", c)
                g.tensor_tensor(xw[:], xt[:], row_of("wend", c), ALU.mult).then_inc(sem("sd_xw"), 1)

            g.wait_ge(sem("sd_zero"), 1)
            g.wait_ge(sem("sp_exp"), 3)
            g.wait_ge(sem("sp_wend"), 1)
            to_end(0)
            decayed(0)
            to_end(1)
            with g.Fori(2, CH) as c:
                decayed(c - 1)
                to_end(c)
            decayed(CH - 1)

        OUT_PAIRS = MIX_T // 2

        def out_w_hi(act, n):
            i, s = n // 2, n % 2
            act.wait_ge(sem("wo_d_in"), 16 * n + 16)
            wait(act, "wo_down_mm", 16 * (i - 1))
            act.copy(out_slots[i % 2][0][:, s], raww[:]).then_inc(sem("wo_d_hi"), 1)

        def out_w_lo(v, n):
            w_h, w_l = out_slots[n // 2 % 2][:2]
            v.wait_ge(sem("wo_d_hi"), n + 1)
            v.tensor_tensor(w_l[:, n % 2], raww[:], w_h[:, n % 2].bitcast(F32), ALU.subtract)\
             .then_inc(sem("wo_d_lo"), 1)

        def mixed_tile(n):
            return mixs[:, n % 2, :] if n < ATT_T else yt[:, n - ATT_T, :]

        def out_a_hi(act, n):
            i, s = n // 2, n % 2
            if n < ATT_T:
                act.wait_ge(sem(f"wo_m_in{s}"), 16 * i + 16)
            else:
                act.wait_ge(sem("gt_y"), n - ATT_T + 1)
            wait(act, "wo_down_mm", 16 * (i - 1))
            act.copy(out_slots[i % 2][2][:, s, :], mixed_tile(n)).then_inc(sem("wo_act_hi"), 1)

        def out_a_lo(v, n):
            a_h, a_l = out_slots[n // 2 % 2][2:]
            v.wait_ge(sem("wo_act_hi"), n + 1)
            v.tensor_tensor(a_l[:, n % 2, :], mixed_tile(n), a_h[:, n % 2, :].bitcast(F32), ALU.subtract)\
             .then_inc(sem("wo_act_lo"), 1)

        def out_sp(sp):
            def z(t):
                if t >= 2:
                    sp.wait_ge(sem("gt_z"), t - 1)
                sp.dma_start(zr[:, t % 2, :], zscr[t]).then_inc(sem(f"gt_z_in{t % 2}"), 16)

            def w(n):
                sp.wait_ge(sem("wo_d_lo"), n)
                sp.dma_start(raww[:], a["w_out"][n]).then_inc(sem("wo_d_in"), 16)

            def m(n):
                sp.wait_ge(sem("wo_act_lo"), n - 1)
                sp.dma_start(mixs[:, n % 2, :], mixed[n]).then_inc(sem(f"wo_m_in{n % 2}"), 16)

            for s in range(2):
                sp.wait_ge(sem(f"z_out{s}"), 16 * (Z_T // 2))
            for n in ("sd_yo", "sd_hp", "sd_xw"):
                sp.wait_ge(sem(n), CH)
            for f, n in ((z, 0), (z, 1), (w, 2), (m, 2), (m, 3), (z, 2), (w, 3), (z, 3), (z, 4), (m, 4), (z, 5), (w, 4),
                         (z, 6), (m, 5), (z, 7), (w, 5), (m, 6), (w, 6), (m, 7)):
                f(n)
            for n in range(7, MIX_T):
                w(n)

        def out_pe(pe):
            for i in range(OUT_PAIRS):
                pe.wait_ge(sem("wo_d_lo"), 2 * i + 2)
                pe.wait_ge(sem("wo_act_lo"), 2 * i + 2)
                if i == 0:
                    pe.wait_ge(sem("sd_yt"), CH)
                    pe.wait_ge(sem("sd_st"), CH)
                for h in range(NH2):
                    down_pe(pe, "wo", i, h, out_slots[i % 2])
                    if (i, h) == (1, 0):
                        rstd_pe_cols(pe, "gt_sum", 4, 2)
                    elif (i, h) == (2, 0):
                        rstd_pe_rows(pe, "gt0", 0)
                        rstd_pe_cols(pe, "gt_sum", 8, 2)
                    elif (i, h) == (3, 0):
                        pe.wait_ge(sem("rstd_rb"), RSTD["gt0"])
                        rstd_pe_rows(pe, "gt1", 0)

        def out_act(act):
            def square(t):
                act.wait_ge(sem("gt_z"), t + 1)
                if t >= 2:
                    act.wait_ge(sem("gt_sum"), t - 1)
                act.activation(gsq[:, t % 2, :], yt[:, t, :], ACT.Square).then_inc(sem("gt_sq"), 1)

            act.wait_ge(sem("sd_y_mm"), CH)
            act.wait_ge(sem("sd_st"), CH)
            for n in range(2):
                out_a_hi(act, n)
            for f, n in ((out_w_hi, 2), (out_a_hi, 2), (square, 0), (out_w_hi, 3), (out_a_hi, 3), (square, 1),
                         (square, 2), (square, 3), (out_w_hi, 4), (out_a_hi, 4), (square, 4), (square, 5),
                         (out_w_hi, 5), (out_a_hi, 5), (square, 6), (square, 7)):
                f(act, n) if f is not square else f(n)
            rstd_act_rms(act, "gt0", 512, 2)
            for n in (6, 7):
                out_w_hi(act, n)
                out_a_hi(act, n)
            rstd_act_rows(act, "gt0", 0)
            rstd_act_rms(act, "gt1", 512, 2)
            for n in (8, 9):
                out_w_hi(act, n)
                out_a_hi(act, n)
            act.wait_ge(sem("gt_y"), 4)
            rstd_act_rows(act, "gt1", 0)
            for n in range(10, MIX_T):
                out_w_hi(act, n)
                out_a_hi(act, n)

        def out_dve(v):
            def skip(t):
                v.scalar_tensor_tensor(out=yt[:, t, :], in0=xbc[:, t, :], scalar=cols[:, DSK + t:DSK + t + 1],
                                       in1=yt[:, t, :], op0=ALU.mult, op1=ALU.add).then_inc(sem("gt_skip"), 1)

            def normed(t):
                v.wait_ge(sem("rstd_rb"), RSTD[f"gt{t // 4}"])
                v.wait_ge(sem("gt_z"), t + 1)
                v.scalar_tensor_tensor(out=yt[:, t, :], in0=yt[:, t, :], scalar=cols[:, SSMN + t:SSMN + t + 1],
                                       in1=rb[:], op0=ALU.mult, op1=ALU.mult).then_inc(sem("gt_y"), 1)

            v.wait_ge(sem("sd_yt"), CH)
            for n in range(2):
                out_a_lo(v, n)
            skip(0)
            for i in range(OUT_PAIRS):
                def between(h, d):
                    if i == 0 and h == 0:
                        if d + 1 < KT:
                            skip(d + 1)
                        v.wait_ge(sem("gt_skip"), d + 1)
                    if i + 1 < OUT_PAIRS:
                        step = {(0, 2): (out_w_lo, 0), (0, 6): (out_a_lo, 0), (1, 2): (out_w_lo, 1),
                                (1, 5): (out_a_lo, 1)}.get((h, d))
                        if step:
                            step[0](v, 2 * i + 2 + step[1])
                    if i == 2 and h == 1 and d in (0, 2, 3, 4):
                        normed((0, 2, 3, 4).index(d))
                    if i == 3 and h == 1 and d % 2 == 0:
                        normed(4 + d // 2)
                    if (i, h, d) in ((2, 0, 0), (3, 0, 0)):
                        rstd_dve(v, f"gt{i - 2}")
                down_dve(v, "wo", i, i == 0, i == OUT_PAIRS - 1, "t2", between)

        def gate_pool(g):
            def total(t):
                g.wait_ge(sem("gt_sq"), t + 1)
                if t % 4 == 0:
                    if t == 4:
                        g.wait_ge(sem("rstd_sum_cols"), RSTD["gt0"])
                    g.tensor_copy(sqs[:], gsq[:, t % 2, :]).then_inc(sem("gt_sum"), 1)
                else:
                    g.wait_ge(sem("gt_sum"), t)
                    g.tensor_tensor(sqs[:], sqs[:], gsq[:, t % 2, :], ALU.add).then_inc(sem("gt_sum"), 1)
            for t in range(8):
                s = t % 2
                g.wait_ge(sem("gt_skip"), t + 1)
                g.wait_ge(sem(f"gt_z_in{s}"), 16 * (t // 2 + 1))
                g.tensor_tensor(yt[:, t, :], yt[:, t, :], zr[:, s, :], ALU.mult).then_inc(sem("gt_z"), 1)
                if t:
                    total(t - 1)
            total(7)

        WO_ACC = 16 * (OUT_PAIRS - 1)

        @block.sync
        def _(sp):
            sp.dma_start(cols[:], a["cols"]).then_inc(sem("cols_in"), 16)
            sp.dma_start(acc[:, 0, :], a["x"][0]).then_inc(sem("x_in0"), 16)
            sp.dma_start(rawg[:], a["gu1"][0]).then_inc(sem("f1_gu_in"), 16)
            for k in range(1, KT):
                sp.dma_start(acc[:, k, :], a["x"][k]).then_inc(sem(f"x_in{k}"), 16)
            for n, t in enumerate((ident, tri, ones, rot)):
                sp.dma_start(t[:], a["squares"][n]).then_inc(sem("consts_in"), 16)
            sp.dma_start(raww[:], a["d1"][0]).then_inc(sem("f1_d_in"), 16)
            sp.dma_start(sin[:].bitcast(I32), a["pos"]).then_inc(sem("pos_in"), 16)
            with sp.Fori(1, FT) as j:
                wait(sp, "f1_gu_lo", j)
                sp.dma_start(rawg[:], tile_of(a["gu1"], j)).then_inc(sem("f1_gu_in"), 16)
                wait(sp, "f1_d_lo", j)
                sp.dma_start(raww[:], tile_of(a["d1"], j)).then_inc(sem("f1_d_in"), 16)
            wait(sp, "f1_gu_lo", FT)
            sp.dma_start(rawg[:], a["w_att"][0:2].rearrange("t p k c -> p t k c")).then_inc(sem("at_first_in"), 16)
            wait(sp, "f1_d_lo", FT)
            sp.dma_start(raww[:], a["w_att"][2]).then_inc(sem("at_w_in"), 16)
            turn_sp(sp, "t1", a["x"], x1)
            sp.wait_ge(sem("turn_out"), past("t2", "out"))
            sp.wait_ge(sem("turn_lo"), past("t2", "lo"))
            sp.wait_ge(sem("turn_sq"), past("t2", "sq"))
            sp.dma_start(vraw[:], a["w_v"]).then_inc(sem("v_in"), 16)
            sp.dma_start(mask[:], a["mask"]).then_inc(sem("mask_in"), 16)
            sp.dma_start(arow[:], a["head_rows"]).then_inc(sem("arow_in"), 16)
            sp.wait_ge(sem("at_w_lo"), 3)
            sp.dma_start(raww[:], a["w_att"][3]).then_inc(sem("at_w_in"), 16)

            def group_weights(g, tiles):
                for t in tiles:
                    sp.wait_ge(sem("at_w_lo"), 3 * g + 3 + t)
                    sp.dma_start(raww[:], tile_of(a["w_att"], 3 * g + 3 + t)).then_inc(sem("at_w_in"), 16)

            def group_out(g):
                sp.wait_ge(sem("at_ov_add"), 16 * g + 16)
                sp.dma_start(mixed[bass.ds(2 * g, 2)].rearrange("t p s -> p t s"), attg[:]).then_inc(sem("att_out"), 16)

            with sp.Fori(0, KVH - 2) as g:
                group_weights(g, (1, 2, 3))
                group_out(g)
            group_weights(KVH - 2, (1, 2, 3))
            sp.wait_ge(sem("at_w_lo"), 3 * KVH + 1)
            sp.dma_start(raww[:], a["w_xz"][1]).then_inc(sem("xz_w_in"), 16)
            group_out(KVH - 2)

            def xz_weights(first, end):
                with sp.Fori(first, end) as n:
                    sp.wait_ge(sem("xz_w_lo"), n - 1)
                    sp.dma_start(raww[:], tile_of(a["w_xz"], n)).then_inc(sem("xz_w_in"), 16)
            xz_weights(2, STAGED + 2)
            group_out(KVH - 1)
            xz_weights(STAGED + 2, XBC_T)
            for n in range(Z_T):
                if XBC_T + n < XBC_T + Z_T:
                    sp.wait_ge(sem("xz_w_lo"), XBC_T + n - 1)
                    sp.dma_start(raww[:], a["w_xz"][XBC_T + n]).then_inc(sem("xz_w_in"), 16)
                if n >= 2:
                    sp.wait_ge(sem("z_silu"), n - 1)
                    sp.dma_start(zscr[n - 2], zs[:, n % 2, :]).then_inc(sem(f"z_out{n % 2}"), 16)
            sp.wait_ge(sem("sp_cst"), 1)
            sp.dma_start(cum, flat(small["cst"])).then_inc(sem("cum_out"), 16)
            sp.wait_ge(sem("cum_out"), 16)

            def rows_in(c):
                src = cum[bass.ds(c * HEADS, HEADS)] if not isinstance(c, int) else cum[c * HEADS:(c + 1) * HEADS]
                sp.dma_start(flat(rows), src.rearrange("h l -> (h l)").unsqueeze(0).to_broadcast([P, HEADS * P]))\
                  .then_inc(sem("sd_rows_in"), 16)
            rows_in(0)
            for n in range(Z_T - 2, Z_T):
                sp.wait_ge(sem("z_silu"), n + 1)
                sp.dma_start(zscr[n], zs[:, n % 2, :]).then_inc(sem(f"z_out{n % 2}"), 16)
            sp.wait_ge(sem("xz_w_lo"), XBC_T + Z_T - 1)
            sp.dma_start(raww[:], a["w_out"][0]).then_inc(sem("wo_d_in"), 16)
            sp.wait_ge(sem("xz_mm"), 2 * (XBC_T + Z_T))
            sp.wait_ge(sem("att_out"), 16 * KVH)
            for s in range(2):
                sp.dma_start(mixs[:, s, :], mixed[s]).then_inc(sem(f"wo_m_in{s}"), 16)
            with sp.Fori(1, CH) as c:
                sp.wait_ge(sem("sd_diff"), c)
                rows_in(c)
            sp.wait_ge(sem("wo_d_lo"), 1)
            sp.dma_start(raww[:], a["w_out"][1]).then_inc(sem("wo_d_in"), 16)
            out_sp(sp)
            sp.wait_ge(sem("wo_act_lo"), MIX_T)
            sp.dma_start(rawg[:], a["gu2"][0]).then_inc(sem("f2_gu_in"), 16)
            sp.wait_ge(sem("wo_d_lo"), MIX_T)
            sp.dma_start(raww[:], a["d2"][0]).then_inc(sem("f2_d_in"), 16)
            sp.wait_ge(sem("turn_out"), past("t2", "out"))

            def second_tile(k):
                if k == 0:
                    wait(sp, "f2_gu_lo", 1)
                    sp.dma_start(rawg[:], a["gu2"][1]).then_inc(sem("f2_gu_in"), 16)
            turn_sp(sp, "t2", x1, x2, second_tile)
            wait(sp, "f2_d_lo", 1)
            sp.dma_start(raww[:], a["d2"][1]).then_inc(sem("f2_d_in"), 16)
            with sp.Fori(2, FT) as j:
                wait(sp, "f2_gu_lo", j)
                sp.dma_start(rawg[:], tile_of(a["gu2"], j)).then_inc(sem("f2_gu_in"), 16)
                wait(sp, "f2_d_lo", j)
                sp.dma_start(raww[:], tile_of(a["d2"], j)).then_inc(sem("f2_d_in"), 16)
            sp.wait_ge(sem("turn_out"), past("t3", "out"))
            turn_sp(sp, "t3", x2, a["out"])
            sp.wait_ge(sem("turn_out"), past("t3", "out") + 16 * KT)

        @block.tensor
        def _(pe):
            ffn_pe(pe, "f1", "t0")
            rstd_pe_cols(pe, "turn_a_sum", past("t1", "a_sum") + 2 * KT)
            rstd_pe_rows(pe, "t1_post")
            first_group_pe(pe)
            att_pe(pe, 0, True, True)
            with pe.Fori(1, KVH - 1) as g:
                att_pe(pe, g, False, True)
            att_pe(pe, KVH - 1, False, False)
            xz_pe(pe)
            ssd_pe(pe)
            out_pe(pe)
            rstd_pe_cols(pe, "turn_a_sum", past("t2", "a_sum") + 2 * KT)
            rstd_pe_rows(pe, "t2_post")
            ffn_pe(pe, "f2", "t2")
            rstd_pe_cols(pe, "turn_a_sum", past("t3", "a_sum") + 2 * KT)
            rstd_pe_rows(pe, "t3_post")

        @block.scalar
        def _(act):
            act.wait_ge(sem("cols_in"), 16)
            f = ffn_act(act, "f1", "t0", rope_tables_act)
            step = next(f)
            step(START)
            turn_act(act, "t0", None, NORM_COLS["ffn1_pre"], step)
            rstd_act(act, "t0_pre", D)
            next(f)
            post_act(act, "t1", "f1_acc", FFN_ACC)
            for t in range(2):
                first_w_hi(act, t)
            rstd_act(act, "t1_post", D)
            turn_act(act, "t1", True, NORM_COLS["mix_pre"])
            rstd_act(act, "t1_pre", D)
            first_group_act(act)
            att_act(act, 0, True, True)
            with act.Fori(1, KVH - 1) as g:
                att_act(act, g, False, True)
            att_act(act, KVH - 1, False, False)
            xz_act(act)
            ssd_act(act)
            out_act(act)
            post_act(act, "t2", "wo_acc", WO_ACC)
            f = ffn_act(act, "f2", "t2", lambda act: None)
            step = next(f)
            step(START)
            rstd_act(act, "t2_post", D)
            turn_act(act, "t2", True, NORM_COLS["ffn2_pre"], step)
            rstd_act(act, "t2_pre", D)
            next(f)
            post_act(act, "t3", "f2_acc", FFN_ACC)
            rstd_act(act, "t3_post", D)

        @block.vector
        def _(v):
            v.wait_ge(sem("cols_in"), 16)
            v.tensor_scalar(hcols[:], cols[:, 0:48], 0.5, None, ALU.mult).then_inc(sem("half_cols"), 1)
            v.wait_ge(sem("half_cols"), 1)
            f = ffn_dve(v, "f1", "t0", "t1", rope_tables_dve)
            step = next(f)
            step(START)
            turn_dve(v, "t0", None, NORM_COLS["ffn1_pre"], step)
            v.wait_ge(sem("consts_in"), 16 * 4)
            rstd_dve(v, "t0_pre")
            next(f)
            for t in range(2):
                first_w_lo(v, t)
            rstd_dve(v, "t1_post")
            turn_dve(v, "t1", hcols[:, 8:16], NORM_COLS["mix_pre"])
            first_group_dve(v)
            att_dve(v, 0, True, True)
            with v.Fori(1, KVH - 1) as g:
                att_dve(v, g, False, True)
            att_dve(v, KVH - 1, False, False)
            xz_dve(v)
            ssd_dve(v)
            out_dve(v)
            f = ffn_dve(v, "f2", "t2", "t3", lambda v: None)
            step = next(f)
            step(START)
            rstd_dve(v, "t2_post")
            turn_dve(v, "t2", cols[:, 24:32], NORM_COLS["ffn2_pre"], step)
            rstd_dve(v, "t2_pre")
            next(f)
            rstd_dve(v, "t3_post")
            turn_dve(v, "t3", hcols[:, 40:48], None)

        @block.gpsimd
        def _(g):
            turn_pool(g, "t0")
            turn_pool_scale(g, "t1")
            turn_pool(g, "t1")
            for n in range(12):
                piece_pool(g, 0, n)
            att_pool(g, 0, True)
            with g.Fori(1, KVH - 1) as i:
                att_pool(g, i, True)
            att_pool(g, KVH - 1, False)
            ssd_pool(g)
            gate_pool(g)
            turn_pool_scale(g, "t2")
            turn_pool(g, "t2")
            turn_pool_scale(g, "t3")


def shape_constants():
    r = np.arange(P)
    ident = np.eye(P)
    tri = (r[:, None] <= r[None, :]) * 1.0
    rot = np.zeros((P, P))
    for b in (0, HD):
        for i in range(HD // 2):
            rot[b + HD // 2 + i, b + i] = -1.0
            rot[b + i, b + HD // 2 + i] = 1.0
    squares = np.stack([ident, tri, np.ones((P, P)), rot]).astype(np.float32)
    dist = r[:, None] + (S - P) - np.arange(S)[None, :]
    times = sum((((dist >= 0) & (dist % dil == 0) & (dist <= (win // dil) * dil)) * 1) for win, dil in ((128, 1), (512, 4), (2048, 16)))
    mask = np.where(times > 0, np.log(np.maximum(times, 1)), -1e30).astype(np.float32)
    inv = (10000.0 ** (-np.arange(0, HD, 2, dtype=np.float64) / HD)).astype(np.float32)
    return squares, mask, np.tile(inv, 4)


def kernel(**inputs):
    import concourse.bacc as bacc
    from concourse.bass_utils import run_bass_kernel_spmd

    x = {n: np.asarray(v) for n, v in inputs.items()}
    squares, mask, inv = shape_constants()

    def col_tiles(w, lo, n):
        w = w[:, lo:lo + n * P].reshape(KT, P, n, P)
        return np.ascontiguousarray(w.transpose(2, 1, 0, 3))

    def row_tiles(w):
        return np.ascontiguousarray(w.reshape(-1, P, KT, P))

    def cols_of(v):
        return v.reshape(-1, P).T

    w_in = x["w_in"][0]
    k0, v0, c0 = HEADS * HD, (HEADS + KVH) * HD, (HEADS + 2 * KVH) * HD
    z0 = c0 + XBC_T * P
    q_tiles = col_tiles(w_in, 0, 8)
    att = []
    for g in range(KVH):
        kg = w_in[:, k0 + g * HD:k0 + (g + 1) * HD]
        att += [q_tiles[2 * g], q_tiles[2 * g + 1], col_tiles(np.concatenate([kg, kg], 1), 0, 1)[0]]
    w_v = np.concatenate([w_in[:, v0:c0], w_in[:, z0 + Z_T * P:]], 1).reshape(KT, P, 272).transpose(1, 0, 2)
    arrays = {
        "x": np.ascontiguousarray(x["x"][0].T).reshape(KT, P, S),
        "pos": np.ascontiguousarray(np.broadcast_to(x["positions"], (P, S))),
        "squares": squares,
        "mask": mask,
        "cols": np.ascontiguousarray(np.concatenate(
            [cols_of(x[n][0]) for n in ("ffn1_pre_norm", "ffn1_post_norm", "mix_pre_norm", "mix_post_norm",
                                        "ffn2_pre_norm", "ffn2_post_norm")]
            + [cols_of(x["conv_w"][0, j]) for j in range(4)] + [cols_of(x["conv_b"][0])]
            + [cols_of(x["ssm_norm"][0]), cols_of(np.repeat(x["d_skip"][0], HD))]
            + [inv[:, None], np.full((P, 1), EPS, np.float32)], 1)),
        "head_rows": np.ascontiguousarray(np.broadcast_to(np.stack([x["dt_bias"][0], x["a_log"][0]]), (P, 2, HEADS))),
        "w_att": np.stack(att + [col_tiles(w_in, c0, 1)[0]]),
        "w_v": np.ascontiguousarray(w_v),
        "w_xz": col_tiles(w_in, c0, XBC_T + Z_T),
        "w_out": row_tiles(x["w_out"][0]),
    }
    for n in (1, 2):
        gate, up = (col_tiles(x[f"ffn{n}_w_{m}"][0], 0, FT) for m in ("gate", "up"))
        arrays[f"gu{n}"] = np.ascontiguousarray(np.stack([gate, up], 2))
        arrays[f"d{n}"] = row_tiles(x[f"ffn{n}_w_down"][0])
    nc = bacc.Bacc("TRN2", target_bir_lowering=False, num_devices=1)
    a = {n: nc.dram_tensor("in_" + n, v.shape, mybir.dt.from_np(v.dtype), kind="ExternalInput").ap()
         for n, v in arrays.items()}
    a["out"] = nc.dram_tensor("out_x", (KT, P, S), F32, kind="ExternalOutput").ap()
    build(nc, a)
    r = run_bass_kernel_spmd(nc, [{"in_" + n: v for n, v in arrays.items()}], core_ids=[0])
    y = r.results[0]["out_x"]
    return np.ascontiguousarray(y.reshape(D, S).T).reshape(x["x"].shape)
```
